# Optimizing a Trainium2 kernel written in Bass

```python
import math
import jax
import jax.numpy as jnp
from jax import lax
import numpy as np

D_MODEL = 2048
BATCH = 1
SEQ = 256
DEPTH = 2
DEC_BATCH = 1
DEC_SEQ = 64
PAST_LEN = 128

CHUNK = 64
N_META = 16
ROPE_THETA = 10000.0
EPS = 1e-6
Q_BLOCK = 128

N_AB = (DEPTH + 1) // 2
N_CD = DEPTH // 2

A_HEADS = 8
A_KV_HEADS = 2
A_HEAD_DIM = D_MODEL // 2 // A_HEADS
IDX_HEADS = 16
IDX_DIM = 64
TOPK_MAX = 256
B_HEADS = 8
B_Q_RANK = D_MODEL // 4
B_KV_RANK = D_MODEL // 8
B_NOPE = 128
B_ROPE = 64
B_V = D_MODEL // 2 // B_HEADS
C_WIDTH = D_MODEL // 2
C_BLOCKS = 8
C_BLOCK = C_WIDTH // C_BLOCKS
CONV_W = 4
RG_C = 8.0
D_HEADS = 4
D_KDIM = D_MODEL // 2 // D_HEADS
D_VDIM = 256
D_FF = 4 * D_MODEL

AB_SPLITS = [A_HEADS * A_HEAD_DIM, A_KV_HEADS * A_HEAD_DIM, A_KV_HEADS * A_HEAD_DIM,
             IDX_HEADS * IDX_DIM, IDX_DIM, IDX_HEADS, B_Q_RANK, B_KV_RANK, B_ROPE]
AB_IN = sum(AB_SPLITS)
AB_OUT = A_HEADS * A_HEAD_DIM + B_HEADS * B_V
CD_SPLITS = [C_WIDTH, C_WIDTH, D_HEADS * D_KDIM, D_HEADS * D_KDIM, D_HEADS * D_VDIM, D_HEADS * D_VDIM]
CD_IN = sum(CD_SPLITS)
CD_OUT = C_WIDTH + D_HEADS * D_VDIM

kernel_name = 'hybrid_streaming_dsa_mla_rglru_retention_step'

F32 = jnp.float32

def rmsnorm(x, g):
    x32 = x.astype(F32)
    y = x32 * lax.rsqrt(jnp.mean(x32 * x32, axis=-1, keepdims=True) + EPS)
    return (y * g.astype(F32)).astype(x.dtype)

def split_cols(z, sizes):
    return jnp.split(z, [int(c) for c in np.cumsum(sizes)[:-1]], axis=-1)

def rope(x, pos):
    d = x.shape[-1]
    inv = ROPE_THETA ** (-jnp.arange(0, d, 2, dtype=F32) / d)
    ang = pos.astype(F32)[:, None] * inv[None, :]
    shape = (pos.shape[0],) + (1,) * (x.ndim - 3) + (d // 2,)
    cos = jnp.cos(ang).reshape(shape)
    sin = jnp.sin(ang).reshape(shape)
    x32 = x.astype(F32)
    x1, x2 = x32[..., : d // 2], x32[..., d // 2:]
    return jnp.concatenate([x1 * cos - x2 * sin, x1 * sin + x2 * cos], axis=-1).astype(x.dtype)

def sweep_query_blocks(fn, q_arrays, cq):
    nb_batch, t = q_arrays[0].shape[:2]
    nblk = -(-t // Q_BLOCK)
    pad = nblk * Q_BLOCK - t
    padded = [jnp.pad(a, [(0, 0), (0, pad)] + [(0, 0)] * (a.ndim - 2)) for a in q_arrays]
    cqp = jnp.pad(cq, (0, pad), mode='edge')

    def body(j):
        start = j * Q_BLOCK
        blk = [lax.dynamic_slice_in_dim(a, start, Q_BLOCK, axis=1) for a in padded]
        return fn(*blk, lax.dynamic_slice_in_dim(cqp, start, Q_BLOCK))

    out = lax.map(body, jnp.arange(nblk))
    out = jnp.moveaxis(out, 0, 1).reshape(nb_batch, nblk * Q_BLOCK, out.shape[-1])
    return out[:, :t]

def dsa_attend(q, qi, wi, cq, k, v, ki, ck, topk):
    s_idx = jnp.einsum('bqhd,bsd->bqhs', qi.astype(F32), ki.astype(F32))
    s_idx = jnp.einsum('bqhs,bqh->bqs', jax.nn.relu(s_idx), wi.astype(F32))
    admissible = ck[None, :] <= cq[:, None]
    s_idx = jnp.where(admissible[None], s_idx, -jnp.inf)
    _, sel = lax.top_k(s_idx, topk)
    valid = ck[sel] <= cq[None, :, None]
    gather = jax.vmap(lambda rows, ids: rows[ids])
    k_sel = gather(k, sel).astype(F32)
    v_sel = gather(v, sel).astype(F32)
    nb, nq = q.shape[:2]
    qg = q.reshape(nb, nq, A_KV_HEADS, A_HEADS // A_KV_HEADS, A_HEAD_DIM).astype(F32)
    s = jnp.einsum('bqcgd,bqscd->bqcgs', qg, k_sel) * (A_HEAD_DIM ** -0.5)
    s = jnp.where(valid[:, :, None, None, :], s, -jnp.inf)
    p = jax.nn.softmax(s, axis=-1)
    o = jnp.einsum('bqcgs,bqscd->bqcgd', p, v_sel)
    return o.reshape(nb, nq, A_HEADS * A_HEAD_DIM).astype(q.dtype)

def mla_attend(qn, qr, cq, kn, kr, v, ck):
    s = (jnp.einsum('bqhd,bshd->bhqs', qn.astype(F32), kn.astype(F32))
         + jnp.einsum('bqhr,bsr->bhqs', qr.astype(F32), kr.astype(F32))) * ((B_NOPE + B_ROPE) ** -0.5)
    mask = ck[None, :] <= cq[:, None]
    s = jnp.where(mask[None, None], s, -jnp.inf)
    p = jax.nn.softmax(s, axis=-1)
    o = jnp.einsum('bhqs,bshd->bqhd', p, v.astype(F32))
    nb, nq = qn.shape[:2]
    return o.reshape(nb, nq, B_HEADS * B_V).astype(qn.dtype)

def ab_mix(u, pos, cq, ck, past, topk, blocked, w_in, w_out, g_aq, g_ak, g_qlat, w_uq,
           g_kvlat, w_ukv, g_qn, g_qr, g_kn, g_kr):
    nb, t, _ = u.shape
    qa, ka, va, qi, ki, wi, cqlat, ckv, kr = split_cols(u @ w_in, AB_SPLITS)
    q = rope(rmsnorm(qa.reshape(nb, t, A_HEADS, A_HEAD_DIM), g_aq), pos)
    k_new = rope(rmsnorm(ka.reshape(nb, t, A_KV_HEADS, A_HEAD_DIM), g_ak), pos)
    v_new = va.reshape(nb, t, A_KV_HEADS, A_HEAD_DIM)
    qi = rope(qi.reshape(nb, t, IDX_HEADS, IDX_DIM), pos) * (IDX_DIM ** -0.5)
    ki_new = rope(ki, pos)
    wi = wi * (IDX_HEADS ** -0.5)
    qb = (rmsnorm(cqlat, g_qlat) @ w_uq).reshape(nb, t, B_HEADS, B_NOPE + B_ROPE)
    qn = rmsnorm(qb[..., :B_NOPE], g_qn)
    qr = rope(rmsnorm(qb[..., B_NOPE:], g_qr), pos)
    lat_new = rmsnorm(ckv, g_kvlat)
    kr_new = rope(rmsnorm(kr, g_kr), pos)
    new_rows = (k_new, v_new, ki_new, lat_new, kr_new)
    if past is None:
        k_all, v_all, ki_all, lat_all, kr_all = new_rows
    else:
        k_all, v_all, ki_all, lat_all, kr_all = [jnp.concatenate([p_.astype(n_.dtype), n_], axis=1)
                                                 for p_, n_ in zip(past, new_rows)]
    kvb = (lat_all @ w_ukv).reshape(nb, lat_all.shape[1], B_HEADS, B_NOPE + B_V)
    kn_all = rmsnorm(kvb[..., :B_NOPE], g_kn)
    vb_all = kvb[..., B_NOPE:]

    def attn_a(q_, qi_, wi_, c_):
        return dsa_attend(q_, qi_, wi_, c_, k_all, v_all, ki_all, ck, topk)

    def attn_b(qn_, qr_, c_):
        return mla_attend(qn_, qr_, c_, kn_all, kr_all, vb_all, ck)

    if blocked:
        oa = sweep_query_blocks(attn_a, (q, qi, wi), cq)
        ob = sweep_query_blocks(attn_b, (qn, qr), cq)
    else:
        oa = attn_a(q, qi, wi, cq)
        ob = attn_b(qn, qr, cq)
    return jnp.concatenate([oa, ob], axis=-1) @ w_out, new_rows

def rglru_scan(a, b, h0):
    b = b.at[:, 0].add(a[:, 0] * h0)

    def combine(l, r):
        return (l[0] * r[0], r[0] * l[1] + r[1])

    _, h = lax.associative_scan(combine, (a, b), axis=1)
    return h, h[:, -1]

def retention_block(q, k, v, s, log_gamma):
    n = q.shape[1]
    i = jnp.arange(n, dtype=F32)
    diff = i[:, None] - i[None, :]
    decay = jnp.where(diff >= 0, jnp.exp(log_gamma[:, None, None] * jnp.maximum(diff, 0.0)), 0.0)
    o = jnp.einsum('bihd,bjhd->bhij', q, k) * decay[None]
    o = jnp.einsum('bhij,bjhe->bihe', o, v)
    inter = jnp.exp(log_gamma[None, :] * (i[:, None] + 1.0))
    o = o + jnp.einsum('bihd,bhde->bihe', q, s) * inter[None, :, :, None]
    kdec = jnp.exp(log_gamma[None, :] * (n - 1.0 - i)[:, None])
    s = (jnp.exp(log_gamma * n)[None, :, None, None] * s
         + jnp.einsum('bjhd,bjhe->bhde', k * kdec[None, :, :, None], v))
    return o, s

def retention(q, k, v, s0, log_gamma):
    t = q.shape[1]
    lead = t % CHUNK
    s = s0
    outs = []
    if lead:
        o0, s = retention_block(q[:, :lead], k[:, :lead], v[:, :lead], s, log_gamma)
        outs.append(o0)
    nc = (t - lead) // CHUNK
    if nc:
        def to_chunks(a):
            return jnp.moveaxis(a[:, lead:].reshape(a.shape[0], nc, CHUNK, *a.shape[2:]), 1, 0)

        def step(s_, blk):
            o_, s_ = retention_block(blk[0], blk[1], blk[2], s_, log_gamma)
            return s_, o_

        s, oc = lax.scan(step, s, (to_chunks(q), to_chunks(k), to_chunks(v)))
        outs.append(jnp.moveaxis(oc, 0, 1).reshape(q.shape[0], t - lead, *oc.shape[3:]))
    return jnp.concatenate(outs, axis=1), s

def cd_mix(u, pos, conv_buf, h0, s0, log_gamma, w_in, w_out, conv_w, conv_b, ga_w, ga_b,
           gx_w, gx_b, lam, g_dn):
    nb, t, _ = u.shape
    cx, cg, dq, dk, dv, dg = split_cols(u @ w_in, CD_SPLITS)
    full = jnp.concatenate([conv_buf.astype(cx.dtype), cx], axis=1)
    xc = conv_b + full[:, :t] * conv_w[0]
    for j in range(1, CONV_W):
        xc = xc + full[:, j:j + t] * conv_w[j]
    new_buf = full[:, t:]
    xc32 = xc.astype(F32)
    xb = xc32.reshape(nb, t, C_BLOCKS, C_BLOCK)
    r = jax.nn.sigmoid(jnp.einsum('btni,nij->btnj', xb, ga_w.astype(F32)).reshape(nb, t, C_WIDTH) + ga_b)
    ig = jax.nn.sigmoid(jnp.einsum('btni,nij->btnj', xb, gx_w.astype(F32)).reshape(nb, t, C_WIDTH) + gx_b)
    log_a = -RG_C * r * jax.nn.softplus(-lam.astype(F32))
    a = jnp.exp(log_a)
    b = jnp.sqrt(-jnp.expm1(2.0 * log_a)) * (ig * xc32)
    hc, h_last = rglru_scan(a, b, h0.astype(F32))
    out_c = (hc * jax.nn.gelu(cg.astype(F32))).astype(u.dtype)
    q = rope(dq.reshape(nb, t, D_HEADS, D_KDIM), pos).astype(F32)
    k = rope(dk.reshape(nb, t, D_HEADS, D_KDIM), pos).astype(F32) * (D_KDIM ** -0.5)
    v = dv.reshape(nb, t, D_HEADS, D_VDIM).astype(F32)
    od, s_last = retention(q, k, v, s0.astype(F32), log_gamma)
    od = rmsnorm(od.astype(u.dtype), g_dn).reshape(nb, t, D_HEADS * D_VDIM) * jax.nn.silu(dg)
    out = jnp.concatenate([out_c, od.astype(u.dtype)], axis=-1) @ w_out
    return out, (new_buf, h_last.astype(u.dtype), s_last.astype(u.dtype))

def sq_relu_mlp(x, g, w_up, w_down):
    return jnp.square(jax.nn.relu(rmsnorm(x, g) @ w_up)) @ w_down

def setup_inputs(seed: int = 0) -> dict:
    key = jax.random.key(seed)
    keys = iter(jax.random.split(key, 48))

    def nrm(shape, scale):
        return jax.random.normal(next(keys), shape, jnp.float32) * scale

    def gain(shape):
        return 1.0 + nrm(shape, 0.02)

    a0 = jax.random.uniform(next(keys), (N_CD, C_WIDTH), jnp.float32, 0.9, 0.999)
    p0 = a0 ** (1.0 / RG_C)
    c_lambda = jnp.log(p0) - jnp.log1p(-p0)
    return {
        'x_prompt': nrm((BATCH, SEQ, D_MODEL), 1.0),
        'x_sample': nrm((DEC_BATCH, DEC_SEQ, D_MODEL), 1.0),
        'cache_a_k': nrm((N_AB, DEC_BATCH, PAST_LEN, A_KV_HEADS, A_HEAD_DIM), 1.0),
        'cache_a_v': nrm((N_AB, DEC_BATCH, PAST_LEN, A_KV_HEADS, A_HEAD_DIM), 1.0),
        'cache_a_kidx': nrm((N_AB, DEC_BATCH, PAST_LEN, IDX_DIM), 1.0),
        'cache_b_latent': nrm((N_AB, DEC_BATCH, PAST_LEN, B_KV_RANK), 1.0),
        'cache_b_krope': nrm((N_AB, DEC_BATCH, PAST_LEN, B_ROPE), 1.0),
        'state_c_conv': nrm((N_CD, DEC_BATCH, CONV_W - 1, C_WIDTH), 1.0),
        'state_c_h': nrm((N_CD, DEC_BATCH, C_WIDTH), 0.5),
        'state_d_s': nrm((N_CD, DEC_BATCH, D_HEADS, D_KDIM, D_VDIM), 0.5),
        'meta_tokens': nrm((N_META, D_MODEL), 1.0),
        'norm_mix': gain((DEPTH, D_MODEL)),
        'norm_mlp': gain((DEPTH, D_MODEL)),
        'ab_w_in': nrm((N_AB, D_MODEL, AB_IN), D_MODEL ** -0.5),
        'ab_w_out': nrm((N_AB, AB_OUT, D_MODEL), AB_OUT ** -0.5),
        'a_q_norm': gain((N_AB, A_HEAD_DIM)),
        'a_k_norm': gain((N_AB, A_HEAD_DIM)),
        'b_q_lat_norm': gain((N_AB, B_Q_RANK)),
        'b_w_uq': nrm((N_AB, B_Q_RANK, B_HEADS * (B_NOPE + B_ROPE)), B_Q_RANK ** -0.5),
        'b_kv_lat_norm': gain((N_AB, B_KV_RANK)),
        'b_w_ukv': nrm((N_AB, B_KV_RANK, B_HEADS * (B_NOPE + B_V)), B_KV_RANK ** -0.5),
        'b_qn_norm': gain((N_AB, B_NOPE)),
        'b_qr_norm': gain((N_AB, B_ROPE)),
        'b_kn_norm': gain((N_AB, B_NOPE)),
        'b_kr_norm': gain((N_AB, B_ROPE)),
        'cd_w_in': nrm((N_CD, D_MODEL, CD_IN), D_MODEL ** -0.5),
        'cd_w_out': nrm((N_CD, CD_OUT, D_MODEL), CD_OUT ** -0.5),
        'c_conv_w': nrm((N_CD, CONV_W, C_WIDTH), 0.5),
        'c_conv_b': nrm((N_CD, C_WIDTH), 0.02),
        'c_gate_a_w': nrm((N_CD, C_BLOCKS, C_BLOCK, C_BLOCK), C_BLOCK ** -0.5),
        'c_gate_a_b': nrm((N_CD, C_WIDTH), 0.02),
        'c_gate_x_w': nrm((N_CD, C_BLOCKS, C_BLOCK, C_BLOCK), C_BLOCK ** -0.5),
        'c_gate_x_b': nrm((N_CD, C_WIDTH), 0.02),
        'c_lambda': c_lambda,
        'd_out_norm': gain((N_CD, D_VDIM)),
        'mlp_w_up': nrm((DEPTH, D_MODEL, D_FF), D_MODEL ** -0.5),
        'mlp_w_down': nrm((DEPTH, D_FF, D_MODEL), D_FF ** -0.5),
    }

def reference(x_prompt, x_sample, cache_a_k, cache_a_v, cache_a_kidx, cache_b_latent, cache_b_krope,
              state_c_conv, state_c_h, state_d_s, meta_tokens, norm_mix, norm_mlp, ab_w_in, ab_w_out,
              a_q_norm, a_k_norm, b_q_lat_norm, b_w_uq, b_kv_lat_norm, b_w_ukv, b_qn_norm, b_qr_norm,
              b_kn_norm, b_kr_norm, cd_w_in, cd_w_out, c_conv_w, c_conv_b, c_gate_a_w, c_gate_a_b,
              c_gate_x_w, c_gate_x_b, c_lambda, d_out_norm, mlp_w_up, mlp_w_down):
    nb_p, seq_p = x_prompt.shape[:2]
    seq_s = x_sample.shape[1]
    past = cache_a_k.shape[2]
    hp = jnp.concatenate([jnp.broadcast_to(meta_tokens[None].astype(x_prompt.dtype), (nb_p, N_META, D_MODEL)),
                          x_prompt], axis=1)
    pos_p = jnp.arange(N_META + seq_p)
    ck_p = jnp.concatenate([jnp.zeros((N_META,), jnp.int32), 1 + jnp.arange(seq_p, dtype=jnp.int32) // CHUNK])
    pos_s_all = jnp.arange(past + seq_s)
    ck_s = pos_s_all // CHUNK
    pos_s = pos_s_all[past:]
    cq_s = ck_s[past:]
    topk_p = min(TOPK_MAX, seq_p // 4)
    topk_s = min(TOPK_MAX, (past + seq_s) // 4)
    log_gamma = jnp.log(1.0 - 2.0 ** (-5.0 - jnp.arange(D_HEADS, dtype=F32)))

    hs = x_sample
    ab_p, ab_s, cd_p, cd_s = [], [], [], []
    for layer in range(DEPTH):
        i = layer // 2
        g_mix = norm_mix[layer]
        if layer % 2 == 0:
            w = (ab_w_in[i], ab_w_out[i], a_q_norm[i], a_k_norm[i], b_q_lat_norm[i], b_w_uq[i],
                 b_kv_lat_norm[i], b_w_ukv[i], b_qn_norm[i], b_qr_norm[i], b_kn_norm[i], b_kr_norm[i])
            yp, rows_p = ab_mix(rmsnorm(hp, g_mix), pos_p, ck_p, ck_p, None, topk_p, True, *w)
            past_rows = (cache_a_k[i], cache_a_v[i], cache_a_kidx[i], cache_b_latent[i], cache_b_krope[i])
            ys, rows_s = ab_mix(rmsnorm(hs, g_mix), pos_s, cq_s, ck_s, past_rows, topk_s, False, *w)
            ab_p.append(rows_p)
            ab_s.append(rows_s)
        else:
            w = (cd_w_in[i], cd_w_out[i], c_conv_w[i], c_conv_b[i], c_gate_a_w[i], c_gate_a_b[i],
                 c_gate_x_w[i], c_gate_x_b[i], c_lambda[i], d_out_norm[i])
            zc = jnp.zeros((nb_p, CONV_W - 1, C_WIDTH), hp.dtype)
            zh = jnp.zeros((nb_p, C_WIDTH), hp.dtype)
            zs = jnp.zeros((nb_p, D_HEADS, D_KDIM, D_VDIM), hp.dtype)
            yp, st_p = cd_mix(rmsnorm(hp, g_mix), pos_p, zc, zh, zs, log_gamma, *w)
            ys, st_s = cd_mix(rmsnorm(hs, g_mix), pos_s, state_c_conv[i], state_c_h[i], state_d_s[i],
                              log_gamma, *w)
            cd_p.append(st_p)
            cd_s.append(st_s)
        hp = hp + yp
        hs = hs + ys
        hp = hp + sq_relu_mlp(hp, norm_mlp[layer], mlp_w_up[layer], mlp_w_down[layer])
        hs = hs + sq_relu_mlp(hs, norm_mlp[layer], mlp_w_up[layer], mlp_w_down[layer])

    def stack(entries, j):
        return jnp.stack([e[j] for e in entries])

    return (hp[:, N_META:], hs,
            stack(ab_p, 0), stack(ab_p, 1), stack(ab_p, 2), stack(ab_p, 3), stack(ab_p, 4),
            stack(cd_p, 0), stack(cd_p, 1), stack(cd_p, 2),
            stack(ab_s, 0), stack(ab_s, 1), stack(ab_s, 2), stack(ab_s, 3), stack(ab_s, 4),
            stack(cd_s, 0), stack(cd_s, 1), stack(cd_s, 2))


_drawn_inputs = setup_inputs


def setup_inputs(seed=0):
    import zlib

    import numpy as np

    out = dict(_drawn_inputs(seed))
    spreads = {}
    factors = {'a_q_norm': 8.0,
     'a_k_norm': 2.851,
     'b_q_lat_norm': 8.0,
     'b_kv_lat_norm': 2.871,
     'b_qn_norm': 8.0,
     'b_qr_norm': 8.0,
     'b_kn_norm': 8.0,
     'b_kr_norm': 2.875,
     'c_gate_a_b': 8.0,
     'c_gate_x_b': 7.392,
     'd_out_norm': 28.997,
     'norm_mlp': 2.789}
    for name, (base, spread) in spreads.items():
        noise = np.random.default_rng([zlib.crc32(name.encode()), seed]).standard_normal(out[name].shape)
        drawn = base * np.exp(spread * noise) if base else spread * noise
        out[name] = jnp.asarray(drawn.astype(out[name].dtype))
    for name, factor in factors.items():
        out[name] = (out[name] * factor).astype(out[name].dtype)
    return out
```

```python
from contextlib import ExitStack

import numpy as np
import concourse.bass as bass
from concourse import mybir

F32 = mybir.dt.float32
F32R = mybir.dt.float32r
ACT = mybir.ActivationFunctionType
ALU = mybir.AluOpType

P = 128
D = 2048
KT = D // P
NS_TOK, NMETA, SEQ = 64, 16, 256
TP = NMETA + SEQ
T = NS_TOK + TP
PAST = 128
KEYS = PAST + T
CHUNK = 64
EPS = 1e-6

UNIT = 1024
CU = 8
NR = 4
U_ABIN, N_ABIN = 0, 7
U_UQ = U_ABIN + CU * N_ABIN
U_KN = U_UQ + 6
U_V = U_KN + 2
U_ABOUT = U_V + 2
U_MLP0 = U_ABOUT + 4 * CU
U_CDIN, N_CDIN = U_MLP0 + 32 * CU, 12
U_GATE = U_CDIN + N_CDIN * CU
U_CDOUT = U_GATE + 2
U_MLP1 = U_CDOUT + 4 * CU
N_UNITS = U_MLP1 + 32 * CU
G_ABIN = 0
G_ABOUT = G_ABIN + N_ABIN
G_MLP0 = G_ABOUT + 4
G_CDIN = G_MLP0 + 32
G_CDOUT = G_CDIN + N_CDIN
G_MLP1 = G_CDOUT + 4
G_END = G_MLP1 + 32

QA, KA, QI, KK, WI, CQ, CKV, VA = 0, 8, 10, 18, 19, 20, 24, 26
CX, CG, DQ, DK, DV, DG = 0, 8, 16, 24, 32, 40

QT = [(0, 0, 208), (80, 128, 336), (208, 128, 464)]
SEG = [0, 208, 416, 752]
QN = [(0, 80), (80, 208), (208, 336)]
KTILE = [(0, 128), (128, 208), (208, 336), (336, 464)]
TT = [(0, 80), (80, 208), (208, 336)]
TOPK_S, TOPK_P = (PAST + NS_TOK) // 4, SEQ // 4
NEG, TAKEN = -1e30, -3e38

GAIN = {}
_n = 0
for _name, _w in (("norm", 64), ("aq", 1), ("ak", 1), ("kk", 1), ("qr", 1), ("qn", 1), ("kn", 1),
                  ("qlat", 4), ("kvlat", 2), ("conv_w", 32), ("conv_b", 8), ("ga_b", 8), ("gx_b", 8),
                  ("lam", 8), ("dn", 2), ("h0", 8), ("eps", 1), ("mkr", 1), ("mki", 1), ("kdec", 12),
                  ("zero", 1)):
    GAIN[_name] = _n
    _n += _w
NGAIN = _n

GAMMA = [1.0 - 2.0 ** (-5.0 - h) for h in range(4)]


def at(i, per, c):
    if i is None:
        return c
    return i * per + c


class Chain:

    def __init__(self, eng, sem):
        self.eng, self.sem, self.n = eng, sem, 0

    def mark(self, ins):
        ins.then_inc(self.sem, 1)
        self.n += 1
        return self.n

    def need(self, n):
        self.eng.wait_ge(self.sem, n)

    def link(self, ins):
        self.need(self.mark(ins))


def build(nc, x_in, wstream, gains_in, cst_in, tabs_in, adm_in, ret_in, decq_in,
          past_k, past_kk, past_v, past_lat, conv_in, s0_in,
          y_out, k_out, v_out, kk_out, lat_out, conv_out, h_out, s_out):
    ctx = ExitStack()
    with ctx:
        def sem(name):
            return ctx.enter_context(nc.semaphore(name))

        base, end = 16512, 229344
        cur = [base]

        def keep(name, shape, dt=F32):
            t = nc.alloc_sbuf_tensor_at(name, shape, dt, offset=cur[0])
            cur[0] += int(np.prod(shape[1:])) * 4
            cur[0] = (cur[0] + 31) // 32 * 32
            return t

        def place(name, shape, offset, dt=F32):
            size = int(np.prod(shape[1:])) * 4
            assert offset % 32 == 0 and offset + size <= end, (name, offset, size, end)
            return nc.alloc_sbuf_tensor_at(name, shape, dt, offset=offset)

        TB = T * 4
        x = keep("x", [P, KT, T])
        stage = keep("stage", [P, NR, UNIT])
        w_hi = keep("w_hi", [P, NR, UNIT], F32R)
        w_lo = keep("w_lo", [P, NR, UNIT], F32R)
        cst = keep("cst", [P, 4, P])
        tab_at = cur[0]
        tab = keep("tab", [P, 4, T])
        rstd = keep("rstd", [P, T])
        gains = keep("gains", [P, NGAIN])
        wiT = keep("wiT", [P, 3, 16])
        m8 = keep("m8", [P, 3, 8])
        mx = keep("mx", [P, 3, 3])
        rsum = keep("rsum", [P, 3, 3])
        sp4 = keep("sp4", [P, 8])
        spt = keep("spt", [P, 4, 8])
        hlast = keep("hlast", [P, 8, 2])
        ident, swap, ones, pairs = (cst[:, i, :] for i in range(4))

        decq = place("decq", [P, 4, NS_TOK], tab_at + 2 * TB)
        A = cur[0]
        xh = place("xh", [P, KT, T], A, F32R)
        xl = place("xl", [P, KT, T], A + KT * TB, F32R)
        moh = place("moh", [P, KT, T], A, F32R)
        mol = place("mol", [P, KT, T], A + KT * TB, F32R)
        qlath = place("qlath", [P, 4, T], A + 8 * TB, F32R)
        lath = place("lath", [P, 2, KEYS], A + 12 * TB, F32R)
        qlatl = place("qlatl", [P, 4, T], A + 24 * TB, F32R)
        latl = place("latl", [P, 2, KEYS], A + 28 * TB, F32R)
        B = A + 2 * KT * TB
        zt = place("zt", [P, 28, T], B)
        qb = place("qb", [P, 12, T], B + 12 * TB)
        kn = place("kn", [P, 8, KEYS], B)
        C = B + 28 * TB
        kpad = place("kpad", [P, 4, KEYS], C)
        C2 = C + 4 * KEYS * 4
        adm = place("adm", [P, SEG[3]], C2)
        C3 = C2 + SEG[3] * 4
        lat = place("lat", [P, 2, KEYS], C3)
        W = C3 + 2 * KEYS * 4
        sqb = place("sqb", [P, 2, KEYS], W)
        sdb = place("sdb", [P, 2, KEYS], W + 2 * KEYS * 4)
        ra = place("ra", [P, 2, T], W + 4 * KEYS * 4)
        rb = place("rb", [P, 2, T], W + 4 * KEYS * 4 + 2 * TB)
        sqm = place("sqm", [P, 6, T], W)
        sdm = place("sdm", [P, 2, T], W + 6 * TB)
        acc = place("acc", [P, SEG[3]], W)
        rt = place("rt", [P, 2, SEG[3]], W + SEG[3] * 4)
        pr = place("pr", [P, 3, SEG[3]], W)
        pta = place("pta", [P, 2, 4, P], W + 9 * 1024)
        ptb = place("ptb", [P, 2, 3, P], W + 9 * 1024 + 4096)
        V = W + 9 * 1024 + 4096 + 3072
        kA = place("kA", [P, 2, KEYS], V)
        kk = place("kk", [P, KEYS], V + 2 * KEYS * 4)
        vA = place("vA", [P, 4, 256], V + 3 * KEYS * 4)
        biasA = place("biasA", [P, SEG[3]], V + 3 * KEYS * 4 + 4096)
        vB = place("vB", [P, 4, 1024], V)
        hh = place("hh", [P, 16, T], B, F32R)
        hl = place("hl", [P, 16, T], B + 16 * TB, F32R)
        mt1 = place("mt1", [P, 4, T], B + 32 * TB)
        mt2 = place("mt2", [P, 4, T], B + 36 * TB)
        ssq = place("ssq", [P, 4, T], W)
        sst = place("sst", [P, 4, T], W + 4 * TB)
        z2 = place("z2", [P, 48, T], B)
        t1 = place("t1", [P, 8, T], B)
        C1 = B + 48 * TB
        cxp = place("cxp", [P, 8, T + 6], C1)
        inv = place("inv", [P, 8, T], C1)
        xc = place("xc", [P, 8, T], C1 + 8 * (T + 6) * 4)
        rg = place("rg", [P, 8, T], A)
        ig = place("ig", [P, 8, T], A + KT * TB)
        rr = place("rr", [P, 4, 4, T], C1)
        ktok = place("ktok", [P, 2, 3, 256], C1)
        vtok = place("vtok", [P, 2, 3, 256], C1 + 6144)
        pT = place("pT", [P, 2, 720], C1 + 12288)
        dmask = place("dmask", [P, 2, 720], C1 + 12288 + 5760)
        s0 = place("s0", [P, 2, 4, 256], B)
        so = place("so", [P, 4, 2, 256], B + 8192)
        qd = place("qd", [P, 2, 2, NS_TOK], B + 16384)
        osq = place("osq", [P, 2, T], B + 17408)
        osd = place("osd", [P, T], B + 17408 + 2 * TB)

        PS = ctx.enter_context(nc.psum_tensor("PS", [P, 8, 512], F32))

        def gcol(name, i=0, rows=slice(0, P)):
            c = GAIN[name] + i
            return gains[rows, c:c + 1]

        stage_full = [sem(f"stage_full{i}") for i in range(NR)]
        hi_ready = sem("hi_ready")
        lo_ready = sem("lo_ready")
        unit_done = sem("unit_done")
        evac = sem("evac")
        const_in = sem("const_in")
        x_in_s = sem("x_in_s")
        past_in = sem("past_in")
        pad_zero = sem("pad_zero")
        xh_ready, xl_ready = sem("xh_ready"), sem("xl_ready")
        ssq_ready, ssum_done, rms_ready = sem("ssq_ready"), sem("ssum_done"), sem("rms_ready")
        dchain, achain, pchain = sem("dchain"), sem("achain"), sem("pchain")
        hh_ready, hl_ready, hsq_done = sem("hh_ready"), sem("hl_ready"), sem("hsq_done")
        sq_ready, msq_ready, sd_ready = sem("sq_ready"), sem("msq_ready"), sem("sd_ready")
        ab_ready, rot_ready, turned = sem("ab_ready"), sem("rot_ready"), sem("turned")
        latsq, latms, latsd, lat_ready, lath_ready, latl_ready = (
            sem("latsq"), sem("latms"), sem("latsd"), sem("lat_ready"), sem("lath_ready"),
            sem("latl_ready"))
        tok_psum, tok_copied = sem("tok_psum"), sem("tok_copied")
        kpad_ready = sem("kpad_ready")
        idx_psum, relu_ready, idx_added, bias_ready = (sem("idx_psum"), sem("relu_ready"),
                                                       sem("idx_added"), sem("bias_ready"))
        qkv_evac = sem("qkv_evac")
        sc_psum, smax, p_ready, pn_ready = sem("sc_psum"), sem("smax"), sem("p_ready"), sem("pn_ready")
        pt_psum, pta_ready, ptb_ready = sem("pt_psum"), sem("pta_ready"), sem("ptb_ready")
        o_psum, moh_ready, mol_ready = sem("o_psum"), sem("moh_ready"), sem("mol_ready")
        out_s = sem("out_s")
        tab2_in, cx_in, cx_copied, conv_outs = sem("tab2_in"), sem("cx_in"), sem("cx_copied"), sem("conv_outs")
        cx_zero = sem("cx_zero")
        xc_ready, xch_ready, xcl_ready = sem("xc_ready"), sem("xch_ready"), sem("xcl_ready")
        gate_psum, gate_ready, tanh_ready, inv_ready = (sem("gate_psum"), sem("gate_ready"),
                                                        sem("tanh_ready"), sem("inv_ready"))
        sqrt_ready, igx_ready, scan_done = sem("sqrt_ready"), sem("igx_ready"), sem("scan_done")
        gelu_in, gelu_sig, gelu_ready = sem("gelu_in"), sem("gelu_sig"), sem("gelu_ready")
        silu_sig, silu_ready = sem("silu_sig"), sem("silu_ready")
        outc_ready, h_outs = sem("outc_ready"), sem("h_outs")
        sp_exp, sp_abs, sp_ready = sem("sp_exp"), sem("sp_abs"), sem("sp_ready")
        rope2_d, rope2_p = sem("rope2_d"), sem("rope2_p")
        s0_in_s = sem("s0_in_s")
        mask_in = [sem("mask_in0"), sem("mask_in1")]
        kv_psum, ktok_ready, ds_psum, pT_ready, qd_ready = (sem("kv_psum"), sem("ktok_ready"),
                                                            sem("ds_psum"), sem("pT_ready"), sem("qd_ready"))
        do_psum, osq_ready, oms_psum, osd_ready, od_ready = (sem("do_psum"), sem("osq_ready"),
                                                             sem("oms_psum"), sem("osd_ready"), sem("od_ready"))
        st_psum, st_sample, st_prompt = sem("st_psum"), sem("st_sample"), sem("st_prompt")
        st_out = [sem("st_out0"), sem("st_out1")]
        doh_ready, dol_ready = sem("doh_ready"), sem("dol_ready")

        block = ctx.enter_context(nc.Block())

        X_FINAL = [0, G_MLP0, G_CDIN, G_MLP1]
        NORM_G = [G_ABIN, G_MLP0, G_CDIN, G_MLP1]

        def SB(n):
            return 4 * (1 - NORM_G[n] % 2) + 3

        def turn_tasks():
            a = [dict(src=zt[:, KA + c, :], dst=kA[:, c, PAST:], g=gcol("ak"), m=ones, n=128, tab=0)
                 for c in range(2)]
            a += [dict(src=zt[:, KK, :], dst=kk[:, PAST:], g=gcol("kk"), m=pairs, n=64, tab=2, kk=True)]
            a += [dict(src=zt[:, QI + c, :], dst=zt[:, QI + c, :], g=None, n=0, tab=2) for c in range(8)]
            a += [dict(src=zt[:, QA + c, :], dst=zt[:, QA + c, :], g=gcol("aq"), m=ones, n=128, tab=0)
                  for c in range(8)]
            b = [dict(src=qb[:, c, :], dst=qb[:, c, :], g=gcol("qn"), m=ones, n=128, tab=None)
                 for c in range(8)]
            b += [dict(src=qb[:, 8 + c, :], dst=qb[:, 8 + c, :], g=gcol("qr"), m=pairs, n=64, tab=2)
                  for c in range(4)]
            b += [dict(src=kn[:, c, :], dst=kn[:, c, :], g=gcol("kn"), m=ones, n=128, tab=None)
                  for c in range(8)]
            ni = ri = 0
            for j, t in enumerate(a + b):
                t["j"], t["ni"], t["ri"] = j, ni, ri
                t["w"] = KEYS if t["dst"].shape[-1] == KEYS else T
                ni += bool(t["n"])
                ri += t["tab"] is not None
            return a, b

        TURN_A, TURN_B = turn_tasks()
        N_TURN_A = len(TURN_A)
        KK_J = 2

        @block.sync
        def _(sp):
            for s in range(NR):
                sp.dma_start(stage[:, s, :], wstream[s]).then_inc(stage_full[s], 16)
            with sp.Fori(1, N_UNITS // NR) as i:
                for s in range(NR):
                    sp.wait_ge(lo_ready, i * NR + (s + 1 - NR))
                    sp.dma_start(stage[:, s, :], wstream[i * NR + s]).then_inc(stage_full[s], 16)

        @block.scalar
        def _(act):
            ch = Chain(act, achain)

            def split(u, i=None, per=0):
                s = u % NR
                act.wait_ge(stage_full[s], at(i, 16 * per // NR, 16 * (u // NR + 1)))
                if u >= NR:
                    act.wait_ge(unit_done, at(i, per, u - NR + 1))
                act.activation(w_hi[:, s, :], stage[:, s, :], ACT.Copy).then_inc(hi_ready, 1)

            def step(u0, i=None, per=0, last=False, hook=None):
                for k in range(NR, CU + (0 if last else NR)):
                    split(u0 + k, i, per)
                    if hook and k == NR + 5:
                        hook()

            def norm_prep(n):
                if n == 0:
                    act.wait_ge(x_in_s, 16)
                    act.wait_ge(const_in, 48)
                else:
                    act.wait_ge(evac, X_FINAL[n])
                for t in range(KT):
                    act.activation(xh[:, t, :], x[:, t, :], ACT.Copy,
                                   scale=gcol("norm", 16 * n + t)).then_inc(xh_ready, 1)

            def rms(n):
                def f():
                    act.wait_ge(ssum_done, n + 1)
                    act.activation(rstd[:], PS[:, SB(n), 0:T], ACT.Sqrt, scale=1.0 / D,
                                   bias=gcol("eps")).then_inc(rms_ready, 1)
                return f

            def turn(tasks):
                prev = None
                for t in tasks + [None]:
                    if t is not None and t["n"]:
                        ni, w = t["ni"], t["w"]
                        if ni >= 2:
                            act.wait_ge(msq_ready, ni - 1)
                        act.activation(sqb[:, ni % 2, 0:w], t["src"], ACT.Square).then_inc(sq_ready, 1)
                    if prev is not None:
                        p = prev
                        if p["n"]:
                            act.wait_ge(msq_ready, p["ni"] + 1)
                            if p["j"] >= 2:
                                act.wait_ge(turned, p["j"] - 1)
                            act.activation(sdb[:, p["ni"] % 2, 0:p["w"]], PS[:, p["ni"] % 2, 0:p["w"]],
                                           ACT.Sqrt, scale=1.0 / p["n"], bias=gcol("eps")).then_inc(sd_ready, 1)
                    prev = t

            def attend(g0, h0):
                for s in range(8 + 3):
                    if s < 8:
                        g = g0 + s
                        act.wait_ge(smax, g + 1)
                        for q in range(3):
                            seg = pr[:, g % 3, SEG[q]:SEG[q + 1]]
                            e = act.activation(seg, seg, ACT.Exp, bias=mx[:, g % 3, q:q + 1],
                                               accum_out=rsum[:, g % 3, q:q + 1])
                        e.then_inc(p_ready, 1)
                    if 2 <= s < 10:
                        g = g0 + s - 2
                        act.wait_ge(pt_psum, g + 1)
                        if g >= 2:
                            act.wait_ge(o_psum, g - 1)
                        act.activation(pta[:, g % 2], PS[:, 4, :].rearrange("p (a b) -> p a b", a=4),
                                       ACT.Copy).then_inc(pta_ready, 1)
                    if s >= 3:
                        g = g0 + s - 3
                        act.wait_ge(o_psum, g + 1)
                        act.activation(moh[:, h0 + s - 3, :], PS[:, 6 + g % 2, 0:T],
                                       ACT.Copy).then_inc(moh_ready, 1)

            def mlp(n, u_mlp, g_mlp, L, whole):
                def body(f):
                    for c in range(4):
                        step(u_mlp + CU * c, f, 64, hook=rms(n) if whole and c == 0 else None)
                        g = 16 * L + c
                        act.wait_ge(evac, at(f, 8, g_mlp + c + 1))
                        if not (whole and c == 0 and L == 0):
                            act.wait_ge(hl_ready, at(f, 4, g))
                        act.activation(mt2[:], mt1[:], ACT.Square).then_inc(hsq_done, 1)
                        act.wait_ge(hsq_done, at(f, 4, g + 1))
                        act.activation(hh[:, 4 * c:4 * c + 4, :], mt2[:], ACT.Copy).then_inc(hh_ready, 1)
                    for c in range(4):
                        step(u_mlp + 32 + CU * c, f, 64)
                return body

            def mlp_last(u_mlp, g_mlp, L):
                f = 3
                for c in range(4):
                    step(u_mlp + 64 * f + CU * c)
                    g = 16 * L + 4 * f + c
                    act.wait_ge(evac, g_mlp + 8 * f + c + 1)
                    act.wait_ge(hl_ready, g)
                    act.activation(mt2[:], mt1[:], ACT.Square).then_inc(hsq_done, 1)
                    act.wait_ge(hsq_done, g + 1)
                    act.activation(hh[:, 4 * c:4 * c + 4, :], mt2[:], ACT.Copy).then_inc(hh_ready, 1)
                for c in range(4):
                    step(u_mlp + 64 * f + 32 + CU * c, last=c == 3)

            act.dma_start(x[:], x_in).then_inc(x_in_s, 16)
            act.dma_start(gains[:], gains_in).then_inc(const_in, 16)
            act.dma_start(cst[:], cst_in).then_inc(const_in, 16)
            act.dma_start(tab[:], tabs_in[:, 0:4, :]).then_inc(const_in, 16)
            act.dma_start(adm[:], adm_in).then_inc(past_in, 16)
            act.dma_start(kA[:, :, 0:PAST], past_k).then_inc(past_in, 16)
            act.dma_start(kk[:, 0:PAST], past_kk).then_inc(past_in, 16)
            act.dma_start(vA[:, 0, :], past_v).then_inc(past_in, 16)
            act.dma_start(lat[:, :, 0:PAST], past_lat).then_inc(past_in, 16)

            for u in range(NR):
                split(u)
            norm_prep(0)
            lam = gains[:, GAIN["lam"]:GAIN["lam"] + 8]
            act.activation(spt[:, 0, :], lam, ACT.Abs).then_inc(sp_abs, 1)
            act.wait_ge(sp_abs, 1)
            act.activation(spt[:, 1, :], spt[:, 0, :], ACT.Exp, scale=-1.0).then_inc(sp_exp, 1)
            step(U_ABIN, hook=rms(0))
            with act.Fori(0, 3) as i:
                for c in range(2):
                    step(U_ABIN + CU * (1 + c), i, 2 * CU)
            act.wait_ge(evac, N_ABIN)
            act.activation(sqm[:, 0:4, :], zt[:, CQ:CQ + 4, :], ACT.Square).then_inc(latsq, 1)
            act.activation(sqm[:, 4:6, :], zt[:, CKV:CKV + 2, :], ACT.Square).then_inc(latsq, 1)
            for i, n in enumerate((512, 256)):
                act.wait_ge(latms, i + 1)
                act.activation(sdm[:, i, :], PS[:, i, 0:T], ACT.Sqrt, scale=1.0 / n,
                               bias=gcol("eps")).then_inc(latsd, 1)
            act.wait_ge(tok_psum, 1)
            act.activation(wiT[:].rearrange("p a b -> p (a b)"), PS[:, 2, 0:48], ACT.Copy)
            act.activation(vA[:, 2:4, :], PS[:, 3, :].rearrange("p (a b) -> p a b", a=2), ACT.Copy)
            act.activation(vA[0:80, 1, :], PS[0:80, 4, 0:256], ACT.Copy).then_inc(tok_copied, 1)
            act.wait_ge(lat_ready, 1)
            act.wait_ge(past_in, 80)
            act.activation(qlath[:], zt[:, CQ:CQ + 4, :], ACT.Copy)
            act.activation(lath[:], lat[:], ACT.Copy).then_inc(lath_ready, 1)
            act.wait_ge(latl_ready, 1)
            turn(TURN_A)
            for h in range(16):
                act.wait_ge(idx_psum, h + 1)
                if h >= 2:
                    act.wait_ge(idx_added, h - 1)
                elif h == 0:
                    act.wait_ge(turned, N_TURN_A)
                b = 2 * (h % 2)
                act.activation(rt[:, h % 2, 0:416], PS[:, b, 0:416], ACT.Relu, scale=1.0 / 32)
                act.activation(rt[:, h % 2, 416:752], PS[:, b + 1, 0:336], ACT.Relu,
                               scale=1.0 / 32).then_inc(relu_ready, 1)
            for c in range(3):
                split(U_UQ + 4 + 2 * c)
                split(U_UQ + 5 + 2 * c)
                act.wait_ge(unit_done, U_UQ + 2 * c + 2)
                act.activation(qb[:, 4 * c:4 * c + 4, :], PS[:, 4:8, 0:T], ACT.Copy).then_inc(qkv_evac, 1)
            attend(0, 0)
            for c in range(2):
                split(U_KN + 4 + c)
                act.wait_ge(unit_done, U_KN + c + 1)
                act.activation(kn[:, 4 * c:4 * c + 4, :], PS[:, 4 * c:4 * c + 4, 0:KEYS],
                               ACT.Copy).then_inc(qkv_evac, 1)
            for c in range(2):
                split(U_V + 4 + c)
                act.wait_ge(unit_done, U_V + c + 1)
                if c == 0:
                    act.wait_ge(out_s, 64)
                dst = vB[:, :, 512 * c:512 * c + 512]
                act.activation(dst[0:80, 1, :], PS[0:80, 4 * c + 1, :], ACT.Copy)
                act.activation(dst[:, 0, :], PS[:, 4 * c, :], ACT.Copy)
                act.activation(dst[:, 2:4, :], PS[:, 4 * c + 2:4 * c + 4, :], ACT.Copy).then_inc(qkv_evac, 1)
            act.wait_ge(qkv_evac, 7)
            turn(TURN_B)
            act.wait_ge(turned, len(TURN_A) + len(TURN_B))
            attend(8, 8)
            with act.Fori(0, 2) as i:
                for c in range(2):
                    step(U_ABOUT + CU * c, i, 2 * CU)
            norm_prep(1)
            mlp(1, U_MLP0, G_MLP0, 0, True)(0)
            with act.Fori(1, 4) as f:
                mlp(1, U_MLP0, G_MLP0, 0, False)(f)

            norm_prep(2)
            step(U_CDIN, hook=rms(2))
            step(U_CDIN + CU)
            with act.Fori(1, 6) as i:
                for c in range(2):
                    if c == 1:
                        step(U_CDIN + CU, i, 2 * CU)
                    else:
                        step(U_CDIN, i, 2 * CU)
            act.wait_ge(evac, G_CDIN + 2)
            act.wait_ge(cx_zero, 1)
            act.activation(cxp[:, :, 3:3 + NS_TOK], z2[:, CX:CX + 8, 0:NS_TOK], ACT.Copy)
            act.activation(cxp[:, :, 6 + NS_TOK:], z2[:, CX:CX + 8, NS_TOK:], ACT.Copy).then_inc(cx_copied, 1)
            act.wait_ge(gelu_in, 1)
            act.activation(t1[:], t1[:], ACT.Sigmoid, scale=2 * 0.7978845608028654).then_inc(gelu_sig, 1)
            act.wait_ge(xc_ready, 16)
            act.activation(moh[:, 8:16, :], xc[:], ACT.Copy).then_inc(xch_ready, 1)
            for n in range(16):
                if n % 8 == 7:
                    act.wait_ge(unit_done, U_GATE + n // 8 + 1)
                else:
                    act.wait_ge(gate_psum, n - n // 8 + 1)
                dst, bias = (rg, "ga_b") if n < 8 else (ig, "gx_b")
                act.activation(dst[:, n % 8, :], PS[:, n % 8, 0:T], ACT.Sigmoid,
                               bias=gcol(bias, n % 8)).then_inc(gate_ready, 1)
            act.wait_ge(gate_ready, 16)
            act.wait_ge(sp_ready, 1)
            for n in range(8):
                e = act.activation(rg[:, n, :], rg[:, n, :], ACT.Tanh, scale=sp4[:, n:n + 1])
            e.then_inc(tanh_ready, 1)
            act.wait_ge(gelu_ready, 1)
            act.wait_ge(evac, G_CDIN + 12)
            act.activation(t1[:], z2[:, DG:DG + 8, :], ACT.Sigmoid).then_inc(silu_sig, 1)
            act.wait_ge(inv_ready, 1)
            act.wait_ge(tanh_ready, 1)
            act.activation(rg[:], rg[:], ACT.Sqrt, scale=4.0).then_inc(sqrt_ready, 1)
            for u in (2, 3):
                split(U_CDOUT + u)
            act.wait_ge(outc_ready, 1)
            act.activation(moh[:, 0:8, :], z2[:, CG:CG + 8, :], ACT.Copy).then_inc(doh_ready, 1)
            for h in range(4):
                act.wait_ge(kv_psum, h + 1)
                if h >= 2:
                    act.wait_ge(st_psum, 2 * (h - 1))
                if h == 0:
                    act.wait_ge(rope2_d, 4)
                    act.wait_ge(rope2_p, 4)
                kd = [gains[r, GAIN["kdec"] + 3 * h + t:GAIN["kdec"] + 3 * h + t + 1]
                      for t, r in ((0, slice(0, 80)), (1, slice(0, P)), (2, slice(0, P)))]
                act.activation(ktok[0:80, h % 2, 0, :], PS[0:80, 1, 0:256], ACT.Copy, scale=kd[0])
                act.activation(ktok[:, h % 2, 1, :], PS[:, 0, 0:256], ACT.Copy, scale=kd[1])
                act.activation(ktok[:, h % 2, 2, :], PS[:, 0, 256:512], ACT.Copy, scale=kd[2])
                act.activation(vtok[0:80, h % 2, 0, :], PS[0:80, 1, 256:512], ACT.Copy)
                act.activation(vtok[:, h % 2, 1:3, :], PS[:, 2, :].rearrange("p (a b) -> p a b", a=2),
                               ACT.Copy).then_inc(ktok_ready, 1)
                act.wait_ge(do_psum, h + 1)
                if h >= 1:
                    act.wait_ge(od_ready, h)
                act.activation(osq[:], PS[:, 5:7, 0:T], ACT.Square).then_inc(osq_ready, 1)
                act.wait_ge(oms_psum, h + 1)
                act.activation(osd[:], PS[:, 4, 0:T], ACT.Sqrt, scale=1.0 / 256,
                               bias=gcol("eps")).then_inc(osd_ready, 1)
                act.wait_ge(st_psum, 2 * h + 2)
                if h >= 2:
                    act.wait_ge(st_out[h % 2], 32)
                act.activation(so[:, 2 + h % 2], PS[:, 0, :].rearrange("p (a b) -> p a b", a=2),
                               ACT.Copy).then_inc(st_prompt, 1)
                act.wait_ge(od_ready, h + 1)
                act.activation(moh[:, 8 + 2 * h:10 + 2 * h, :], z2[:, DG + 2 * h:DG + 2 * h + 2, :],
                               ACT.Copy).then_inc(doh_ready, 1)
            with act.Fori(0, 2) as i:
                for c in range(2):
                    step(U_CDOUT + CU * c, i, 2 * CU)
            norm_prep(3)
            mlp(3, U_MLP1, G_MLP1, 1, True)(0)
            with act.Fori(1, 3) as f:
                mlp(3, U_MLP1, G_MLP1, 1, False)(f)
            mlp_last(U_MLP1, G_MLP1, 1)

        @block.vector
        def _(dve):
            ch = Chain(dve, dchain)

            def split(u, i=None, per=0):
                s = u % NR
                dve.wait_ge(hi_ready, at(i, per, u + 1))
                dve.tensor_tensor(w_lo[:, s, :], stage[:, s, :], w_hi[:, s, :].bitcast(F32),
                                  ALU.subtract).then_inc(lo_ready, 1)

            def step(u0, i=None, per=0, last=False):
                for k in range(NR, CU + (0 if last else NR)):
                    split(u0 + k, i, per)

            def norm_prep(n):
                if n:
                    dve.wait_ge(evac, X_FINAL[n])
                for t in range(KT):
                    dve.wait_ge(xh_ready, 16 * n + t + 1)
                    dve.scalar_tensor_tensor(xl[:, t, :], x[:, t, :], gcol("norm", 16 * n + t),
                                             xh[:, t, :].bitcast(F32), ALU.mult,
                                             ALU.subtract).then_inc(xl_ready, 1)

            def rms(n):
                dve.wait_ge(rms_ready, n + 1)
                ch.link(dve.reciprocal(rstd[:], rstd[:]))

            rstd4 = rstd[:].unsqueeze(1).to_broadcast([P, 4, T])

            def banks(g):
                b = 4 * (g % 2)
                return PS[:, b:b + 4, 0:T]

            def take_scaled(u0, g, dst, i=None, su=0, sg=0):
                dve.wait_ge(unit_done, at(i, su, u0 + CU))
                dve.tensor_tensor(dst, banks(g), rstd4, ALU.mult).then_inc(evac, 1)

            def take_added(u0, g, dst, i=None, su=0, sg=0):
                dve.wait_ge(unit_done, at(i, su, u0 + CU))
                dve.tensor_tensor(dst, banks(g), dst, ALU.add).then_inc(evac, 1)

            x4 = x[:].rearrange("p (c m) t -> p c m t", m=4)
            zt4 = zt[:].rearrange("p (c m) t -> p c m t", m=4)
            z24 = z2[:].rearrange("p (c m) t -> p c m t", m=4)

            def turn(tasks):
                prev = None
                for t in tasks + [None]:
                    if t is not None and t["tab"] is not None:
                        ri, k = t["ri"], t["tab"]
                        if ri >= 2:
                            dve.wait_ge(rot_ready, ri - 1)
                        if t["g"] is None:
                            dve.tensor_tensor(ra[:, ri % 2, :], t["src"], tab[:, k, :], ALU.mult)
                            dve.tensor_tensor(rb[:, ri % 2, :], t["src"], tab[:, k + 1, :],
                                              ALU.mult).then_inc(ab_ready, 1)
                        else:
                            dve.scalar_tensor_tensor(ra[:, ri % 2, :], t["src"], t["g"], tab[:, k, :],
                                                     ALU.mult, ALU.mult)
                            dve.scalar_tensor_tensor(rb[:, ri % 2, :], t["src"], t["g"], tab[:, k + 1, :],
                                                     ALU.mult, ALU.mult).then_inc(ab_ready, 1)
                    if prev is not None:
                        p = prev
                        if p["n"]:
                            sd = sdb[:, p["ni"] % 2, 0:p["w"]]
                            dve.wait_ge(sd_ready, p["ni"] + 1)
                            ch.link(dve.reciprocal(sd, sd))
                            if p.get("kk"):
                                ch.link(dve.tensor_scalar(sd, sd, gcol("mkr"), gcol("mki"), ALU.mult, ALU.add))
                            if p["tab"] is None:
                                dve.scalar_tensor_tensor(p["dst"], p["src"], p["g"], sd, ALU.mult,
                                                         ALU.mult).then_inc(turned, 1)
                            else:
                                dve.wait_ge(rot_ready, p["ri"] + 1)
                                dve.tensor_tensor(p["dst"], PS[:, 2 + p["ri"] % 2, 0:T], sd,
                                                  ALU.mult).then_inc(turned, 1)
                        else:
                            dve.wait_ge(rot_ready, p["ri"] + 1)
                            dve.tensor_copy(p["dst"], PS[:, 2 + p["ri"] % 2, 0:T]).then_inc(turned, 1)
                        if p.get("kk"):
                            kpad_fill()
                    prev = t

            def kpad_fill():
                dve.wait_ge(turned, KK_J + 1)
                dve.wait_ge(pad_zero, 1)
                dve.wait_ge(past_in, 80)
                for slot, (src, dst) in enumerate(((0, 0), (0, 32), (32, 0), (32, 32))):
                    for half in (0, 64):
                        e = dve.tensor_copy(kpad[dst + half:dst + half + 32, slot, :],
                                            kk[src + half:src + half + 32, :])
                e.then_inc(kpad_ready, 1)

            def attend(g0, h0, bias, scale):
                for s in range(8 + 3):
                    if s < 8:
                        g = g0 + s
                        dve.wait_ge(sc_psum, g + 1)
                        if g >= 3:
                            dve.wait_ge(pt_psum, g - 2)
                        for q in range(3):
                            src = PS[:, 2 * (g % 2) + q // 2, SEG[q] - 416 * (q // 2):SEG[q + 1] - 416 * (q // 2)]
                            e = dve.tensor_tensor_reduce(pr[:, g % 3, SEG[q]:SEG[q + 1]], src,
                                                         bias[:, SEG[q]:SEG[q + 1]], scale, TAKEN,
                                                         ALU.add, ALU.max, mx[:, g % 3, q:q + 1])
                        ch.link(e)
                        dve.tensor_scalar(mx[:, g % 3, :], mx[:, g % 3, :], -1.0, None,
                                          ALU.mult).then_inc(smax, 1)
                    if 1 <= s < 9:
                        g = g0 + s - 1
                        dve.wait_ge(p_ready, g + 1)
                        ch.link(dve.reciprocal(rsum[:, g % 3, :], rsum[:, g % 3, :]))
                        for q in range(3):
                            seg = pr[:, g % 3, SEG[q]:SEG[q + 1]]
                            e = dve.tensor_scalar(seg, seg, rsum[:, g % 3, q:q + 1], None, ALU.mult)
                        e.then_inc(pn_ready, 1)
                    if 2 <= s < 10:
                        g = g0 + s - 2
                        dve.wait_ge(pt_psum, g + 1)
                        if g >= 2:
                            dve.wait_ge(o_psum, g - 1)
                        dve.tensor_copy(ptb[0:80, g % 2], PS[0:80, 5, 0:384].rearrange(
                            "p (a b) -> p a b", a=3)).then_inc(ptb_ready, 1)
                    if s >= 3:
                        g = g0 + s - 3
                        dve.wait_ge(moh_ready, g + 1)
                        dve.tensor_tensor(mol[:, h0 + s - 3, :], PS[:, 6 + g % 2, 0:T],
                                          moh[:, h0 + s - 3, :].bitcast(F32),
                                          ALU.subtract).then_inc(mol_ready, 1)

            def take_up(u0, g, c, f, whole, L):
                dve.wait_ge(unit_done, at(f, 64, u0 + CU))
                if not (whole and c == 0 and L == 0):
                    dve.wait_ge(hh_ready, at(f, 4, 16 * L + c))
                dve.scalar_tensor_tensor(mt1[:], banks(g), 0.0, rstd4, ALU.max, ALU.mult).then_inc(evac, 1)

            def low_h(c, f, L):
                dve.wait_ge(hh_ready, at(f, 4, 16 * L + c + 1))
                dve.tensor_tensor(hl[:, 4 * c:4 * c + 4, :], mt2[:], hh[:, 4 * c:4 * c + 4, :].bitcast(F32),
                                  ALU.subtract).then_inc(hl_ready, 1)

            def mlp(n, u_mlp, g_mlp, L, whole, last=False):
                def body(f):
                    for c in range(4):
                        step(u_mlp + CU * c, f, 64)
                        if whole and c == 0:
                            rms(n)
                        take_up(u_mlp + CU * c, g_mlp + c, c, f, whole, L)
                        low_h(c, f, L)
                    for c in range(4):
                        step(u_mlp + 32 + CU * c, f, 64, last=last and c == 3)
                        take_added(u_mlp + 32 + CU * c, g_mlp + c, x4[:, c], f, 64)
                return body

            for u in range(NR):
                split(u)
            norm_prep(0)
            u_, z_, z2_ = spt[:, 1, :], spt[:, 2, :], spt[:, 3, :]
            dve.wait_ge(sp_exp, 1)
            ch.link(dve.tensor_scalar(z_, u_, 2.0, None, ALU.add))
            ch.link(dve.reciprocal(z_, z_))
            ch.link(dve.tensor_tensor(z_, z_, u_, ALU.mult))
            ch.link(dve.tensor_tensor(z2_, z_, z_, ALU.mult))
            ch.link(dve.tensor_scalar(u_, z2_, 1.0 / 17, 1.0 / 15, ALU.mult, ALU.add))
            for k in (13, 11, 9, 7, 5, 3, 1):
                ch.link(dve.tensor_tensor(u_, u_, z2_, ALU.mult))
                ch.link(dve.tensor_scalar(u_, u_, 1.0 / k, None, ALU.add))
            ch.link(dve.tensor_tensor(u_, u_, z_, ALU.mult))
            lam = gains[:, GAIN["lam"]:GAIN["lam"] + 8]
            ch.link(dve.tensor_scalar(z_, lam, -1.0, 0.0, ALU.mult, ALU.max))
            ch.link(dve.scalar_tensor_tensor(u_, u_, 2.0, z_, ALU.mult, ALU.add))
            dve.tensor_scalar(sp4[:], u_, 4.0, None, ALU.mult).then_inc(sp_ready, 1)

            step(U_ABIN)
            rms(0)
            take_scaled(U_ABIN, 0, zt4[:, 0])
            with dve.Fori(0, 3) as i:
                for c in range(2):
                    step(U_ABIN + CU * (1 + c), i, 2 * CU)
                    take_scaled(U_ABIN + CU * (1 + c), 1 + c, zt4[:, i * 2 + (1 + c)], i, 2 * CU)
            dve.wait_ge(latsd, 2)
            ch.link(dve.reciprocal(sdm[:], sdm[:]))
            dve.wait_ge(evac, N_ABIN)
            dve.wait_ge(latsq, 2)
            for t in range(4):
                dve.scalar_tensor_tensor(zt[:, CQ + t, :], zt[:, CQ + t, :], gcol("qlat", t), sdm[:, 0, :],
                                         ALU.mult, ALU.mult)
            for t in range(2):
                e = dve.scalar_tensor_tensor(lat[:, t, PAST:], zt[:, CKV + t, :], gcol("kvlat", t),
                                             sdm[:, 1, :], ALU.mult, ALU.mult)
            e.then_inc(lat_ready, 1)
            dve.wait_ge(lath_ready, 1)
            dve.tensor_tensor(qlatl[:], zt[:, CQ:CQ + 4, :], qlath[:].bitcast(F32), ALU.subtract)
            dve.tensor_tensor(latl[:], lat[:], lath[:].bitcast(F32), ALU.subtract).then_inc(latl_ready, 1)
            dve.wait_ge(latl_ready, 1)
            turn(TURN_A)
            dve.wait_ge(turned, N_TURN_A)
            dve.wait_ge(tok_copied, 1)
            for h in range(16):
                dve.wait_ge(relu_ready, h + 1)
                if h:
                    dve.wait_ge(idx_added, h)
                for q in range(3):
                    sl = slice(SEG[q], SEG[q + 1])
                    e = dve.scalar_tensor_tensor(acc[:, sl], rt[:, h % 2, sl], wiT[:, q, h:h + 1],
                                                 (adm if h == 0 else acc)[:, sl], ALU.mult, ALU.add)
                e.then_inc(idx_added, 1)
            dve.wait_ge(idx_added, 16)
            for r in range(TOPK_P // 8):
                rows = [q for q in range(3) if r < (TOPK_S if q == 0 else TOPK_P) // 8]
                for q in rows:
                    e = dve.max(m8[:, q, :], acc[:, SEG[q]:SEG[q + 1]])
                ch.link(e)
                for q in rows:
                    sl = slice(SEG[q], SEG[q + 1])
                    e = dve.match_replace(acc[:, sl], m8[:, q, :], acc[:, sl], TAKEN)
                ch.link(e)
                if r < 6:
                    split(U_UQ + 4 + r)
            ch.link(dve.tensor_scalar(biasA[:], acc[:], TAKEN / 2, NEG, ALU.is_gt, ALU.mult))
            ch.link(dve.tensor_tensor(biasA[:], biasA[:], adm[:], ALU.add))
            attend(0, 0, biasA, 128 ** -0.5)
            for u in range(4):
                split(U_KN + 4 + u)
            dve.wait_ge(qkv_evac, 7)
            turn(TURN_B)
            dve.wait_ge(turned, len(TURN_A) + len(TURN_B))
            attend(8, 8, adm, 192 ** -0.5)
            with dve.Fori(0, 2) as i:
                for c in range(2):
                    step(U_ABOUT + CU * c, i, 2 * CU)
                    take_added(U_ABOUT + CU * c, G_ABOUT + c, x4[:, i * 2 + c], i, 2 * CU)
            norm_prep(1)
            mlp(1, U_MLP0, G_MLP0, 0, True)(0)
            with dve.Fori(1, 4) as f:
                mlp(1, U_MLP0, G_MLP0, 0, False)(f)

            norm_prep(2)
            step(U_CDIN)
            rms(2)
            take_scaled(U_CDIN, G_CDIN, z24[:, 0])
            step(U_CDIN + CU)
            take_scaled(U_CDIN + CU, G_CDIN + 1, z24[:, 1])
            with dve.Fori(1, 6) as i:
                for c in range(2):
                    step(U_CDIN + CU * c, i, 2 * CU)
                    take_scaled(U_CDIN + CU * c, G_CDIN + c, z24[:, i * 2 + c], i, 2 * CU)
            dve.wait_ge(cx_copied, 1)
            dve.wait_ge(cx_in, 16)
            parts = ((0, NS_TOK, 0), (NS_TOK, T, 3))
            marks = {}
            for j in range(4):
                for n in range(8):
                    for a, b, off in parts:
                        dst, src = xc[:, n, a:b], cxp[:, n, a + off + j:b + off + j]
                        w = gcol("conv_w", 8 * j + n)
                        if j == 0:
                            e = dve.tensor_scalar(dst, src, w, gcol("conv_b", n), ALU.mult, ALU.add)
                        else:
                            ch.need(marks[j - 1, n, a])
                            e = dve.scalar_tensor_tensor(dst, src, w, dst, ALU.mult, ALU.add)
                        if j == 3:
                            e.then_inc(xc_ready, 1)
                        else:
                            marks[j, n, a] = ch.mark(e)
            dve.wait_ge(xch_ready, 1)
            dve.tensor_tensor(mol[:, 8:16, :], xc[:], moh[:, 8:16, :].bitcast(F32),
                              ALU.subtract).then_inc(xcl_ready, 1)
            dve.wait_ge(tanh_ready, 1)
            dve.wait_ge(conv_outs, 32)
            ch.link(dve.tensor_scalar(inv[:], rg[:], 1.0, None, ALU.add))
            dve.reciprocal(inv[:], inv[:]).then_inc(inv_ready, 1)
            for u in (2, 3):
                split(U_CDOUT + u)
            dve.wait_ge(inv_ready, 1)
            dve.wait_ge(sqrt_ready, 1)
            ch.link(dve.tensor_tensor(rg[:], rg[:], inv[:], ALU.mult))
            a_ = ch.mark(dve.tensor_scalar(inv[:], inv[:], 2.0, -1.0, ALU.mult, ALU.add))
            dve.wait_ge(igx_ready, 1)
            b_ = ch.mark(dve.tensor_tensor(rg[:], rg[:], ig[:], ALU.mult))
            ch.need(b_)
            for n in range(8):
                dve.tensor_tensor_scan(xc[:, n, 0:NS_TOK], inv[:, n, 0:NS_TOK], rg[:, n, 0:NS_TOK],
                                       gcol("h0", n), ALU.mult, ALU.add)
                e = dve.tensor_tensor_scan(xc[:, n, NS_TOK:], inv[:, n, NS_TOK:], rg[:, n, NS_TOK:],
                                           0.0, ALU.mult, ALU.add)
            e.then_inc(scan_done, 1)
            dve.wait_ge(scan_done, 1)
            dve.wait_ge(gelu_ready, 1)
            dve.tensor_tensor(z2[:, CG:CG + 8, :], z2[:, CG:CG + 8, :], xc[:], ALU.mult).then_inc(outc_ready, 1)
            dve.wait_ge(doh_ready, 1)
            dve.wait_ge(outc_ready, 1)
            dve.tensor_tensor(mol[:, 0:8, :], z2[:, CG:CG + 8, :], moh[:, 0:8, :].bitcast(F32),
                              ALU.subtract).then_inc(dol_ready, 1)
            dve.wait_ge(h_outs, 16)
            dve.wait_ge(tab2_in, 32)
            cosb = tab[:, 0, :].unsqueeze(1).to_broadcast([P, 4, T])
            sinb = tab[:, 1, :].unsqueeze(1).to_broadcast([P, 4, T])
            for k, base_t in enumerate((DQ, DK)):
                x1 = z2[:, base_t:base_t + 8, :].rearrange("p (h e) t -> p h e t", e=2)[:, :, 0, :]
                x2 = z2[:, base_t:base_t + 8, :].rearrange("p (h e) t -> p h e t", e=2)[:, :, 1, :]
                dve.tensor_tensor(rr[:, 0], x1, cosb, ALU.mult)
                dve.tensor_tensor(rr[:, 1], x2, sinb, ALU.mult).then_inc(rope2_d, 1)
                dve.wait_ge(rope2_d, 2 * k + 1)
                dve.wait_ge(rope2_p, 2 * k + 1)
                dve.tensor_tensor(x1, rr[:, 0], rr[:, 1], ALU.subtract).then_inc(rope2_d, 1)
                dve.wait_ge(rope2_d, 2 * k + 2)
            dve.wait_ge(s0_in_s, 16)
            for h in range(4):
                q8 = z2[:, DQ + 2 * h:DQ + 2 * h + 2, 0:NS_TOK]
                if h >= 2:
                    dve.wait_ge(do_psum, h - 1)
                dve.tensor_tensor(qd[:, h % 2], q8, decq[:, h, :].unsqueeze(1).to_broadcast([P, 2, NS_TOK]),
                                  ALU.mult).then_inc(qd_ready, 1)
                dve.wait_ge(ds_psum, h + 1)
                dve.wait_ge(mask_in[h % 2], 16 * (h // 2 + 1))
                if h == 0:
                    dve.wait_ge(rope2_p, 4)
                dve.tensor_tensor(pT[0:80, h % 2, 0:336], PS[0:80, 3, 0:336], dmask[0:80, h % 2, 0:336],
                                  ALU.mult)
                dve.tensor_tensor(pT[:, h % 2, 336:720], PS[:, 4, 0:384], dmask[:, h % 2, 336:720],
                                  ALU.mult).then_inc(pT_ready, 1)
                dve.wait_ge(osd_ready, h + 1)
                ch.link(dve.reciprocal(osd[:], osd[:]))
                for e_ in range(2):
                    e = dve.scalar_tensor_tensor(osq[:, e_, :], PS[:, 5 + e_, 0:T], gcol("dn", e_), osd[:],
                                                 ALU.mult, ALU.mult)
                ch.link(e)
                dve.wait_ge(silu_ready, 1)
                dg = z2[:, DG + 2 * h:DG + 2 * h + 2, :]
                dve.tensor_tensor(dg, dg, osq[:], ALU.mult).then_inc(od_ready, 1)
                dve.wait_ge(st_psum, 2 * h + 1)
                if h >= 2:
                    dve.wait_ge(st_out[h % 2], 32)
                dve.scalar_tensor_tensor(so[:, h % 2], s0[:, :, h, :], float(np.float32(GAMMA[h] ** NS_TOK)),
                                         PS[:, 7, :].rearrange("p (a b) -> p a b", a=2),
                                         ALU.mult, ALU.add).then_inc(st_sample, 1)
                dve.wait_ge(doh_ready, h + 2)
                dve.wait_ge(od_ready, h + 1)
                dve.tensor_tensor(mol[:, 8 + 2 * h:10 + 2 * h, :], dg,
                                  moh[:, 8 + 2 * h:10 + 2 * h, :].bitcast(F32),
                                  ALU.subtract).then_inc(dol_ready, 1)
            with dve.Fori(0, 2) as i:
                for c in range(2):
                    step(U_CDOUT + CU * c, i, 2 * CU)
                    take_added(U_CDOUT + CU * c, G_CDOUT + c, x4[:, i * 2 + c], i, 2 * CU)
            norm_prep(3)
            mlp(3, U_MLP1, G_MLP1, 1, True)(0)
            with dve.Fori(1, 3) as f:
                mlp(3, U_MLP1, G_MLP1, 1, False)(f)
            mlp(3, U_MLP1, G_MLP1, 1, False, last=True)(3)

        @block.tensor
        def _(pe):
            def product(u, j, kt, rh, rl, first, last, bank0, m=4, i=None, su=0, width=T):
                s = u % NR
                for o in range(m):
                    c = 512 * j + P * o
                    wh, wl = w_hi[:, s, c:c + P], w_lo[:, s, c:c + P]
                    out = PS[:, bank0 + o, 0:width]
                    pe.matmul(out, wh, rh, start=first, stop=False)
                    pe.matmul(out, wh, rl, start=False, stop=False)
                    mm = pe.matmul(out, wl, rh, start=False, stop=last)
                return mm

            def chunk(u0, g, xh, xl, i=None, su=0, sg=0, need=None, hook=None):
                if g >= 2 or i is not None:
                    pe.wait_ge(evac, at(i, sg, g - 1))
                for k in range(CU):
                    if need:
                        need(k)
                    pe.wait_ge(lo_ready, at(i, su, u0 + k + 1))
                    for j in range(2):
                        kt = 2 * k + j
                        mm = product(u0 + k, j, kt, xh[:, kt, :], xl[:, kt, :], kt == 0, kt == KT - 1,
                                     4 * (g % 2))
                    mm.then_inc(unit_done, 1)
                    if hook and k == 5:
                        hook()

            def need_x(n):
                return lambda k: pe.wait_ge(xl_ready, 16 * n + 2 * k + 2)

            def sum_squares(n):
                def f():
                    pe.wait_ge(ssq_ready, n + 1)
                    if n:
                        pe.wait_ge(evac, NORM_G[n])
                    for j in range(4):
                        mm = pe.matmul(PS[:, SB(n), 0:T], ones, ssq[:, j, :], start=j == 0, stop=j == 3)
                    mm.then_inc(ssum_done, 1)
                return f

            def turn(tasks):
                for t in tasks:
                    w = t["w"]
                    if t["n"]:
                        ni = t["ni"]
                        pe.wait_ge(sq_ready, ni + 1)
                        if ni >= 2:
                            pe.wait_ge(sd_ready, ni - 1)
                        pe.matmul(PS[:, ni % 2, 0:w], t["m"], sqb[:, ni % 2, 0:w], start=True,
                                  stop=True).then_inc(msq_ready, 1)
                    if t["tab"] is not None:
                        ri = t["ri"]
                        pe.wait_ge(ab_ready, ri + 1)
                        if t["j"] >= 2 and ri >= 2:
                            pe.wait_ge(turned, t["j"] - 1)
                        out = PS[:, 2 + ri % 2, 0:T]
                        pe.matmul(out, ident, ra[:, ri % 2, :], start=True, stop=False)
                        pe.matmul(out, swap, rb[:, ri % 2, :], start=False, stop=True).then_inc(rot_ready, 1)

            def attend(g0, scores, values):
                for s in range(8 + 3):
                    if s < 8:
                        g = g0 + s
                        if s >= 2:
                            pe.wait_ge(smax, g - 1)
                        for q, (t0, k0, k1) in enumerate(QT):
                            o = SEG[q] - 416 * (q // 2)
                            mm = scores(s, PS[:, 2 * (g % 2) + q // 2, o:o + k1 - k0], t0, k0, k1)
                        mm.then_inc(sc_psum, 1)
                    if 2 <= s < 10:
                        g = g0 + s - 2
                        pe.wait_ge(pn_ready, g + 1)
                        if s >= 3:
                            pe.wait_ge(pta_ready, g)
                            pe.wait_ge(ptb_ready, g)
                        for a, (q, k) in enumerate(((0, 0), (1, 2), (2, 2), (2, 3))):
                            o = SEG[q] + KTILE[k][0] - QT[q][1]
                            pe.transpose(PS[:, 4, P * a:P * a + P], pr[:, g % 3, o:o + P], ident)
                        for q in range(3):
                            o = SEG[q] + KTILE[1][0] - QT[q][1]
                            mm = pe.transpose(PS[0:80, 5, P * q:P * q + P], pr[:, g % 3, o:o + 80], ident)
                        mm.then_inc(pt_psum, 1)
                    if s >= 3:
                        g = g0 + s - 3
                        h = s - 3
                        pe.wait_ge(pta_ready, g + 1)
                        pe.wait_ge(ptb_ready, g + 1)
                        if s >= 5:
                            pe.wait_ge(mol_ready, g - 1)
                        for q, (t0, t1_) in enumerate(QN):
                            out = PS[:, 6 + g % 2, t0:t1_]
                            n = t1_ - t0
                            full = {0: [(0, 0)], 1: [(1, 2)], 2: [(2, 2), (3, 3)]}[q]
                            pe.matmul(out, values(h, 1)[0:80], ptb[0:80, g % 2, q, 0:n], start=True,
                                      stop=False)
                            for a, (slot, k) in enumerate(full):
                                mm = pe.matmul(out, values(h, k), pta[:, g % 2, slot, 0:n], start=False,
                                               stop=a == len(full) - 1)
                        mm.then_inc(o_psum, 1)

            pe.wait_ge(const_in, 48)
            chunk(U_ABIN, 0, xh, xl, need=need_x(0), hook=sum_squares(0))
            pe.wait_ge(rms_ready, 1)
            chunk(U_ABIN + CU, 1, xh, xl)
            chunk(U_ABIN + 2 * CU, 2, xh, xl)
            with pe.Fori(1, 3) as i:
                for c in range(2):
                    chunk(U_ABIN + CU * (1 + c), 1 + c, xh, xl, i, 2 * CU, 2)
            pe.wait_ge(evac, N_ABIN)
            pe.wait_ge(latsq, 1)
            for j in range(4):
                mm = pe.matmul(PS[:, 0, 0:T], ones, sqm[:, j, :], start=j == 0, stop=j == 3)
            mm.then_inc(latms, 1)
            pe.wait_ge(latsq, 2)
            for j in range(2):
                mm = pe.matmul(PS[:, 1, 0:T], ones, sqm[:, 4 + j, :], start=j == 0, stop=j == 1)
            mm.then_inc(latms, 1)
            for q, (t0, _, _) in enumerate(QT):
                pe.transpose(PS[:, 2, 16 * q:16 * q + 16], zt[0:16, WI, t0:t0 + P], ident[0:16, 0:16])
            for c in range(2):
                pe.transpose(PS[0:80, 4, P * c:P * c + P], zt[:, VA + c, 0:80], ident)
                for k in range(2):
                    a, b = TT[1 + k]
                    mm = pe.transpose(PS[:, 3, 256 * k + P * c:256 * k + P * c + P], zt[:, VA + c, a:b], ident)
            mm.then_inc(tok_psum, 1)
            pe.wait_ge(latsd, 2)
            pe.wait_ge(tok_copied, 1)
            turn(TURN_A)
            pe.wait_ge(kpad_ready, 1)
            pe.wait_ge(turned, N_TURN_A)
            for h in range(16):
                if h >= 2:
                    pe.wait_ge(relu_ready, h - 1)
                b = 2 * (h % 2)
                for q, (t0, k0, k1) in enumerate(QT):
                    o = SEG[q] - 416 * (q // 2)
                    mm = pe.matmul(PS[:, b + q // 2, o:o + k1 - k0], zt[:, QI + h // 2, t0:t0 + P],
                                   kpad[:, h % 2, k0:k1], start=True, stop=True)
                mm.then_inc(idx_psum, 1)
            pe.wait_ge(latl_ready, 1)
            for c in range(3):
                if c:
                    pe.wait_ge(qkv_evac, c)
                for k in range(2):
                    u = U_UQ + 2 * c + k
                    pe.wait_ge(lo_ready, u + 1)
                    for j in range(2):
                        kt = 2 * k + j
                        mm = product(u, j, kt, qlath[:, kt, :], qlatl[:, kt, :], kt == 0, kt == 3, 4)
                    mm.then_inc(unit_done, 1)
            pe.wait_ge(relu_ready, 16)
            pe.wait_ge(qkv_evac, 3)

            def scores_a(h, out, t0, k0, k1):
                return pe.matmul(out, zt[:, QA + h, t0:t0 + P], kA[:, h // 4, k0:k1], start=True, stop=True)

            attend(0, scores_a, lambda h, k: vA[:, k, P * (h // 4):P * (h // 4) + P])
            pe.wait_ge(mol_ready, 8)
            for c in range(2):
                u = U_KN + c
                pe.wait_ge(lo_ready, u + 1)
                for j in range(2):
                    mm = product(u, j, j, lath[:, j, :], latl[:, j, :], j == 0, j == 1, 4 * c, width=KEYS)
                mm.then_inc(unit_done, 1)
            for c in range(2):
                u = U_V + c
                s = u % NR
                pe.wait_ge(lo_ready, u + 1)
                pe.wait_ge(qkv_evac, 4 + c)
                for k, (a, b) in enumerate(KTILE):
                    out = PS[0:b - a, 4 * c + k, :]
                    for j in range(2):
                        wh, wl = w_hi[:, s, 512 * j:512 * j + 512], w_lo[:, s, 512 * j:512 * j + 512]
                        pe.matmul(out, lath[:, j, a:b], wh, start=j == 0, stop=False)
                        pe.matmul(out, latl[:, j, a:b], wh, start=False, stop=False)
                        mm = pe.matmul(out, lath[:, j, a:b], wl, start=False, stop=j == 1)
                mm.then_inc(unit_done, 1)
            pe.wait_ge(qkv_evac, 7)
            turn(TURN_B)
            pe.wait_ge(turned, len(TURN_A) + len(TURN_B))

            def scores_b(h, out, t0, k0, k1):
                pe.matmul(out, qb[:, h, t0:t0 + P], kn[:, h, k0:k1], start=True, stop=False)
                return pe.matmul(out, qb[:, 8 + h // 2, t0:t0 + P], kpad[:, 2 + h % 2, k0:k1], start=False,
                                 stop=True)

            attend(8, scores_b, lambda h, k: vB[:, k, P * h:P * h + P])
            pe.wait_ge(mol_ready, 16)
            with pe.Fori(0, 2) as i:
                for c in range(2):
                    chunk(U_ABOUT + CU * c, G_ABOUT + c, moh, mol, i, 2 * CU, 2)

            def mlp(n, u_mlp, g_mlp, L, whole):
                def body(f):
                    for c in range(4):
                        if whole and c == 1:
                            pe.wait_ge(rms_ready, n + 1)
                        chunk(u_mlp + CU * c, g_mlp + c, xh, xl, f, 64, 8,
                              need=need_x(n) if whole and c == 0 else None,
                              hook=sum_squares(n) if whole and c == 0 else None)
                    for c in range(4):
                        chunk(u_mlp + 32 + CU * c, g_mlp + 4 + c, hh, hl, f, 64, 8,
                              need=(lambda k: pe.wait_ge(hl_ready, at(f, 4, 16 * L + k // 2 + 1)))
                              if c == 0 else None)
                return body

            mlp(1, U_MLP0, G_MLP0, 0, True)(0)
            with pe.Fori(1, 4) as f:
                mlp(1, U_MLP0, G_MLP0, 0, False)(f)
            chunk(U_CDIN, G_CDIN, xh, xl, need=need_x(2), hook=sum_squares(2))
            pe.wait_ge(rms_ready, 3)
            chunk(U_CDIN + CU, G_CDIN + 1, xh, xl)
            with pe.Fori(1, 6) as i:
                for c in range(2):
                    chunk(U_CDIN + CU * c, G_CDIN + c, xh, xl, i, 2 * CU, 2)
            pe.wait_ge(xcl_ready, 1)
            pe.wait_ge(evac, G_CDIN + 12)
            for n in range(16):
                u = U_GATE + n // 8
                s, c = u % NR, P * (n % 8)
                if n % 8 == 0:
                    pe.wait_ge(lo_ready, u + 1)
                if n >= 8:
                    pe.wait_ge(gate_ready, n - 7)
                wh, wl = w_hi[:, s, c:c + P], w_lo[:, s, c:c + P]
                out = PS[:, n % 8, 0:T]
                pe.matmul(out, wh, moh[:, 8 + n % 8, :], start=True, stop=False)
                pe.matmul(out, wh, mol[:, 8 + n % 8, :], start=False, stop=False)
                mm = pe.matmul(out, wl, moh[:, 8 + n % 8, :], start=False, stop=True)
                mm.then_inc(unit_done if n % 8 == 7 else gate_psum, 1)
            pe.wait_ge(gate_ready, 16)
            pe.wait_ge(rope2_d, 4)
            pe.wait_ge(rope2_p, 4)
            for h in range(4):
                kq = [DK + 2 * h, DK + 2 * h + 1]
                vq = [DV + 2 * h, DV + 2 * h + 1]
                if h:
                    pe.wait_ge(ktok_ready, h)
                    pe.wait_ge(st_prompt, h)
                for d in range(2):
                    pe.transpose(PS[0:80, 1, P * d:P * d + P], z2[:, kq[d], 0:80], ident)
                    pe.transpose(PS[0:80, 1, 256 + P * d:256 + P * d + P], z2[:, vq[d], 0:80], ident)
                    for k in range(2):
                        a, b = TT[1 + k]
                        o = 256 * k + P * d
                        pe.transpose(PS[:, 0, o:o + P], z2[:, kq[d], a:b], ident)
                        mm = pe.transpose(PS[:, 2, o:o + P], z2[:, vq[d], a:b], ident)
                mm.then_inc(kv_psum, 1)
                if h:
                    pe.wait_ge(pT_ready, h)
                    pe.wait_ge(osd_ready, h)
                for j, (bank, o, i0) in enumerate(((3, 0, 0), (4, 0, 80), (4, 256, 208))):
                    a, b = TT[j]
                    for d in range(2):
                        mm = pe.matmul(PS[0:b - a, bank, o:o + T - i0], z2[:, kq[d], a:b],
                                       z2[:, DQ + 2 * h + d, i0:T], start=d == 0, stop=d == 1)
                mm.then_inc(ds_psum, 1)
                pe.wait_ge(ktok_ready, h + 1)
                pe.wait_ge(pT_ready, h + 1)
                pe.wait_ge(qd_ready, h + 1)
                if h:
                    pe.wait_ge(od_ready, h)
                for e in range(2):
                    bank = 5 + e
                    c = P * e
                    pe.matmul(PS[:, bank, 0:T], vtok[0:80, h % 2, 0, c:c + P], pT[0:80, h % 2, 0:336],
                              start=True, stop=False)
                    pe.matmul(PS[:, bank, 80:T], vtok[:, h % 2, 1, c:c + P], pT[:, h % 2, 336:592],
                              start=False, stop=False)
                    pe.matmul(PS[:, bank, 208:T], vtok[:, h % 2, 2, c:c + P], pT[:, h % 2, 592:720],
                              start=False, stop=False)
                    for d in range(2):
                        mm = pe.matmul(PS[:, bank, 0:NS_TOK], s0[:, d, h, c:c + P], qd[:, h % 2, d, :],
                                       start=False, stop=d == 1)
                mm.then_inc(do_psum, 1)
                if h:
                    pe.wait_ge(st_sample, h)
                for d in range(2):
                    mm = pe.matmul(PS[:, 7, 256 * d:256 * d + 256], ktok[0:64, h % 2, 0, P * d:P * d + P],
                                   vtok[0:64, h % 2, 0, :], start=True, stop=True)
                mm.then_inc(st_psum, 1)
                for d in range(2):
                    out = PS[:, 0, 256 * d:256 * d + 256]
                    pe.matmul(out, ktok[64:80, h % 2, 0, P * d:P * d + P], vtok[64:80, h % 2, 0, :],
                              start=True, stop=False)
                    for k in (1, 2):
                        mm = pe.matmul(out, ktok[:, h % 2, k, P * d:P * d + P], vtok[:, h % 2, k, :],
                                       start=False, stop=k == 2)
                mm.then_inc(st_psum, 1)
                pe.wait_ge(osq_ready, h + 1)
                for e in range(2):
                    mm = pe.matmul(PS[:, 4, 0:T], ones, osq[:, e, :], start=e == 0, stop=e == 1)
                mm.then_inc(oms_psum, 1)
            pe.wait_ge(dol_ready, 5)
            pe.wait_ge(st_prompt, 4)
            pe.wait_ge(st_sample, 4)
            with pe.Fori(0, 2) as i:
                for c in range(2):
                    chunk(U_CDOUT + CU * c, G_CDOUT + c, moh, mol, i, 2 * CU, 2)
            mlp(3, U_MLP1, G_MLP1, 1, True)(0)
            with pe.Fori(1, 4) as f:
                mlp(3, U_MLP1, G_MLP1, 1, False)(f)

        @block.gpsimd
        def _(pool):
            ch = Chain(pool, pchain)

            def sum_squares(n):
                if n == 0:
                    pool.wait_ge(x_in_s, 16)
                else:
                    pool.wait_ge(evac, X_FINAL[n])
                for g in range(4):
                    xs = x[:, 4 * g:4 * g + 4, :]
                    if g == 0:
                        ch.link(pool.tensor_tensor(ssq[:], xs, xs, ALU.mult))
                    else:
                        ch.link(pool.tensor_tensor(sst[:], xs, xs, ALU.mult))
                        e = pool.tensor_tensor(ssq[:], ssq[:], sst[:], ALU.add)
                        if g < 3:
                            ch.link(e)
                e.then_inc(ssq_ready, 1)

            outs = [0]

            def send(dst, src):
                pool.dma_start(dst, src).then_inc(out_s, 16)
                outs[0] += 16

            pool.memset(kpad[:], 0.0).then_inc(pad_zero, 1)
            sum_squares(0)
            pool.wait_ge(evac, N_ABIN)
            send(v_out, zt[:, VA:VA + 2, :])
            pool.wait_ge(lat_ready, 1)
            send(lat_out, lat[:, :, PAST:])
            pool.wait_ge(turned, KK_J + 1)
            send(k_out, kA[:, :, PAST:])
            send(kk_out, kk[:, PAST:])
            pool.wait_ge(mol_ready, 16)
            pool.wait_ge(out_s, outs[0])
            sum_squares(1)
            sum_squares(2)
            pool.wait_ge(mol_ready, 16)
            pool.dma_start(tab[:, 0:2, :], tabs_in[:, 4:6, :]).then_inc(tab2_in, 16)
            pool.dma_start(decq[:], decq_in).then_inc(tab2_in, 16)
            pool.wait_ge(ssum_done, 3)
            pool.dma_start(cxp[:, :, 0:3], conv_in).then_inc(cx_in, 16)
            pool.memset(cxp[:, :, 3 + NS_TOK:6 + NS_TOK], 0.0).then_inc(cx_zero, 1)
            pool.wait_ge(cx_copied, 1)
            pool.dma_start(conv_out[:, :, 0, :], cxp[:, :, NS_TOK:NS_TOK + 3]).then_inc(conv_outs, 16)
            pool.dma_start(conv_out[:, :, 1, :], cxp[:, :, T + 3:T + 6]).then_inc(conv_outs, 16)
            cg = z2[:, CG:CG + 8, :]
            pool.wait_ge(evac, G_CDIN + 4)
            ch.link(pool.tensor_tensor(t1[:], cg, cg, ALU.mult))
            ch.link(pool.tensor_scalar(t1[:], t1[:], 0.044715, 1.0, ALU.mult, ALU.add))
            pool.tensor_tensor(t1[:], t1[:], cg, ALU.mult).then_inc(gelu_in, 1)
            pool.wait_ge(gelu_sig, 1)
            pool.tensor_tensor(cg, cg, t1[:], ALU.mult).then_inc(gelu_ready, 1)
            pool.wait_ge(gate_ready, 16)
            pool.wait_ge(xc_ready, 16)
            pool.tensor_tensor(ig[:], ig[:], xc[:], ALU.mult).then_inc(igx_ready, 1)
            pool.wait_ge(silu_sig, 1)
            dg = z2[:, DG:DG + 8, :]
            pool.tensor_tensor(dg, dg, t1[:], ALU.mult).then_inc(silu_ready, 1)
            pool.wait_ge(scan_done, 1)
            for e, c in enumerate((NS_TOK - 1, T - 1)):
                ch.link(pool.tensor_copy(hlast[:, :, e], xc[:, :, c]))
            pool.dma_start(h_out, hlast[:]).then_inc(h_outs, 16)
            pool.wait_ge(outc_ready, 1)
            pool.wait_ge(h_outs, 16)
            pool.wait_ge(tab2_in, 32)
            pool.wait_ge(silu_ready, 1)
            pool.wait_ge(dol_ready, 1)
            pool.dma_start(s0[:], s0_in).then_inc(s0_in_s, 16)
            cosb = tab[:, 0, :].unsqueeze(1).to_broadcast([P, 4, T])
            sinb = tab[:, 1, :].unsqueeze(1).to_broadcast([P, 4, T])
            for k, base_t in enumerate((DQ, DK)):
                x1 = z2[:, base_t:base_t + 8, :].rearrange("p (h e) t -> p h e t", e=2)[:, :, 0, :]
                x2 = z2[:, base_t:base_t + 8, :].rearrange("p (h e) t -> p h e t", e=2)[:, :, 1, :]
                pool.tensor_tensor(rr[:, 2], x1, sinb, ALU.mult)
                pool.tensor_tensor(rr[:, 3], x2, cosb, ALU.mult).then_inc(rope2_p, 1)
                pool.wait_ge(rope2_p, 2 * k + 1)
                pool.wait_ge(rope2_d, 2 * k + 1)
                pool.tensor_tensor(x2, rr[:, 2], rr[:, 3], ALU.add).then_inc(rope2_p, 1)
                pool.wait_ge(rope2_p, 2 * k + 2)
            pool.wait_ge(rope2_d, 4)
            for h in range(4):
                if h >= 2:
                    pool.wait_ge(pT_ready, h - 1)
                pool.dma_start(dmask[:, h % 2, :], ret_in[:, h, :]).then_inc(mask_in[h % 2], 16)
                if h >= 1:
                    send_state(pool, h - 1, so, s_out, st_sample, st_prompt, st_out)
            send_state(pool, 3, so, s_out, st_sample, st_prompt, st_out)
            for h in range(2):
                pool.wait_ge(st_out[h], 64)
            sum_squares(3)
            pool.wait_ge(evac, G_END)
            send(y_out, x[:])
            pool.wait_ge(out_s, outs[0])
            pool.wait_ge(conv_outs, 32)


def send_state(pool, h, so, s_out, st_sample, st_prompt, st_out):
    pool.wait_ge(st_sample, h + 1)
    pool.dma_start(s_out[:, 0, h], so[:, h % 2]).then_inc(st_out[h % 2], 16)
    pool.wait_ge(st_prompt, h + 1)
    pool.dma_start(s_out[:, 1, h], so[:, 2 + h % 2]).then_inc(st_out[h % 2], 16)


def constants():
    pos = np.concatenate([PAST + np.arange(NS_TOK), np.arange(TP)]).astype(np.float32)

    def angles(dim):
        inv = (np.float32(10000.0) ** (-np.arange(0, dim, 2, dtype=np.float32) / np.float32(dim))).astype(np.float32)
        return (inv[:, None] * pos[None, :]).astype(np.float32).astype(np.float64)

    tabs = np.zeros((P, 6, T), np.float32)
    a = np.tile(angles(128), (2, 1))
    tabs[:, 0], tabs[:, 1] = np.cos(a), np.sin(a)
    a = np.tile(angles(64), (4, 1))
    tabs[:, 2], tabs[:, 3] = np.cos(a), np.sin(a)
    for k in (1, 3):
        tabs[64:, k] *= -1
    a = angles(256)
    tabs[:, 4], tabs[:, 5] = np.cos(a), np.sin(a)

    cst = np.zeros((P, 4, P), np.float32)
    p = np.arange(P)
    cst[p, 0, p] = 1
    cst[p, 1, (p + 64) % P] = 1
    cst[:, 2] = 1
    cst[:, 3] = (p[:, None] // 32) % 2 == (p[None, :] // 32) % 2

    tok_c = np.concatenate([(PAST + np.arange(NS_TOK)) // CHUNK, np.zeros(NMETA, int), 1 + np.arange(SEQ) // CHUNK])
    tok_g = np.arange(T) >= NS_TOK
    key_c = np.concatenate([np.arange(PAST) // CHUNK, tok_c])
    key_g = np.concatenate([np.zeros(PAST, bool), tok_g])
    adm = np.zeros((P, SEG[3]), np.float32)
    for q, (t0, k0, k1) in enumerate(QT):
        n = QN[q][1] - QN[q][0]
        ok = (tok_g[t0:t0 + n, None] == key_g[None, k0:k1]) & (key_c[None, k0:k1] <= tok_c[t0:t0 + n, None])
        adm[0:n, SEG[q]:SEG[q + 1]] = np.where(ok, 0, NEG)

    lg = [np.log(np.float32(g)).astype(np.float64) for g in GAMMA]
    ret = np.zeros((P, 4, 720), np.float32)
    kdec = np.zeros((P, 4, 3), np.float32)
    loc = np.concatenate([np.arange(NS_TOK), np.arange(TP)])
    glen = np.concatenate([np.full(NS_TOK, NS_TOK), np.full(TP, TP)])
    for h in range(4):
        o = 0
        for t, (a, b) in enumerate(TT):
            i0 = (0, 80, 208)[t]
            i = np.arange(i0, T)
            j = np.arange(a, b)
            d = i[None, :] - j[:, None]
            ok = (d >= 0) & (tok_g[i][None, :] == tok_g[j][:, None])
            ret[0:b - a, h, o:o + T - i0] = np.where(ok, np.exp(lg[h] * np.maximum(d, 0)), 0) / 16
            kdec[0:b - a, h, t] = np.exp(lg[h] * (glen[j] - 1 - loc[j])) / 16
            o += T - i0
    decq = np.zeros((P, 4, NS_TOK), np.float32)
    for h in range(4):
        decq[:, h] = np.exp(lg[h] * (np.arange(NS_TOK) + 1))[None, :]
    return tabs, cst, adm, ret, kdec.reshape(P, 12), decq


def kernel(**inputs):
    import concourse.bacc as _bacc
    from concourse.bass_utils import run_bass_kernel_spmd as _run
    np_ = np
    a = {k: np_.asarray(v) for k, v in inputs.items()}
    f4 = np_.float32
    tabs, cst, adm, ret, kdec, decq = constants()

    def cols(v):
        return v.reshape(-1, P).T

    def pair_rows(v):
        return np_.concatenate([v[:32], v[:32], v[32:], v[32:]])[:, None]

    tok = np_.concatenate([a["x_sample"][0], a["meta_tokens"], a["x_prompt"][0]], 0)
    x_in = tok.T.reshape(KT, P, T).transpose(1, 0, 2)

    w = a["ab_w_in"][0]
    qi0 = 1536
    heads = []
    for i in range(8):
        c0, c1 = qi0 + 128 * i, qi0 + 128 * i + 64
        heads += [w[:, c0:c0 + 32], w[:, c1:c1 + 32], w[:, c0 + 32:c0 + 64], w[:, c1 + 32:c1 + 64]]
    ki, kr = 2560, 3408
    abin = np_.concatenate([w[:, 0:1280]] + heads
                           + [w[:, ki:ki + 32], w[:, kr:kr + 32], w[:, ki + 32:ki + 64], w[:, kr + 32:kr + 64]]
                           + [w[:, 2624:2640], np_.zeros((D, 112), f4), w[:, 2640:3152], w[:, 3152:3408],
                              w[:, 1280:1536]], 1)
    uq = a["b_w_uq"][0].reshape(512, 8, 192)
    ropes = []
    for i in range(4):
        r0, r1 = uq[:, 2 * i, 128:], uq[:, 2 * i + 1, 128:]
        ropes += [r0[:, :32], r1[:, :32], r0[:, 32:], r1[:, 32:]]
    uqp = np_.concatenate([uq[:, :, :128].reshape(512, 1024)] + ropes, 1)
    ukv = a["b_w_ukv"][0].reshape(256, 8, 256)

    def units(m):
        k, n = m.shape
        return m.reshape(k // 256, 2, P, n // 512, 512).transpose(3, 0, 2, 1, 4).reshape(-1, P, UNIT)

    def mlp_units(i):
        up, down = a["mlp_w_up"][i], a["mlp_w_down"][i]
        return [x_ for f in range(4) for x_ in (units(up[:, D * f:D * f + D]), units(down[D * f:D * f + D]))]

    gate = [a[n][0].transpose(1, 0, 2).reshape(1, P, UNIT) for n in ("c_gate_a_w", "c_gate_x_w")]
    wstream = np_.concatenate(
        [units(abin), units(uqp), units(np_.ascontiguousarray(ukv[:, :, :128]).reshape(256, 1024)),
         units(np_.ascontiguousarray(ukv[:, :, 128:]).reshape(256, 1024)), units(a["ab_w_out"][0])]
        + mlp_units(0) + [units(a["cd_w_in"][0])] + gate + [units(a["cd_w_out"][0])] + mlp_units(1), 0)

    norms = [a["norm_mix"][0], a["norm_mlp"][0], a["norm_mix"][1], a["norm_mlp"][1]]
    kkg = np_.ones((P, 1), f4)
    kkg[32:64, 0], kkg[96:128, 0] = a["b_kr_norm"][0][:32], a["b_kr_norm"][0][32:]
    mkr = np_.zeros((P, 1), f4)
    mkr[32:64] = mkr[96:128] = 1
    gains = np_.concatenate(
        [cols(n) for n in norms]
        + [a["a_q_norm"][0][:, None], a["a_k_norm"][0][:, None], kkg, pair_rows(a["b_qr_norm"][0]),
           a["b_qn_norm"][0][:, None], a["b_kn_norm"][0][:, None], cols(a["b_q_lat_norm"][0]),
           cols(a["b_kv_lat_norm"][0])]
        + [cols(a["c_conv_w"][0][j]) for j in range(4)]
        + [cols(a[n][0]) for n in ("c_conv_b", "c_gate_a_b", "c_gate_x_b", "c_lambda", "d_out_norm", "state_c_h")]
        + [np_.full((P, 1), EPS, f4), mkr, np_.where(mkr > 0, 0, 1).astype(f4), kdec, np_.zeros((P, 1), f4)], 1)
    past_k = a["cache_a_k"][0, 0].transpose(2, 1, 0)
    idx, rope = a["cache_a_kidx"][0, 0].T, a["cache_b_krope"][0, 0].T
    past_kk = np_.concatenate([idx[:32], rope[:32], idx[32:], rope[32:]], 0)
    past_v = a["cache_a_v"][0, 0].reshape(PAST, 256)
    past_lat = a["cache_b_latent"][0, 0].T.reshape(2, P, PAST).transpose(1, 0, 2)
    conv_in = a["state_c_conv"][0, 0].T.reshape(8, P, 3).transpose(1, 0, 2)
    s0_in = a["state_d_s"][0, 0].reshape(4, 2, P, 256).transpose(2, 1, 0, 3)

    ins = [("x_in", x_in), ("wstream", wstream), ("gains", gains), ("cst", cst), ("tabs", tabs), ("adm", adm),
           ("ret", ret), ("decq", decq), ("past_k", past_k), ("past_kk", past_kk), ("past_v", past_v),
           ("past_lat", past_lat), ("conv_in", conv_in), ("s0_in", s0_in)]
    outs = [("y", (P, KT, T)), ("k", (P, 2, T)), ("v", (P, 2, T)), ("kk", (P, T)), ("lat", (P, 2, T)),
            ("conv", (P, 8, 2, 3)), ("h", (P, 8, 2)), ("s", (P, 2, 4, 2, 256))]
    nc = _bacc.Bacc("TRN2", target_bir_lowering=False, num_devices=1)
    arrays, args = {}, []
    for name, v in ins:
        v = np_.ascontiguousarray(v)
        arrays[f"in_{name}"] = v
        args.append(nc.dram_tensor(f"in_{name}", v.shape, mybir.dt.from_np(v.dtype), kind="ExternalInput").ap())
    for name, shape in outs:
        args.append(nc.dram_tensor(f"out_{name}", shape, F32, kind="ExternalOutput").ap())
    build(nc, *args)
    r = _run(nc, [arrays], core_ids=[0])
    o = {name: np_.asarray(r.results[0][f"out_{name}"]) for name, _ in outs}

    def rows(v):
        return v.transpose(2, 1, 0).reshape(v.shape[2], -1)

    y, k, v, lat = rows(o["y"]), rows(o["k"]), rows(o["v"]), rows(o["lat"])
    kk = o["kk"].T
    kidx = np_.concatenate([kk[:, 0:32], kk[:, 64:96]], 1)
    krope = np_.concatenate([kk[:, 32:64], kk[:, 96:128]], 1)
    res = [y[NS_TOK + NMETA:][None], y[:NS_TOK][None]]
    for g, sl in ((1, slice(NS_TOK, T)), (0, slice(0, NS_TOK))):
        n = TP if g else NS_TOK
        res += [k[sl].reshape(1, 1, n, 2, P), v[sl].reshape(1, 1, n, 2, P), kidx[sl][None, None],
                lat[sl][None, None], krope[sl][None, None],
                o["conv"][:, :, g].transpose(2, 1, 0).reshape(1, 1, 3, 1024),
                o["h"][:, :, g].T.reshape(1, 1, 1024),
                o["s"][:, g].transpose(1, 2, 0, 3).reshape(1, 1, 4, 256, 256)]
    return tuple(np_.ascontiguousarray(z) for z in res)
```

```python
from contextlib import ExitStack

import numpy as np
import concourse.bass as bass
from concourse import mybir

F32 = mybir.dt.float32
F32R = mybir.dt.float32r
ACT = mybir.ActivationFunctionType
ALU = mybir.AluOpType

P = 128
D = 2048
KT = D // P
NS_TOK, NMETA, SEQ = 64, 16, 256
TP = NMETA + SEQ
T = NS_TOK + TP
PAST = 128
KEYS = PAST + T
CHUNK = 64
EPS = 1e-6

UNIT = 1024
CU = 8
NR = 4
U_ABIN, N_ABIN = 0, 7
U_UQ = U_ABIN + CU * N_ABIN
U_KN = U_UQ + 6
U_V = U_KN + 2
U_ABOUT = U_V + 2
U_MLP0 = U_ABOUT + 4 * CU
U_CDIN, N_CDIN = U_MLP0 + 32 * CU, 12
GATE_CHUNKS, GATE_AT = (2, 3, 4, 5), 7
U_CDOUT = U_CDIN + N_CDIN * CU + len(GATE_CHUNKS)
U_MLP1 = U_CDOUT + 4 * CU
N_UNITS = U_MLP1 + 32 * CU
G_ABIN = 0
G_ABOUT = G_ABIN + N_ABIN
G_MLP0 = G_ABOUT + 4
G_CDIN = G_MLP0 + 32
G_CDOUT = G_CDIN + N_CDIN
G_MLP1 = G_CDOUT + 4
G_END = G_MLP1 + 32

QA, KA, QI, KK, WI, CQ, CKV, VA = 0, 8, 10, 18, 19, 20, 24, 26
CX, CG, DK, DQ, DV, DG = 0, 8, 16, 24, 32, 40


def cd_chunk(c):
    return U_CDIN + CU * c + sum(g < c for g in GATE_CHUNKS), CU + (c in GATE_CHUNKS)


QT = [(0, 0, 208), (80, 128, 336), (208, 128, 464)]
SEG = [0, 208, 416, 752]
QN = [(0, 80), (80, 208), (208, 336)]
KTILE = [(0, 128), (128, 208), (208, 336), (336, 464)]
TT = [(0, 80), (80, 208), (208, 336)]
TOPK_S, TOPK_P = (PAST + NS_TOK) // 4, SEQ // 4
NEG, TAKEN = -1e30, -3e38

GAIN = {}
_n = 0
for _name, _w in (("norm", 64), ("aq", 1), ("ak", 1), ("kk", 1), ("qr", 1), ("qn", 1), ("kn", 1),
                  ("qlat", 4), ("kvlat", 2), ("conv_w", 32), ("conv_b", 8), ("ga_b", 8), ("gx_b", 8),
                  ("lam", 8), ("dn", 2), ("h0", 8), ("eps", 1), ("mkr", 1), ("mki", 1), ("kdec", 12),
                  ("zero", 1)):
    GAIN[_name] = _n
    _n += _w
NGAIN = _n

GAMMA = [1.0 - 2.0 ** (-5.0 - h) for h in range(4)]


def at(i, per, c):
    if i is None:
        return c
    return i * per + c


class Chain:

    def __init__(self, eng, sem):
        self.eng, self.sem, self.n = eng, sem, 0

    def mark(self, ins):
        ins.then_inc(self.sem, 1)
        self.n += 1
        return self.n

    def need(self, n):
        self.eng.wait_ge(self.sem, n)

    def link(self, ins):
        self.need(self.mark(ins))


def build(nc, x_in, wstream, gains_in, cst_in, tabs_in, adm_in, ret_in, decq_in,
          past_k, past_kk, past_v, past_lat, conv_in, s0_in,
          y_out, k_out, v_out, kk_out, lat_out, conv_out, h_out, s_out):
    ctx = ExitStack()
    with ctx:
        def sem(name):
            return ctx.enter_context(nc.semaphore(name))

        base, end = 16512, 229344
        cur = [base]

        def keep(name, shape, dt=F32):
            t = nc.alloc_sbuf_tensor_at(name, shape, dt, offset=cur[0])
            cur[0] += int(np.prod(shape[1:])) * 4
            cur[0] = (cur[0] + 31) // 32 * 32
            return t

        def place(name, shape, offset, dt=F32):
            size = int(np.prod(shape[1:])) * 4
            assert offset % 32 == 0 and offset + size <= end, (name, offset, size, end)
            return nc.alloc_sbuf_tensor_at(name, shape, dt, offset=offset)

        TB = T * 4
        x = keep("x", [P, KT, T])
        stage = keep("stage", [P, NR, UNIT])
        w_hi = keep("w_hi", [P, NR, UNIT], F32R)
        w_lo = keep("w_lo", [P, NR, UNIT], F32R)
        cst = keep("cst", [P, 4, P])
        tab_at = cur[0]
        tab = keep("tab", [P, 4, T])
        rstd = keep("rstd", [P, T])
        gains = keep("gains", [P, NGAIN])
        wiT = keep("wiT", [P, 3, 16])
        m8 = keep("m8", [P, 3, 8])
        mx = keep("mx", [P, 3, 3])
        rsum = keep("rsum", [P, 3, 3])
        sp8 = keep("sp8", [P, 2, 8])
        spt = keep("spt", [P, 4, 8])
        hlast = keep("hlast", [P, 8, 2])
        clast = keep("clast", [P, 8, 2, 3])
        cstate = keep("cstate", [P, 8, 3])
        ident, swap, ones, pairs = (cst[:, i, :] for i in range(4))

        decq = place("decq", [P, 4, NS_TOK], tab_at + 2 * TB)
        A = cur[0]
        xh = place("xh", [P, KT, T], A, F32R)
        xl = place("xl", [P, KT, T], A + KT * TB, F32R)
        moh = place("moh", [P, KT, T], A, F32R)
        mol = place("mol", [P, KT, T], A + KT * TB, F32R)
        qlath = place("qlath", [P, 4, T], A + 8 * TB, F32R)
        lath = place("lath", [P, 2, KEYS], A + 12 * TB, F32R)
        qlatl = place("qlatl", [P, 4, T], A + 24 * TB, F32R)
        latl = place("latl", [P, 2, KEYS], A + 28 * TB, F32R)
        B = A + 2 * KT * TB
        zt = place("zt", [P, 28, T], B)
        qb = place("qb", [P, 12, T], B + 12 * TB)
        kn = place("kn", [P, 8, KEYS], B)
        C = B + 28 * TB
        kpad = place("kpad", [P, 4, KEYS], C)
        C2 = C + 4 * KEYS * 4
        adm = place("adm", [P, SEG[3]], C2)
        C3 = C2 + SEG[3] * 4
        lat = place("lat", [P, 2, KEYS], C3)
        W = C3 + 2 * KEYS * 4
        sqb = place("sqb", [P, 2, KEYS], W)
        sdb = place("sdb", [P, 2, KEYS], W + 2 * KEYS * 4)
        ra = place("ra", [P, 2, T], W + 4 * KEYS * 4)
        rb = place("rb", [P, 2, T], W + 4 * KEYS * 4 + 2 * TB)
        sqm = place("sqm", [P, 6, T], W)
        sdm = place("sdm", [P, 2, T], W + 6 * TB)
        acc = place("acc", [P, SEG[3]], W)
        rt = place("rt", [P, 2, SEG[3]], W + SEG[3] * 4)
        pr = place("pr", [P, 3, SEG[3]], W)
        pta = place("pta", [P, 2, 4, P], W + 9 * 1024)
        ptb = place("ptb", [P, 2, 3, P], W + 9 * 1024 + 4096)
        V = W + 9 * 1024 + 4096 + 3072
        kA = place("kA", [P, 2, KEYS], V)
        kk = place("kk", [P, KEYS], V + 2 * KEYS * 4)
        vA = place("vA", [P, 4, 256], V + 3 * KEYS * 4)
        biasA = place("biasA", [P, SEG[3]], V + 3 * KEYS * 4 + 4096)
        vB = place("vB", [P, 4, 1024], V)
        hh = place("hh", [P, 16, T], B, F32R)
        hl = place("hl", [P, 16, T], B + 16 * TB, F32R)
        mt1 = place("mt1", [P, 4, T], B + 32 * TB)
        mt2 = place("mt2", [P, 4, T], B + 36 * TB)
        ssq = place("ssq", [P, 4, T], W)
        sst = place("sst", [P, 4, T], W + 4 * TB)
        z2 = place("z2", [P, 48, T], B)
        t1 = place("t1", [P, 8, T], B + DG * TB)
        C1 = B + 48 * TB
        cxp = place("cxp", [P, 2, T + 6], C1)
        G1 = (C1 + 2 * (T + 6) * 4 + 31) // 32 * 32
        xc = place("xc", [P, 2, T], G1)
        xch = place("xch", [P, 2, T], G1 + 2 * TB, F32R)
        xcl = place("xcl", [P, 2, T], G1 + 4 * TB, F32R)
        rg = place("rg", [P, 2, T], G1 + 6 * TB)
        ig = place("ig", [P, 2, T], G1 + 8 * TB)
        av = place("av", [P, 2, T], G1 + 10 * TB)
        tv = place("tv", [P, 2, T], G1 + 12 * TB)
        rr = place("rr", [P, 4, 2, T], C1)
        sgd = place("sgd", [P, 8, T], A + 24 * TB)
        ktok = place("ktok", [P, 2, 3, 256], C1)
        vtok = place("vtok", [P, 2, 3, 256], C1 + 6144)
        pT = place("pT", [P, 2, 720], C1 + 12288)
        dmask = place("dmask", [P, 2, 720], C1 + 12288 + 5760)
        s0 = place("s0", [P, 2, 4, 256], B)
        so = place("so", [P, 4, 2, 256], B + 8192)
        qd = place("qd", [P, 2, 2, NS_TOK], B + 16384)
        osq = place("osq", [P, 2, T], B + 17408)
        osd = place("osd", [P, T], B + 17408 + 2 * TB)

        PS = ctx.enter_context(nc.psum_tensor("PS", [P, 8, 512], F32))

        def gcol(name, i=0, rows=slice(0, P)):
            c = GAIN[name] + i
            return gains[rows, c:c + 1]

        stage_full = [sem(f"stage_full{i}") for i in range(NR)]
        hi_ready = sem("hi_ready")
        lo_ready = sem("lo_ready")
        unit_done = sem("unit_done")
        evac = sem("evac")
        const_in = sem("const_in")
        x_in_s = sem("x_in_s")
        past_in = sem("past_in")
        pad_zero = sem("pad_zero")
        xh_ready, xl_ready = sem("xh_ready"), sem("xl_ready")
        ssq_ready, ssum_done, rms_ready = sem("ssq_ready"), sem("ssum_done"), sem("rms_ready")
        dchain, achain, pchain = sem("dchain"), sem("achain"), sem("pchain")
        hh_ready, hl_ready, hsq_done = sem("hh_ready"), sem("hl_ready"), sem("hsq_done")
        sq_ready, msq_ready, sd_ready = sem("sq_ready"), sem("msq_ready"), sem("sd_ready")
        ab_ready, rot_ready, turned = sem("ab_ready"), sem("rot_ready"), sem("turned")
        latsq, latms, latsd, lat_ready, lath_ready, latl_ready = (
            sem("latsq"), sem("latms"), sem("latsd"), sem("lat_ready"), sem("lath_ready"),
            sem("latl_ready"))
        tok_psum, tok_copied = sem("tok_psum"), sem("tok_copied")
        kpad_ready = sem("kpad_ready")
        idx_psum, relu_ready, idx_added, bias_ready = (sem("idx_psum"), sem("relu_ready"),
                                                       sem("idx_added"), sem("bias_ready"))
        qkv_evac = sem("qkv_evac")
        sc_psum, smax, p_ready, pn_ready = sem("sc_psum"), sem("smax"), sem("p_ready"), sem("pn_ready")
        pt_psum, pta_ready, ptb_ready = sem("pt_psum"), sem("pta_ready"), sem("ptb_ready")
        o_psum, moh_ready, mol_ready = sem("o_psum"), sem("moh_ready"), sem("mol_ready")
        out_s = sem("out_s")
        tab2_in, cx_in, cx_copied, conv_outs = sem("tab2_in"), sem("cx_in"), sem("cx_copied"), sem("conv_outs")
        clast_ready, exp_ready, tanh_ready, asq_ready, w_ready = (
            sem("clast_ready"), sem("exp_ready"), sem("tanh_ready"), sem("asq_ready"), sem("w_ready"))
        cx_zero = sem("cx_zero")
        xc_ready, xch_ready, xcl_ready = sem("xc_ready"), sem("xch_ready"), sem("xcl_ready")
        gate_ready = sem("gate_ready")
        sqrt_ready, igx_ready, scan_done = sem("sqrt_ready"), sem("igx_ready"), sem("scan_done")
        gelu_in, gelu_sig, gelu_ready = sem("gelu_in"), sem("gelu_sig"), sem("gelu_ready")
        silu_sig, silu_ready = sem("silu_sig"), sem("silu_ready")
        outc_ready, h_outs = sem("outc_ready"), sem("h_outs")
        sp_exp, sp_abs, sp_ready = sem("sp_exp"), sem("sp_abs"), sem("sp_ready")
        rope2_d, rope2_p = sem("rope2_d"), sem("rope2_p")
        s0_in_s = sem("s0_in_s")
        mask_in = [sem("mask_in0"), sem("mask_in1")]
        kv_psum, ktok_ready, ds_psum, pT_ready, qd_ready = (sem("kv_psum"), sem("ktok_ready"),
                                                            sem("ds_psum"), sem("pT_ready"), sem("qd_ready"))
        do_psum, osq_ready, oms_psum, osd_ready, od_ready = (sem("do_psum"), sem("osq_ready"),
                                                             sem("oms_psum"), sem("osd_ready"), sem("od_ready"))
        st_psum, st_sample, st_prompt = sem("st_psum"), sem("st_sample"), sem("st_prompt")
        st_out = [sem("st_out0"), sem("st_out1")]
        doh_ready, dol_ready = sem("doh_ready"), sem("dol_ready")

        block = ctx.enter_context(nc.Block())
        cosb = tab[:, 0, :].unsqueeze(1).to_broadcast([P, 2, T])
        sinb = tab[:, 1, :].unsqueeze(1).to_broadcast([P, 2, T])

        def halves(k):
            t0 = (DK, DQ)[k // 2] + 4 * (k % 2)
            v = z2[:, t0:t0 + 4, :].rearrange("p (h e) t -> p h e t", e=2)
            return v[:, :, 0, :], v[:, :, 1, :]

        X_FINAL = [0, G_MLP0, G_CDIN, G_MLP1]
        NORM_G = [G_ABIN, G_MLP0, G_CDIN, G_MLP1]

        def SB(n):
            return 4 * (1 - NORM_G[n] % 2) + 3

        def turn_tasks():
            a = [dict(src=zt[:, KA + c, :], dst=kA[:, c, PAST:], g=gcol("ak"), m=ones, n=128, tab=0)
                 for c in range(2)]
            a += [dict(src=zt[:, KK, :], dst=kk[:, PAST:], g=gcol("kk"), m=pairs, n=64, tab=2, kk=True)]
            a += [dict(src=zt[:, QI + c, :], dst=zt[:, QI + c, :], g=None, n=0, tab=2) for c in range(8)]
            a += [dict(src=zt[:, QA + c, :], dst=zt[:, QA + c, :], g=gcol("aq"), m=ones, n=128, tab=0)
                  for c in range(8)]
            b = [dict(src=qb[:, c, :], dst=qb[:, c, :], g=gcol("qn"), m=ones, n=128, tab=None)
                 for c in range(8)]
            b += [dict(src=qb[:, 8 + c, :], dst=qb[:, 8 + c, :], g=gcol("qr"), m=pairs, n=64, tab=2)
                  for c in range(4)]
            b += [dict(src=kn[:, c, :], dst=kn[:, c, :], g=gcol("kn"), m=ones, n=128, tab=None)
                  for c in range(8)]
            ni = ri = 0
            for j, t in enumerate(a + b):
                t["j"], t["ni"], t["ri"] = j, ni, ri
                t["w"] = KEYS if t["dst"].shape[-1] == KEYS else T
                ni += bool(t["n"])
                ri += t["tab"] is not None
            return a, b

        TURN_A, TURN_B = turn_tasks()
        N_TURN_A = len(TURN_A)
        KK_J = 2

        @block.sync
        def _(sp):
            for s in range(NR):
                sp.dma_start(stage[:, s, :], wstream[s]).then_inc(stage_full[s], 16)
            with sp.Fori(1, N_UNITS // NR) as i:
                for s in range(NR):
                    sp.wait_ge(lo_ready, i * NR + (s + 1 - NR))
                    sp.dma_start(stage[:, s, :], wstream[i * NR + s]).then_inc(stage_full[s], 16)
            for u in range(N_UNITS // NR * NR, N_UNITS):
                sp.wait_ge(lo_ready, u - NR + 1)
                sp.dma_start(stage[:, u % NR, :], wstream[u]).then_inc(stage_full[u % NR], 16)

        @block.scalar
        def _(act):
            ch = Chain(act, achain)

            def split(u, i=None, per=0):
                s = u % NR
                act.wait_ge(stage_full[s], at(i, 16 * per // NR, 16 * (u // NR + 1)))
                if u >= NR:
                    act.wait_ge(unit_done, at(i, per, u - NR + 1))
                act.activation(w_hi[:, s, :], stage[:, s, :], ACT.Copy).then_inc(hi_ready, 1)

            def step(u0, i=None, per=0, last=False, hook=None):
                for k in range(NR, CU + (0 if last else NR)):
                    split(u0 + k, i, per)
                    if hook and k == NR + 5:
                        hook()

            def norm_prep(n):
                if n == 0:
                    act.wait_ge(x_in_s, 16)
                    act.wait_ge(const_in, 48)
                else:
                    act.wait_ge(evac, X_FINAL[n])
                for t in range(KT):
                    act.activation(xh[:, t, :], x[:, t, :], ACT.Copy,
                                   scale=gcol("norm", 16 * n + t)).then_inc(xh_ready, 1)

            def rms(n):
                def f():
                    act.wait_ge(ssum_done, n + 1)
                    act.activation(rstd[:], PS[:, SB(n), 0:T], ACT.Sqrt, scale=1.0 / D,
                                   bias=gcol("eps")).then_inc(rms_ready, 1)
                return f

            def turn(tasks):
                prev = None
                for t in tasks + [None]:
                    if t is not None and t["n"]:
                        ni, w = t["ni"], t["w"]
                        if ni >= 2:
                            act.wait_ge(msq_ready, ni - 1)
                        act.activation(sqb[:, ni % 2, 0:w], t["src"], ACT.Square).then_inc(sq_ready, 1)
                    if prev is not None:
                        p = prev
                        if p["n"]:
                            act.wait_ge(msq_ready, p["ni"] + 1)
                            if p["j"] >= 2:
                                act.wait_ge(turned, p["j"] - 1)
                            act.activation(sdb[:, p["ni"] % 2, 0:p["w"]], PS[:, p["ni"] % 2, 0:p["w"]],
                                           ACT.Sqrt, scale=1.0 / p["n"], bias=gcol("eps")).then_inc(sd_ready, 1)
                    prev = t

            def attend(g0, h0):
                for s in range(8 + 3):
                    if s < 8:
                        g = g0 + s
                        act.wait_ge(smax, g + 1)
                        for q in range(3):
                            seg = pr[:, g % 3, SEG[q]:SEG[q + 1]]
                            e = act.activation(seg, seg, ACT.Exp, bias=mx[:, g % 3, q:q + 1],
                                               accum_out=rsum[:, g % 3, q:q + 1])
                        e.then_inc(p_ready, 1)
                    if 2 <= s < 10:
                        g = g0 + s - 2
                        act.wait_ge(pt_psum, g + 1)
                        if g >= 2:
                            act.wait_ge(o_psum, g - 1)
                        act.activation(pta[:, g % 2], PS[:, 4, :].rearrange("p (a b) -> p a b", a=4),
                                       ACT.Copy).then_inc(pta_ready, 1)
                    if s >= 3:
                        g = g0 + s - 3
                        act.wait_ge(o_psum, g + 1)
                        act.activation(moh[:, h0 + s - 3, :], PS[:, 6 + g % 2, 0:T],
                                       ACT.Copy).then_inc(moh_ready, 1)

            def mlp(n, u_mlp, g_mlp, L, whole):
                def body(f):
                    for c in range(4):
                        step(u_mlp + CU * c, f, 64, hook=rms(n) if whole and c == 0 else None)
                        g = 16 * L + c
                        act.wait_ge(evac, at(f, 8, g_mlp + c + 1))
                        if not (whole and c == 0 and L == 0):
                            act.wait_ge(hl_ready, at(f, 4, g))
                        act.activation(mt2[:], mt1[:], ACT.Square).then_inc(hsq_done, 1)
                        act.wait_ge(hsq_done, at(f, 4, g + 1))
                        act.activation(hh[:, 4 * c:4 * c + 4, :], mt2[:], ACT.Copy).then_inc(hh_ready, 1)
                    for c in range(4):
                        step(u_mlp + 32 + CU * c, f, 64)
                return body

            def mlp_last(u_mlp, g_mlp, L):
                f = 3
                for c in range(4):
                    step(u_mlp + 64 * f + CU * c)
                    g = 16 * L + 4 * f + c
                    act.wait_ge(evac, g_mlp + 8 * f + c + 1)
                    act.wait_ge(hl_ready, g)
                    act.activation(mt2[:], mt1[:], ACT.Square).then_inc(hsq_done, 1)
                    act.wait_ge(hsq_done, g + 1)
                    act.activation(hh[:, 4 * c:4 * c + 4, :], mt2[:], ACT.Copy).then_inc(hh_ready, 1)
                for c in range(4):
                    step(u_mlp + 64 * f + 32 + CU * c, last=c == 3)

            act.dma_start(x[:], x_in).then_inc(x_in_s, 16)
            act.dma_start(gains[:], gains_in).then_inc(const_in, 16)
            act.dma_start(cst[:], cst_in).then_inc(const_in, 16)
            act.dma_start(tab[:], tabs_in[:, 0:4, :]).then_inc(const_in, 16)
            act.dma_start(adm[:], adm_in).then_inc(past_in, 16)
            act.dma_start(kA[:, :, 0:PAST], past_k).then_inc(past_in, 16)
            act.dma_start(kk[:, 0:PAST], past_kk).then_inc(past_in, 16)
            act.dma_start(vA[:, 0, :], past_v).then_inc(past_in, 16)
            act.dma_start(lat[:, :, 0:PAST], past_lat).then_inc(past_in, 16)

            for u in range(NR):
                split(u)
            norm_prep(0)
            lam = gains[:, GAIN["lam"]:GAIN["lam"] + 8]
            act.activation(spt[:, 0, :], lam, ACT.Abs).then_inc(sp_abs, 1)
            act.wait_ge(sp_abs, 1)
            act.activation(spt[:, 1, :], spt[:, 0, :], ACT.Exp, scale=-1.0).then_inc(sp_exp, 1)
            step(U_ABIN, hook=rms(0))
            with act.Fori(0, 3) as i:
                for c in range(2):
                    step(U_ABIN + CU * (1 + c), i, 2 * CU)
            act.wait_ge(evac, N_ABIN)
            act.activation(sqm[:, 0:4, :], zt[:, CQ:CQ + 4, :], ACT.Square).then_inc(latsq, 1)
            act.activation(sqm[:, 4:6, :], zt[:, CKV:CKV + 2, :], ACT.Square).then_inc(latsq, 1)
            for i, n in enumerate((512, 256)):
                act.wait_ge(latms, i + 1)
                act.activation(sdm[:, i, :], PS[:, i, 0:T], ACT.Sqrt, scale=1.0 / n,
                               bias=gcol("eps")).then_inc(latsd, 1)
            act.wait_ge(tok_psum, 1)
            act.activation(wiT[:].rearrange("p a b -> p (a b)"), PS[:, 2, 0:48], ACT.Copy)
            act.activation(vA[:, 2:4, :], PS[:, 3, :].rearrange("p (a b) -> p a b", a=2), ACT.Copy)
            act.activation(vA[0:80, 1, :], PS[0:80, 4, 0:256], ACT.Copy).then_inc(tok_copied, 1)
            act.wait_ge(lat_ready, 1)
            act.wait_ge(past_in, 80)
            act.activation(qlath[:], zt[:, CQ:CQ + 4, :], ACT.Copy)
            act.activation(lath[:], lat[:], ACT.Copy).then_inc(lath_ready, 1)
            act.wait_ge(latl_ready, 1)
            turn(TURN_A)
            for h in range(16):
                act.wait_ge(idx_psum, h + 1)
                if h >= 2:
                    act.wait_ge(idx_added, h - 1)
                elif h == 0:
                    act.wait_ge(turned, N_TURN_A)
                b = 2 * (h % 2)
                act.activation(rt[:, h % 2, 0:416], PS[:, b, 0:416], ACT.Relu, scale=1.0 / 32)
                act.activation(rt[:, h % 2, 416:752], PS[:, b + 1, 0:336], ACT.Relu,
                               scale=1.0 / 32).then_inc(relu_ready, 1)
            for c in range(3):
                split(U_UQ + 4 + 2 * c)
                split(U_UQ + 5 + 2 * c)
                act.wait_ge(unit_done, U_UQ + 2 * c + 2)
                act.activation(qb[:, 4 * c:4 * c + 4, :], PS[:, 4:8, 0:T], ACT.Copy).then_inc(qkv_evac, 1)
            attend(0, 0)
            for c in range(2):
                split(U_KN + 4 + c)
                act.wait_ge(unit_done, U_KN + c + 1)
                act.activation(kn[:, 4 * c:4 * c + 4, :], PS[:, 4 * c:4 * c + 4, 0:KEYS],
                               ACT.Copy).then_inc(qkv_evac, 1)
            for c in range(2):
                split(U_V + 4 + c)
                act.wait_ge(unit_done, U_V + c + 1)
                if c == 0:
                    act.wait_ge(out_s, 64)
                dst = vB[:, :, 512 * c:512 * c + 512]
                act.activation(dst[0:80, 1, :], PS[0:80, 4 * c + 1, :], ACT.Copy)
                act.activation(dst[:, 0, :], PS[:, 4 * c, :], ACT.Copy)
                act.activation(dst[:, 2:4, :], PS[:, 4 * c + 2:4 * c + 4, :], ACT.Copy).then_inc(qkv_evac, 1)
            act.wait_ge(qkv_evac, 7)
            turn(TURN_B)
            act.wait_ge(turned, len(TURN_A) + len(TURN_B))
            attend(8, 8)
            with act.Fori(0, 2) as i:
                for c in range(2):
                    step(U_ABOUT + CU * c, i, 2 * CU)
            norm_prep(1)
            mlp(1, U_MLP0, G_MLP0, 0, True)(0)
            with act.Fori(1, 4) as f:
                mlp(1, U_MLP0, G_MLP0, 0, False)(f)

            norm_prep(2)
            def gate_piece(c, j):
                g = c - 2
                if 0 <= g < 4:
                    if j == 4:
                        act.wait_ge(evac, G_CDIN + 1 + g // 2)
                        if g == 0:
                            act.wait_ge(cx_zero, 1)
                            act.wait_ge(cx_in, 16)
                        else:
                            act.wait_ge(xc_ready, 4 * g)
                        src = z2[:, CX + 2 * g:CX + 2 * g + 2, :]
                        act.activation(cxp[:, :, 0:3], cstate[:, 2 * g:2 * g + 2, :], ACT.Copy)
                        act.activation(cxp[:, :, 3:3 + NS_TOK], src[:, :, 0:NS_TOK], ACT.Copy)
                        act.activation(cxp[:, :, 6 + NS_TOK:], src[:, :, NS_TOK:], ACT.Copy).then_inc(cx_copied, 1)
                    if j == 8:
                        act.wait_ge(xc_ready, 4 * g + 4)
                        act.activation(xch[:], xc[:], ACT.Copy).then_inc(xch_ready, 1)
                    if j == 11:
                        act.wait_ge(unit_done, cd_chunk(c)[0] + GATE_AT + 1)
                        if g:
                            act.wait_ge(w_ready, g)
                            act.wait_ge(scan_done, 4 * g)
                        for n in range(4):
                            dst, bias = (rg, "ga_b") if n < 2 else (ig, "gx_b")
                            act.activation(dst[:, n % 2, :], PS[:, 4 * (1 - (G_CDIN + c) % 2) + n, 0:T],
                                           ACT.Sigmoid, bias=gcol(bias, 2 * g + n % 2)).then_inc(gate_ready, 1)
                g = c - 3
                if 0 <= g < 4:
                    if j == 5:
                        act.wait_ge(gate_ready, 4 * g + 4)
                        act.wait_ge(sp_ready, 2)
                        for n in range(2):
                            act.activation(av[:, n, :], rg[:, n, :], ACT.Exp,
                                           scale=sp8[:, 1, 2 * g + n:2 * g + n + 1]).then_inc(exp_ready, 1)
                        for n in range(2):
                            act.activation(tv[:, n, :], rg[:, n, :], ACT.Tanh,
                                           scale=sp8[:, 0, 2 * g + n:2 * g + n + 1]).then_inc(tanh_ready, 1)
                    if j == 6:
                        act.wait_ge(exp_ready, 2 * g + 2)
                        act.wait_ge(tanh_ready, 2 * g + 2)
                        act.activation(rg[:], av[:], ACT.Square).then_inc(asq_ready, 1)
                    if j == 9:
                        act.wait_ge(w_ready, g + 1)
                        act.activation(tv[:], tv[:], ACT.Sqrt).then_inc(sqrt_ready, 1)
                if c == 6 and j == 10:
                    act.wait_ge(gelu_in, 1)
                    act.activation(t1[:, 0:4], t1[:, 0:4], ACT.Sigmoid, scale=2 * 0.7978845608028654)
                if c == 6 and j == 11:
                    act.activation(t1[:, 4:8], t1[:, 4:8], ACT.Sigmoid,
                                   scale=2 * 0.7978845608028654).then_inc(gelu_sig, 1)

            for c in range(N_CDIN):
                u0, n = cd_chunk(c)
                for j in range(NR, n + NR):
                    split(u0 + j)
                    if c == 0 and j == NR + 5:
                        rms(2)()
                    gate_piece(c, j)
            act.wait_ge(evac, G_CDIN + 12)
            act.wait_ge(outc_ready, 1)
            act.activation(moh[:, 0:8, :], z2[:, CG:CG + 8, :], ACT.Copy).then_inc(doh_ready, 1)
            act.activation(sgd[:], z2[:, DG:DG + 8, :], ACT.Sigmoid).then_inc(silu_sig, 1)
            for h in range(4):
                act.wait_ge(kv_psum, h + 1)
                if h >= 2:
                    act.wait_ge(st_psum, 2 * (h - 1))
                kd = [gains[r, GAIN["kdec"] + 3 * h + t:GAIN["kdec"] + 3 * h + t + 1]
                      for t, r in ((0, slice(0, 80)), (1, slice(0, P)), (2, slice(0, P)))]
                act.activation(ktok[0:80, h % 2, 0, :], PS[0:80, 1, 0:256], ACT.Copy, scale=kd[0])
                act.activation(ktok[:, h % 2, 1, :], PS[:, 0, 0:256], ACT.Copy, scale=kd[1])
                act.activation(ktok[:, h % 2, 2, :], PS[:, 0, 256:512], ACT.Copy, scale=kd[2])
                act.activation(vtok[0:80, h % 2, 0, :], PS[0:80, 1, 256:512], ACT.Copy)
                act.activation(vtok[:, h % 2, 1:3, :], PS[:, 2, :].rearrange("p (a b) -> p a b", a=2),
                               ACT.Copy).then_inc(ktok_ready, 1)
                act.wait_ge(do_psum, h + 1)
                if h >= 1:
                    act.wait_ge(od_ready, h)
                act.activation(osq[:], PS[:, 5:7, 0:T], ACT.Square).then_inc(osq_ready, 1)
                act.wait_ge(oms_psum, h + 1)
                act.activation(osd[:], PS[:, 4, 0:T], ACT.Sqrt, scale=1.0 / 256,
                               bias=gcol("eps")).then_inc(osd_ready, 1)
                act.wait_ge(st_psum, 2 * h + 2)
                if h >= 2:
                    act.wait_ge(st_out[h % 2], 32)
                act.activation(so[:, 2 + h % 2], PS[:, 0, :].rearrange("p (a b) -> p a b", a=2),
                               ACT.Copy).then_inc(st_prompt, 1)
                act.wait_ge(od_ready, h + 1)
                act.activation(moh[:, 8 + 2 * h:10 + 2 * h, :], z2[:, DG + 2 * h:DG + 2 * h + 2, :],
                               ACT.Copy).then_inc(doh_ready, 1)
            with act.Fori(0, 2) as i:
                for c in range(2):
                    step(U_CDOUT + CU * c, i, 2 * CU)
            norm_prep(3)
            mlp(3, U_MLP1, G_MLP1, 1, True)(0)
            with act.Fori(1, 3) as f:
                mlp(3, U_MLP1, G_MLP1, 1, False)(f)
            mlp_last(U_MLP1, G_MLP1, 1)

        @block.vector
        def _(dve):
            ch = Chain(dve, dchain)

            def split(u, i=None, per=0):
                s = u % NR
                dve.wait_ge(hi_ready, at(i, per, u + 1))
                dve.tensor_tensor(w_lo[:, s, :], stage[:, s, :], w_hi[:, s, :].bitcast(F32),
                                  ALU.subtract).then_inc(lo_ready, 1)

            def step(u0, i=None, per=0, last=False):
                for k in range(NR, CU + (0 if last else NR)):
                    split(u0 + k, i, per)

            def norm_prep(n):
                if n:
                    dve.wait_ge(evac, X_FINAL[n])
                for t in range(KT):
                    dve.wait_ge(xh_ready, 16 * n + t + 1)
                    dve.scalar_tensor_tensor(xl[:, t, :], x[:, t, :], gcol("norm", 16 * n + t),
                                             xh[:, t, :].bitcast(F32), ALU.mult,
                                             ALU.subtract).then_inc(xl_ready, 1)

            def rms(n):
                dve.wait_ge(rms_ready, n + 1)
                ch.link(dve.reciprocal(rstd[:], rstd[:]))

            rstd4 = rstd[:].unsqueeze(1).to_broadcast([P, 4, T])

            def banks(g):
                b = 4 * (g % 2)
                return PS[:, b:b + 4, 0:T]

            def take_scaled(u0, g, dst, i=None, su=0, sg=0):
                dve.wait_ge(unit_done, at(i, su, u0 + CU))
                dve.tensor_tensor(dst, banks(g), rstd4, ALU.mult).then_inc(evac, 1)

            def take_added(u0, g, dst, i=None, su=0, sg=0):
                dve.wait_ge(unit_done, at(i, su, u0 + CU))
                dve.tensor_tensor(dst, banks(g), dst, ALU.add).then_inc(evac, 1)

            x4 = x[:].rearrange("p (c m) t -> p c m t", m=4)
            zt4 = zt[:].rearrange("p (c m) t -> p c m t", m=4)
            z24 = z2[:].rearrange("p (c m) t -> p c m t", m=4)

            def turn(tasks):
                prev = None
                for t in tasks + [None]:
                    if t is not None and t["tab"] is not None:
                        ri, k = t["ri"], t["tab"]
                        if ri >= 2:
                            dve.wait_ge(rot_ready, ri - 1)
                        if t["g"] is None:
                            dve.tensor_tensor(ra[:, ri % 2, :], t["src"], tab[:, k, :], ALU.mult)
                            dve.tensor_tensor(rb[:, ri % 2, :], t["src"], tab[:, k + 1, :],
                                              ALU.mult).then_inc(ab_ready, 1)
                        else:
                            dve.scalar_tensor_tensor(ra[:, ri % 2, :], t["src"], t["g"], tab[:, k, :],
                                                     ALU.mult, ALU.mult)
                            dve.scalar_tensor_tensor(rb[:, ri % 2, :], t["src"], t["g"], tab[:, k + 1, :],
                                                     ALU.mult, ALU.mult).then_inc(ab_ready, 1)
                    if prev is not None:
                        p = prev
                        if p["n"]:
                            sd = sdb[:, p["ni"] % 2, 0:p["w"]]
                            dve.wait_ge(sd_ready, p["ni"] + 1)
                            ch.link(dve.reciprocal(sd, sd))
                            if p.get("kk"):
                                ch.link(dve.tensor_scalar(sd, sd, gcol("mkr"), gcol("mki"), ALU.mult, ALU.add))
                            if p["tab"] is None:
                                dve.scalar_tensor_tensor(p["dst"], p["src"], p["g"], sd, ALU.mult,
                                                         ALU.mult).then_inc(turned, 1)
                            else:
                                dve.wait_ge(rot_ready, p["ri"] + 1)
                                dve.tensor_tensor(p["dst"], PS[:, 2 + p["ri"] % 2, 0:T], sd,
                                                  ALU.mult).then_inc(turned, 1)
                        else:
                            dve.wait_ge(rot_ready, p["ri"] + 1)
                            dve.tensor_copy(p["dst"], PS[:, 2 + p["ri"] % 2, 0:T]).then_inc(turned, 1)
                        if p.get("kk"):
                            kpad_fill()
                    prev = t

            def kpad_fill():
                dve.wait_ge(turned, KK_J + 1)
                dve.wait_ge(pad_zero, 1)
                dve.wait_ge(past_in, 80)
                for slot, (src, dst) in enumerate(((0, 0), (0, 32), (32, 0), (32, 32))):
                    for half in (0, 64):
                        e = dve.tensor_copy(kpad[dst + half:dst + half + 32, slot, :],
                                            kk[src + half:src + half + 32, :])
                e.then_inc(kpad_ready, 1)

            def attend(g0, h0, bias, scale):
                for s in range(8 + 3):
                    if s < 8:
                        g = g0 + s
                        dve.wait_ge(sc_psum, g + 1)
                        if g >= 3:
                            dve.wait_ge(pt_psum, g - 2)
                        for q in range(3):
                            src = PS[:, 2 * (g % 2) + q // 2, SEG[q] - 416 * (q // 2):SEG[q + 1] - 416 * (q // 2)]
                            e = dve.tensor_tensor_reduce(pr[:, g % 3, SEG[q]:SEG[q + 1]], src,
                                                         bias[:, SEG[q]:SEG[q + 1]], scale, TAKEN,
                                                         ALU.add, ALU.max, mx[:, g % 3, q:q + 1])
                        ch.link(e)
                        dve.tensor_scalar(mx[:, g % 3, :], mx[:, g % 3, :], -1.0, None,
                                          ALU.mult).then_inc(smax, 1)
                    if 1 <= s < 9:
                        g = g0 + s - 1
                        dve.wait_ge(p_ready, g + 1)
                        ch.link(dve.reciprocal(rsum[:, g % 3, :], rsum[:, g % 3, :]))
                        for q in range(3):
                            seg = pr[:, g % 3, SEG[q]:SEG[q + 1]]
                            e = dve.tensor_scalar(seg, seg, rsum[:, g % 3, q:q + 1], None, ALU.mult)
                        e.then_inc(pn_ready, 1)
                    if 2 <= s < 10:
                        g = g0 + s - 2
                        dve.wait_ge(pt_psum, g + 1)
                        if g >= 2:
                            dve.wait_ge(o_psum, g - 1)
                        dve.tensor_copy(ptb[0:80, g % 2], PS[0:80, 5, 0:384].rearrange(
                            "p (a b) -> p a b", a=3)).then_inc(ptb_ready, 1)
                    if s >= 3:
                        g = g0 + s - 3
                        dve.wait_ge(moh_ready, g + 1)
                        dve.tensor_tensor(mol[:, h0 + s - 3, :], PS[:, 6 + g % 2, 0:T],
                                          moh[:, h0 + s - 3, :].bitcast(F32),
                                          ALU.subtract).then_inc(mol_ready, 1)

            def take_up(u0, g, c, f, whole, L):
                dve.wait_ge(unit_done, at(f, 64, u0 + CU))
                if not (whole and c == 0 and L == 0):
                    dve.wait_ge(hh_ready, at(f, 4, 16 * L + c))
                dve.scalar_tensor_tensor(mt1[:], banks(g), 0.0, rstd4, ALU.max, ALU.mult).then_inc(evac, 1)

            def low_h(c, f, L):
                dve.wait_ge(hh_ready, at(f, 4, 16 * L + c + 1))
                dve.tensor_tensor(hl[:, 4 * c:4 * c + 4, :], mt2[:], hh[:, 4 * c:4 * c + 4, :].bitcast(F32),
                                  ALU.subtract).then_inc(hl_ready, 1)

            def mlp(n, u_mlp, g_mlp, L, whole, last=False):
                def body(f):
                    for c in range(4):
                        step(u_mlp + CU * c, f, 64)
                        if whole and c == 0:
                            rms(n)
                        take_up(u_mlp + CU * c, g_mlp + c, c, f, whole, L)
                        low_h(c, f, L)
                    for c in range(4):
                        step(u_mlp + 32 + CU * c, f, 64, last=last and c == 3)
                        take_added(u_mlp + 32 + CU * c, g_mlp + c, x4[:, c], f, 64)
                return body

            for u in range(NR):
                split(u)
            norm_prep(0)
            u_, z_, z2_ = spt[:, 1, :], spt[:, 2, :], spt[:, 3, :]
            dve.wait_ge(sp_exp, 1)
            ch.link(dve.tensor_scalar(z_, u_, 2.0, None, ALU.add))
            ch.link(dve.reciprocal(z_, z_))
            ch.link(dve.tensor_tensor(z_, z_, u_, ALU.mult))
            ch.link(dve.tensor_tensor(z2_, z_, z_, ALU.mult))
            ch.link(dve.tensor_scalar(u_, z2_, 1.0 / 17, 1.0 / 15, ALU.mult, ALU.add))
            for k in (13, 11, 9, 7, 5, 3, 1):
                ch.link(dve.tensor_tensor(u_, u_, z2_, ALU.mult))
                ch.link(dve.tensor_scalar(u_, u_, 1.0 / k, None, ALU.add))
            ch.link(dve.tensor_tensor(u_, u_, z_, ALU.mult))
            lam = gains[:, GAIN["lam"]:GAIN["lam"] + 8]
            ch.link(dve.tensor_scalar(z_, lam, -1.0, 0.0, ALU.mult, ALU.max))
            ch.link(dve.scalar_tensor_tensor(u_, u_, 2.0, z_, ALU.mult, ALU.add))
            dve.tensor_scalar(sp8[:, 0, :], u_, 8.0, None, ALU.mult).then_inc(sp_ready, 1)
            dve.tensor_scalar(sp8[:, 1, :], u_, -8.0, None, ALU.mult).then_inc(sp_ready, 1)

            step(U_ABIN)
            rms(0)
            take_scaled(U_ABIN, 0, zt4[:, 0])
            with dve.Fori(0, 3) as i:
                for c in range(2):
                    step(U_ABIN + CU * (1 + c), i, 2 * CU)
                    take_scaled(U_ABIN + CU * (1 + c), 1 + c, zt4[:, i * 2 + (1 + c)], i, 2 * CU)
            dve.wait_ge(latsd, 2)
            ch.link(dve.reciprocal(sdm[:], sdm[:]))
            dve.wait_ge(evac, N_ABIN)
            dve.wait_ge(latsq, 2)
            for t in range(4):
                dve.scalar_tensor_tensor(zt[:, CQ + t, :], zt[:, CQ + t, :], gcol("qlat", t), sdm[:, 0, :],
                                         ALU.mult, ALU.mult)
            for t in range(2):
                e = dve.scalar_tensor_tensor(lat[:, t, PAST:], zt[:, CKV + t, :], gcol("kvlat", t),
                                             sdm[:, 1, :], ALU.mult, ALU.mult)
            e.then_inc(lat_ready, 1)
            dve.wait_ge(lath_ready, 1)
            dve.tensor_tensor(qlatl[:], zt[:, CQ:CQ + 4, :], qlath[:].bitcast(F32), ALU.subtract)
            dve.tensor_tensor(latl[:], lat[:], lath[:].bitcast(F32), ALU.subtract).then_inc(latl_ready, 1)
            dve.wait_ge(latl_ready, 1)
            turn(TURN_A)
            dve.wait_ge(turned, N_TURN_A)
            dve.wait_ge(tok_copied, 1)
            for h in range(16):
                dve.wait_ge(relu_ready, h + 1)
                if h:
                    dve.wait_ge(idx_added, h)
                for q in range(3):
                    sl = slice(SEG[q], SEG[q + 1])
                    e = dve.scalar_tensor_tensor(acc[:, sl], rt[:, h % 2, sl], wiT[:, q, h:h + 1],
                                                 (adm if h == 0 else acc)[:, sl], ALU.mult, ALU.add)
                e.then_inc(idx_added, 1)
            dve.wait_ge(idx_added, 16)
            for r in range(TOPK_P // 8):
                rows = [q for q in range(3) if r < (TOPK_S if q == 0 else TOPK_P) // 8]
                for q in rows:
                    e = dve.max(m8[:, q, :], acc[:, SEG[q]:SEG[q + 1]])
                ch.link(e)
                for q in rows:
                    sl = slice(SEG[q], SEG[q + 1])
                    e = dve.match_replace(acc[:, sl], m8[:, q, :], acc[:, sl], TAKEN)
                ch.link(e)
                if r < 6:
                    split(U_UQ + 4 + r)
            ch.link(dve.tensor_scalar(biasA[:], acc[:], TAKEN / 2, NEG, ALU.is_gt, ALU.mult))
            ch.link(dve.tensor_tensor(biasA[:], biasA[:], adm[:], ALU.add))
            attend(0, 0, biasA, 128 ** -0.5)
            for u in range(4):
                split(U_KN + 4 + u)
            dve.wait_ge(qkv_evac, 7)
            turn(TURN_B)
            dve.wait_ge(turned, len(TURN_A) + len(TURN_B))
            attend(8, 8, adm, 192 ** -0.5)
            with dve.Fori(0, 2) as i:
                for c in range(2):
                    step(U_ABOUT + CU * c, i, 2 * CU)
                    take_added(U_ABOUT + CU * c, G_ABOUT + c, x4[:, i * 2 + c], i, 2 * CU)
            norm_prep(1)
            mlp(1, U_MLP0, G_MLP0, 0, True)(0)
            with dve.Fori(1, 4) as f:
                mlp(1, U_MLP0, G_MLP0, 0, False)(f)

            norm_prep(2)
            parts = ((0, NS_TOK, 0), (NS_TOK, T, 3))

            def gate_piece(c, j):
                g = c - 2
                if 0 <= g < 4:
                    if 5 <= j <= 8:
                        k = j - 5
                        if k == 0:
                            dve.wait_ge(cx_copied, g + 1)
                            if g:
                                dve.wait_ge(igx_ready, g)
                        else:
                            ch.need(ch.n)
                        for n in range(2):
                            for a, b, off in parts:
                                dst, src = xc[:, n, a:b], cxp[:, n, a + off + k:b + off + k]
                                w = gcol("conv_w", 8 * k + 2 * g + n)
                                if k == 0:
                                    e = dve.tensor_scalar(dst, src, w, gcol("conv_b", 2 * g + n), ALU.mult, ALU.add)
                                else:
                                    e = dve.scalar_tensor_tensor(dst, src, w, dst, ALU.mult, ALU.add)
                                if k == 3:
                                    e.then_inc(xc_ready, 1)
                                else:
                                    ch.mark(e)
                    if j == 9:
                        dve.wait_ge(xch_ready, g + 1)
                        dve.tensor_tensor(xcl[:], xc[:], xch[:].bitcast(F32), ALU.subtract).then_inc(xcl_ready, 1)
                g = c - 3
                if 0 <= g < 4:
                    if j == 8:
                        dve.wait_ge(asq_ready, g + 1)
                        dve.scalar_tensor_tensor(tv[:], rg[:], 1.0, tv[:], ALU.add, ALU.mult).then_inc(w_ready, 1)
                    if j == 10:
                        dve.wait_ge(sqrt_ready, g + 1)
                        dve.wait_ge(igx_ready, g + 1)
                        dve.wait_ge(clast_ready, 1)
                        ch.link(dve.tensor_tensor(tv[:], tv[:], ig[:], ALU.mult))
                        for n in range(2):
                            for a, b, h0 in ((0, NS_TOK, gcol("h0", 2 * g + n)), (NS_TOK, T, 0.0)):
                                dve.tensor_tensor_scan(z2[:, CX + 2 * g + n, a:b], av[:, n, a:b], tv[:, n, a:b],
                                                       h0, ALU.mult, ALU.add).then_inc(scan_done, 1)
                if 7 <= c <= 10:
                    k = c - 7
                    x1, x2 = halves(k)
                    if j == 5:
                        if k == 0:
                            dve.wait_ge(scan_done, 16)
                            dve.wait_ge(tab2_in, 32)
                        dve.wait_ge(evac, G_CDIN + (6, 6, 8, 8)[k])
                        dve.tensor_tensor(rr[:, 0], x1, cosb, ALU.mult)
                    if j == 6:
                        dve.tensor_tensor(rr[:, 1], x2, sinb, ALU.mult).then_inc(rope2_d, 1)
                    if j == 9:
                        dve.wait_ge(rope2_d, 2 * k + 1)
                        dve.wait_ge(rope2_p, 2 * k + 1)
                        dve.tensor_tensor(x1, rr[:, 0], rr[:, 1], ALU.subtract).then_inc(rope2_d, 1)
                    if j == 10:
                        dve.wait_ge(rope2_d, 2 * k + 2)

            for c in range(N_CDIN):
                u0, n = cd_chunk(c)
                for j in range(NR, n + NR):
                    split(u0 + j)
                    gate_piece(c, j)
                if c == 0:
                    rms(2)
                if c == 10:
                    dve.wait_ge(outc_ready, 1)
                dve.wait_ge(unit_done, u0 + n)
                dve.tensor_tensor(z24[:, c], banks(G_CDIN + c), rstd4, ALU.mult).then_inc(evac, 1)
            dve.wait_ge(doh_ready, 1)
            dve.wait_ge(outc_ready, 1)
            dve.tensor_tensor(mol[:, 0:8, :], z2[:, CG:CG + 8, :], moh[:, 0:8, :].bitcast(F32),
                              ALU.subtract).then_inc(dol_ready, 1)
            dve.wait_ge(s0_in_s, 16)
            for h in range(4):
                q8 = z2[:, DQ + 2 * h:DQ + 2 * h + 2, 0:NS_TOK]
                if h >= 2:
                    dve.wait_ge(do_psum, h - 1)
                dve.tensor_tensor(qd[:, h % 2], q8, decq[:, h, :].unsqueeze(1).to_broadcast([P, 2, NS_TOK]),
                                  ALU.mult).then_inc(qd_ready, 1)
                dve.wait_ge(ds_psum, h + 1)
                dve.wait_ge(mask_in[h % 2], 16 * (h // 2 + 1))
                if h == 0:
                    dve.wait_ge(rope2_p, 8)
                dve.tensor_tensor(pT[0:80, h % 2, 0:336], PS[0:80, 3, 0:336], dmask[0:80, h % 2, 0:336],
                                  ALU.mult)
                dve.tensor_tensor(pT[:, h % 2, 336:720], PS[:, 4, 0:384], dmask[:, h % 2, 336:720],
                                  ALU.mult).then_inc(pT_ready, 1)
                dve.wait_ge(osd_ready, h + 1)
                ch.link(dve.reciprocal(osd[:], osd[:]))
                for e_ in range(2):
                    e = dve.scalar_tensor_tensor(osq[:, e_, :], PS[:, 5 + e_, 0:T], gcol("dn", e_), osd[:],
                                                 ALU.mult, ALU.mult)
                ch.link(e)
                dve.wait_ge(silu_ready, 1)
                dg = z2[:, DG + 2 * h:DG + 2 * h + 2, :]
                dve.tensor_tensor(dg, dg, osq[:], ALU.mult).then_inc(od_ready, 1)
                dve.wait_ge(st_psum, 2 * h + 1)
                if h >= 2:
                    dve.wait_ge(st_out[h % 2], 32)
                dve.scalar_tensor_tensor(so[:, h % 2], s0[:, :, h, :], float(np.float32(GAMMA[h] ** NS_TOK)),
                                         PS[:, 7, :].rearrange("p (a b) -> p a b", a=2),
                                         ALU.mult, ALU.add).then_inc(st_sample, 1)
                dve.wait_ge(doh_ready, h + 2)
                dve.wait_ge(od_ready, h + 1)
                dve.tensor_tensor(mol[:, 8 + 2 * h:10 + 2 * h, :], dg,
                                  moh[:, 8 + 2 * h:10 + 2 * h, :].bitcast(F32),
                                  ALU.subtract).then_inc(dol_ready, 1)
            with dve.Fori(0, 2) as i:
                for c in range(2):
                    step(U_CDOUT + CU * c, i, 2 * CU)
                    take_added(U_CDOUT + CU * c, G_CDOUT + c, x4[:, i * 2 + c], i, 2 * CU)
            norm_prep(3)
            mlp(3, U_MLP1, G_MLP1, 1, True)(0)
            with dve.Fori(1, 3) as f:
                mlp(3, U_MLP1, G_MLP1, 1, False)(f)
            mlp(3, U_MLP1, G_MLP1, 1, False, last=True)(3)

        @block.tensor
        def _(pe):
            def product(u, j, kt, rh, rl, first, last, bank0, m=4, i=None, su=0, width=T):
                s = u % NR
                for o in range(m):
                    c = 512 * j + P * o
                    wh, wl = w_hi[:, s, c:c + P], w_lo[:, s, c:c + P]
                    out = PS[:, bank0 + o, 0:width]
                    pe.matmul(out, wh, rh, start=first, stop=False)
                    pe.matmul(out, wh, rl, start=False, stop=False)
                    mm = pe.matmul(out, wl, rh, start=False, stop=last)
                return mm

            def chunk(u0, g, xh, xl, i=None, su=0, sg=0, need=None, hook=None):
                if g >= 2 or i is not None:
                    pe.wait_ge(evac, at(i, sg, g - 1))
                for k in range(CU):
                    if need:
                        need(k)
                    pe.wait_ge(lo_ready, at(i, su, u0 + k + 1))
                    for j in range(2):
                        kt = 2 * k + j
                        mm = product(u0 + k, j, kt, xh[:, kt, :], xl[:, kt, :], kt == 0, kt == KT - 1,
                                     4 * (g % 2))
                    mm.then_inc(unit_done, 1)
                    if hook and k == 5:
                        hook()

            def need_x(n):
                return lambda k: pe.wait_ge(xl_ready, 16 * n + 2 * k + 2)

            def sum_squares(n):
                def f():
                    pe.wait_ge(ssq_ready, n + 1)
                    if n:
                        pe.wait_ge(evac, NORM_G[n])
                    for j in range(4):
                        mm = pe.matmul(PS[:, SB(n), 0:T], ones, ssq[:, j, :], start=j == 0, stop=j == 3)
                    mm.then_inc(ssum_done, 1)
                return f

            def turn(tasks):
                for t in tasks:
                    w = t["w"]
                    if t["n"]:
                        ni = t["ni"]
                        pe.wait_ge(sq_ready, ni + 1)
                        if ni >= 2:
                            pe.wait_ge(sd_ready, ni - 1)
                        pe.matmul(PS[:, ni % 2, 0:w], t["m"], sqb[:, ni % 2, 0:w], start=True,
                                  stop=True).then_inc(msq_ready, 1)
                    if t["tab"] is not None:
                        ri = t["ri"]
                        pe.wait_ge(ab_ready, ri + 1)
                        if t["j"] >= 2 and ri >= 2:
                            pe.wait_ge(turned, t["j"] - 1)
                        out = PS[:, 2 + ri % 2, 0:T]
                        pe.matmul(out, ident, ra[:, ri % 2, :], start=True, stop=False)
                        pe.matmul(out, swap, rb[:, ri % 2, :], start=False, stop=True).then_inc(rot_ready, 1)

            def attend(g0, scores, values):
                for s in range(8 + 3):
                    if s < 8:
                        g = g0 + s
                        if s >= 2:
                            pe.wait_ge(smax, g - 1)
                        for q, (t0, k0, k1) in enumerate(QT):
                            o = SEG[q] - 416 * (q // 2)
                            mm = scores(s, PS[:, 2 * (g % 2) + q // 2, o:o + k1 - k0], t0, k0, k1)
                        mm.then_inc(sc_psum, 1)
                    if 2 <= s < 10:
                        g = g0 + s - 2
                        pe.wait_ge(pn_ready, g + 1)
                        if s >= 3:
                            pe.wait_ge(pta_ready, g)
                            pe.wait_ge(ptb_ready, g)
                        for a, (q, k) in enumerate(((0, 0), (1, 2), (2, 2), (2, 3))):
                            o = SEG[q] + KTILE[k][0] - QT[q][1]
                            pe.transpose(PS[:, 4, P * a:P * a + P], pr[:, g % 3, o:o + P], ident)
                        for q in range(3):
                            o = SEG[q] + KTILE[1][0] - QT[q][1]
                            mm = pe.transpose(PS[0:80, 5, P * q:P * q + P], pr[:, g % 3, o:o + 80], ident)
                        mm.then_inc(pt_psum, 1)
                    if s >= 3:
                        g = g0 + s - 3
                        h = s - 3
                        pe.wait_ge(pta_ready, g + 1)
                        pe.wait_ge(ptb_ready, g + 1)
                        if s >= 5:
                            pe.wait_ge(mol_ready, g - 1)
                        for q, (t0, t1_) in enumerate(QN):
                            out = PS[:, 6 + g % 2, t0:t1_]
                            n = t1_ - t0
                            full = {0: [(0, 0)], 1: [(1, 2)], 2: [(2, 2), (3, 3)]}[q]
                            pe.matmul(out, values(h, 1)[0:80], ptb[0:80, g % 2, q, 0:n], start=True,
                                      stop=False)
                            for a, (slot, k) in enumerate(full):
                                mm = pe.matmul(out, values(h, k), pta[:, g % 2, slot, 0:n], start=False,
                                               stop=a == len(full) - 1)
                        mm.then_inc(o_psum, 1)

            pe.wait_ge(const_in, 48)
            chunk(U_ABIN, 0, xh, xl, need=need_x(0), hook=sum_squares(0))
            pe.wait_ge(rms_ready, 1)
            chunk(U_ABIN + CU, 1, xh, xl)
            chunk(U_ABIN + 2 * CU, 2, xh, xl)
            with pe.Fori(1, 3) as i:
                for c in range(2):
                    chunk(U_ABIN + CU * (1 + c), 1 + c, xh, xl, i, 2 * CU, 2)
            pe.wait_ge(evac, N_ABIN)
            pe.wait_ge(latsq, 1)
            for j in range(4):
                mm = pe.matmul(PS[:, 0, 0:T], ones, sqm[:, j, :], start=j == 0, stop=j == 3)
            mm.then_inc(latms, 1)
            pe.wait_ge(latsq, 2)
            for j in range(2):
                mm = pe.matmul(PS[:, 1, 0:T], ones, sqm[:, 4 + j, :], start=j == 0, stop=j == 1)
            mm.then_inc(latms, 1)
            for q, (t0, _, _) in enumerate(QT):
                pe.transpose(PS[:, 2, 16 * q:16 * q + 16], zt[0:16, WI, t0:t0 + P], ident[0:16, 0:16])
            for c in range(2):
                pe.transpose(PS[0:80, 4, P * c:P * c + P], zt[:, VA + c, 0:80], ident)
                for k in range(2):
                    a, b = TT[1 + k]
                    mm = pe.transpose(PS[:, 3, 256 * k + P * c:256 * k + P * c + P], zt[:, VA + c, a:b], ident)
            mm.then_inc(tok_psum, 1)
            pe.wait_ge(latsd, 2)
            pe.wait_ge(tok_copied, 1)
            turn(TURN_A)
            pe.wait_ge(kpad_ready, 1)
            pe.wait_ge(turned, N_TURN_A)
            for h in range(16):
                if h >= 2:
                    pe.wait_ge(relu_ready, h - 1)
                b = 2 * (h % 2)
                for q, (t0, k0, k1) in enumerate(QT):
                    o = SEG[q] - 416 * (q // 2)
                    mm = pe.matmul(PS[:, b + q // 2, o:o + k1 - k0], zt[:, QI + h // 2, t0:t0 + P],
                                   kpad[:, h % 2, k0:k1], start=True, stop=True)
                mm.then_inc(idx_psum, 1)
            pe.wait_ge(latl_ready, 1)
            for c in range(3):
                if c:
                    pe.wait_ge(qkv_evac, c)
                for k in range(2):
                    u = U_UQ + 2 * c + k
                    pe.wait_ge(lo_ready, u + 1)
                    for j in range(2):
                        kt = 2 * k + j
                        mm = product(u, j, kt, qlath[:, kt, :], qlatl[:, kt, :], kt == 0, kt == 3, 4)
                    mm.then_inc(unit_done, 1)
            pe.wait_ge(relu_ready, 16)
            pe.wait_ge(qkv_evac, 3)

            def scores_a(h, out, t0, k0, k1):
                return pe.matmul(out, zt[:, QA + h, t0:t0 + P], kA[:, h // 4, k0:k1], start=True, stop=True)

            attend(0, scores_a, lambda h, k: vA[:, k, P * (h // 4):P * (h // 4) + P])
            pe.wait_ge(mol_ready, 8)
            for c in range(2):
                u = U_KN + c
                pe.wait_ge(lo_ready, u + 1)
                for j in range(2):
                    mm = product(u, j, j, lath[:, j, :], latl[:, j, :], j == 0, j == 1, 4 * c, width=KEYS)
                mm.then_inc(unit_done, 1)
            for c in range(2):
                u = U_V + c
                s = u % NR
                pe.wait_ge(lo_ready, u + 1)
                pe.wait_ge(qkv_evac, 4 + c)
                for k, (a, b) in enumerate(KTILE):
                    out = PS[0:b - a, 4 * c + k, :]
                    for j in range(2):
                        wh, wl = w_hi[:, s, 512 * j:512 * j + 512], w_lo[:, s, 512 * j:512 * j + 512]
                        pe.matmul(out, lath[:, j, a:b], wh, start=j == 0, stop=False)
                        pe.matmul(out, latl[:, j, a:b], wh, start=False, stop=False)
                        mm = pe.matmul(out, lath[:, j, a:b], wl, start=False, stop=j == 1)
                mm.then_inc(unit_done, 1)
            pe.wait_ge(qkv_evac, 7)
            turn(TURN_B)
            pe.wait_ge(turned, len(TURN_A) + len(TURN_B))

            def scores_b(h, out, t0, k0, k1):
                pe.matmul(out, qb[:, h, t0:t0 + P], kn[:, h, k0:k1], start=True, stop=False)
                return pe.matmul(out, qb[:, 8 + h // 2, t0:t0 + P], kpad[:, 2 + h % 2, k0:k1], start=False,
                                 stop=True)

            attend(8, scores_b, lambda h, k: vB[:, k, P * h:P * h + P])
            pe.wait_ge(mol_ready, 16)
            with pe.Fori(0, 2) as i:
                for c in range(2):
                    chunk(U_ABOUT + CU * c, G_ABOUT + c, moh, mol, i, 2 * CU, 2)

            def mlp(n, u_mlp, g_mlp, L, whole):
                def body(f):
                    for c in range(4):
                        if whole and c == 1:
                            pe.wait_ge(rms_ready, n + 1)
                        chunk(u_mlp + CU * c, g_mlp + c, xh, xl, f, 64, 8,
                              need=need_x(n) if whole and c == 0 else None,
                              hook=sum_squares(n) if whole and c == 0 else None)
                    for c in range(4):
                        chunk(u_mlp + 32 + CU * c, g_mlp + 4 + c, hh, hl, f, 64, 8,
                              need=(lambda k: pe.wait_ge(hl_ready, at(f, 4, 16 * L + k // 2 + 1)))
                              if c == 0 else None)
                return body

            mlp(1, U_MLP0, G_MLP0, 0, True)(0)
            with pe.Fori(1, 4) as f:
                mlp(1, U_MLP0, G_MLP0, 0, False)(f)
            for c in range(N_CDIN):
                g = G_CDIN + c
                u0, nu = cd_chunk(c)
                pe.wait_ge(evac, g - 1)
                if c == 1:
                    pe.wait_ge(rms_ready, 3)
                if c - 1 in GATE_CHUNKS:
                    pe.wait_ge(gate_ready, 4 * (c - 2))
                for j in range(nu):
                    u = u0 + j
                    s = u % NR
                    if nu > CU and j == GATE_AT:
                        b = c - 2
                        pe.wait_ge(evac, g)
                        pe.wait_ge(xcl_ready, b + 1)
                        pe.wait_ge(lo_ready, u + 1)
                        for n in range(4):
                            wh, wl = w_hi[:, s, P * n:P * n + P], w_lo[:, s, P * n:P * n + P]
                            out = PS[:, 4 * (1 - g % 2) + n, 0:T]
                            pe.matmul(out, wh, xch[:, n % 2, :], start=True, stop=False)
                            pe.matmul(out, wh, xcl[:, n % 2, :], start=False, stop=False)
                            mm = pe.matmul(out, wl, xch[:, n % 2, :], start=False, stop=True)
                    else:
                        k = j - (nu > CU and j > GATE_AT)
                        if c == 0:
                            need_x(2)(k)
                        pe.wait_ge(lo_ready, u + 1)
                        for i in range(2):
                            kt = 2 * k + i
                            mm = product(u, i, kt, xh[:, kt, :], xl[:, kt, :], kt == 0, kt == KT - 1, 4 * (g % 2))
                    mm.then_inc(unit_done, 1)
                    if c == 0 and j == 5:
                        sum_squares(2)()
            pe.wait_ge(evac, G_CDIN + 12)
            pe.wait_ge(rope2_d, 8)
            pe.wait_ge(rope2_p, 8)
            for h in range(4):
                kq = [DK + 2 * h, DK + 2 * h + 1]
                vq = [DV + 2 * h, DV + 2 * h + 1]
                if h:
                    pe.wait_ge(ktok_ready, h)
                    pe.wait_ge(st_prompt, h)
                for d in range(2):
                    pe.transpose(PS[0:80, 1, P * d:P * d + P], z2[:, kq[d], 0:80], ident)
                    pe.transpose(PS[0:80, 1, 256 + P * d:256 + P * d + P], z2[:, vq[d], 0:80], ident)
                    for k in range(2):
                        a, b = TT[1 + k]
                        o = 256 * k + P * d
                        pe.transpose(PS[:, 0, o:o + P], z2[:, kq[d], a:b], ident)
                        mm = pe.transpose(PS[:, 2, o:o + P], z2[:, vq[d], a:b], ident)
                mm.then_inc(kv_psum, 1)
                if h:
                    pe.wait_ge(pT_ready, h)
                    pe.wait_ge(osd_ready, h)
                for j, (bank, o, i0) in enumerate(((3, 0, 0), (4, 0, 80), (4, 256, 208))):
                    a, b = TT[j]
                    for d in range(2):
                        mm = pe.matmul(PS[0:b - a, bank, o:o + T - i0], z2[:, kq[d], a:b],
                                       z2[:, DQ + 2 * h + d, i0:T], start=d == 0, stop=d == 1)
                mm.then_inc(ds_psum, 1)
                pe.wait_ge(ktok_ready, h + 1)
                pe.wait_ge(pT_ready, h + 1)
                pe.wait_ge(qd_ready, h + 1)
                if h:
                    pe.wait_ge(od_ready, h)
                for e in range(2):
                    bank = 5 + e
                    c = P * e
                    pe.matmul(PS[:, bank, 0:T], vtok[0:80, h % 2, 0, c:c + P], pT[0:80, h % 2, 0:336],
                              start=True, stop=False)
                    pe.matmul(PS[:, bank, 80:T], vtok[:, h % 2, 1, c:c + P], pT[:, h % 2, 336:592],
                              start=False, stop=False)
                    pe.matmul(PS[:, bank, 208:T], vtok[:, h % 2, 2, c:c + P], pT[:, h % 2, 592:720],
                              start=False, stop=False)
                    for d in range(2):
                        mm = pe.matmul(PS[:, bank, 0:NS_TOK], s0[:, d, h, c:c + P], qd[:, h % 2, d, :],
                                       start=False, stop=d == 1)
                mm.then_inc(do_psum, 1)
                if h:
                    pe.wait_ge(st_sample, h)
                for d in range(2):
                    mm = pe.matmul(PS[:, 7, 256 * d:256 * d + 256], ktok[0:64, h % 2, 0, P * d:P * d + P],
                                   vtok[0:64, h % 2, 0, :], start=True, stop=True)
                mm.then_inc(st_psum, 1)
                for d in range(2):
                    out = PS[:, 0, 256 * d:256 * d + 256]
                    pe.matmul(out, ktok[64:80, h % 2, 0, P * d:P * d + P], vtok[64:80, h % 2, 0, :],
                              start=True, stop=False)
                    for k in (1, 2):
                        mm = pe.matmul(out, ktok[:, h % 2, k, P * d:P * d + P], vtok[:, h % 2, k, :],
                                       start=False, stop=k == 2)
                mm.then_inc(st_psum, 1)
                pe.wait_ge(osq_ready, h + 1)
                for e in range(2):
                    mm = pe.matmul(PS[:, 4, 0:T], ones, osq[:, e, :], start=e == 0, stop=e == 1)
                mm.then_inc(oms_psum, 1)
            pe.wait_ge(dol_ready, 5)
            pe.wait_ge(st_prompt, 4)
            pe.wait_ge(st_sample, 4)
            with pe.Fori(0, 2) as i:
                for c in range(2):
                    chunk(U_CDOUT + CU * c, G_CDOUT + c, moh, mol, i, 2 * CU, 2)
            mlp(3, U_MLP1, G_MLP1, 1, True)(0)
            with pe.Fori(1, 4) as f:
                mlp(3, U_MLP1, G_MLP1, 1, False)(f)

        @block.gpsimd
        def _(pool):
            ch = Chain(pool, pchain)

            def sum_squares(n):
                if n == 0:
                    pool.wait_ge(x_in_s, 16)
                else:
                    pool.wait_ge(evac, X_FINAL[n])
                for g in range(4):
                    xs = x[:, 4 * g:4 * g + 4, :]
                    if g == 0:
                        ch.link(pool.tensor_tensor(ssq[:], xs, xs, ALU.mult))
                    else:
                        ch.link(pool.tensor_tensor(sst[:], xs, xs, ALU.mult))
                        e = pool.tensor_tensor(ssq[:], ssq[:], sst[:], ALU.add)
                        if g < 3:
                            ch.link(e)
                e.then_inc(ssq_ready, 1)

            outs = [0]

            def send(dst, src):
                pool.dma_start(dst, src).then_inc(out_s, 16)
                outs[0] += 16

            pool.memset(kpad[:], 0.0).then_inc(pad_zero, 1)
            sum_squares(0)
            pool.wait_ge(evac, N_ABIN)
            send(v_out, zt[:, VA:VA + 2, :])
            pool.wait_ge(lat_ready, 1)
            send(lat_out, lat[:, :, PAST:])
            pool.wait_ge(turned, KK_J + 1)
            send(k_out, kA[:, :, PAST:])
            send(kk_out, kk[:, PAST:])
            pool.wait_ge(mol_ready, 16)
            pool.wait_ge(out_s, outs[0])
            sum_squares(1)
            sum_squares(2)
            pool.wait_ge(mol_ready, 16)
            pool.dma_start(tab[:, 0:2, :], tabs_in[:, 4:6, :]).then_inc(tab2_in, 16)
            pool.dma_start(decq[:], decq_in).then_inc(tab2_in, 16)
            pool.dma_start(cstate[:], conv_in).then_inc(cx_in, 16)
            pool.wait_ge(evac, G_CDIN)
            pool.memset(cxp[:, :, 3 + NS_TOK:6 + NS_TOK], 0.0).then_inc(cx_zero, 1)
            pool.wait_ge(evac, G_CDIN + 2)
            for e, c in enumerate((NS_TOK, T)):
                pool.tensor_copy(clast[:, :, e, :], z2[:, CX:CX + 8, c - 3:c]).then_inc(clast_ready, 1)
            pool.wait_ge(clast_ready, 2)
            pool.dma_start(conv_out, clast[:]).then_inc(conv_outs, 16)
            cg = z2[:, CG:CG + 8, :]

            def gate_input(g):
                pool.wait_ge(gate_ready, 4 * g + 4)
                pool.tensor_tensor(ig[:], ig[:], xc[:], ALU.mult).then_inc(igx_ready, 1)

            gate_input(0)
            pool.wait_ge(evac, G_CDIN + 4)
            half = [slice(0, 4), slice(4, 8)]
            gate_input(1)
            for r in half:
                ch.link(pool.tensor_tensor(t1[:, r], cg[:, r], cg[:, r], ALU.mult))
            gate_input(2)
            for r in half:
                ch.link(pool.tensor_scalar(t1[:, r], t1[:, r], 0.044715, 1.0, ALU.mult, ALU.add))
            gate_input(3)
            for r in half:
                e = pool.tensor_tensor(t1[:, r], t1[:, r], cg[:, r], ALU.mult)
            e.then_inc(gelu_in, 1)
            pool.wait_ge(gelu_sig, 1)
            ch.link(pool.tensor_tensor(cg, cg, t1[:], ALU.mult))
            pool.wait_ge(scan_done, 16)
            for e, c in enumerate((NS_TOK - 1, T - 1)):
                ch.link(pool.tensor_copy(hlast[:, :, e], z2[:, CX:CX + 8, c]))
            pool.dma_start(h_out, hlast[:]).then_inc(h_outs, 16)
            pool.tensor_tensor(cg, cg, z2[:, CX:CX + 8, :], ALU.mult).then_inc(outc_ready, 1)
            pool.wait_ge(outc_ready, 1)
            pool.wait_ge(tab2_in, 32)
            for k in range(4):
                x1, x2 = halves(k)
                pool.wait_ge(evac, G_CDIN + (6, 6, 8, 8)[k])
                if k:
                    pool.wait_ge(rope2_p, 2 * k)
                pool.tensor_tensor(rr[:, 2], x1, sinb, ALU.mult)
                pool.tensor_tensor(rr[:, 3], x2, cosb, ALU.mult).then_inc(rope2_p, 1)
                pool.wait_ge(rope2_p, 2 * k + 1)
                pool.wait_ge(rope2_d, 2 * k + 1)
                pool.tensor_tensor(x2, rr[:, 2], rr[:, 3], ALU.add).then_inc(rope2_p, 1)
            pool.wait_ge(rope2_p, 8)
            pool.wait_ge(dol_ready, 1)
            pool.dma_start(s0[:], s0_in).then_inc(s0_in_s, 16)
            pool.wait_ge(silu_sig, 1)
            dg = z2[:, DG:DG + 8, :]
            pool.tensor_tensor(dg, dg, sgd[:], ALU.mult).then_inc(silu_ready, 1)
            pool.wait_ge(rope2_d, 8)
            for h in range(4):
                if h >= 2:
                    pool.wait_ge(pT_ready, h - 1)
                pool.dma_start(dmask[:, h % 2, :], ret_in[:, h, :]).then_inc(mask_in[h % 2], 16)
                if h >= 1:
                    send_state(pool, h - 1, so, s_out, st_sample, st_prompt, st_out)
            send_state(pool, 3, so, s_out, st_sample, st_prompt, st_out)
            for h in range(2):
                pool.wait_ge(st_out[h], 64)
            sum_squares(3)
            pool.wait_ge(evac, G_END)
            send(y_out, x[:])
            pool.wait_ge(out_s, outs[0])
            pool.wait_ge(conv_outs, 16)
            pool.wait_ge(h_outs, 16)


def send_state(pool, h, so, s_out, st_sample, st_prompt, st_out):
    pool.wait_ge(st_sample, h + 1)
    pool.dma_start(s_out[:, 0, h], so[:, h % 2]).then_inc(st_out[h % 2], 16)
    pool.wait_ge(st_prompt, h + 1)
    pool.dma_start(s_out[:, 1, h], so[:, 2 + h % 2]).then_inc(st_out[h % 2], 16)


def constants():
    pos = np.concatenate([PAST + np.arange(NS_TOK), np.arange(TP)]).astype(np.float32)

    def angles(dim):
        inv = (np.float32(10000.0) ** (-np.arange(0, dim, 2, dtype=np.float32) / np.float32(dim))).astype(np.float32)
        return (inv[:, None] * pos[None, :]).astype(np.float32).astype(np.float64)

    tabs = np.zeros((P, 6, T), np.float32)
    a = np.tile(angles(128), (2, 1))
    tabs[:, 0], tabs[:, 1] = np.cos(a), np.sin(a)
    a = np.tile(angles(64), (4, 1))
    tabs[:, 2], tabs[:, 3] = np.cos(a), np.sin(a)
    for k in (1, 3):
        tabs[64:, k] *= -1
    a = angles(256)
    tabs[:, 4], tabs[:, 5] = np.cos(a), np.sin(a)

    cst = np.zeros((P, 4, P), np.float32)
    p = np.arange(P)
    cst[p, 0, p] = 1
    cst[p, 1, (p + 64) % P] = 1
    cst[:, 2] = 1
    cst[:, 3] = (p[:, None] // 32) % 2 == (p[None, :] // 32) % 2

    tok_c = np.concatenate([(PAST + np.arange(NS_TOK)) // CHUNK, np.zeros(NMETA, int), 1 + np.arange(SEQ) // CHUNK])
    tok_g = np.arange(T) >= NS_TOK
    key_c = np.concatenate([np.arange(PAST) // CHUNK, tok_c])
    key_g = np.concatenate([np.zeros(PAST, bool), tok_g])
    adm = np.zeros((P, SEG[3]), np.float32)
    for q, (t0, k0, k1) in enumerate(QT):
        n = QN[q][1] - QN[q][0]
        ok = (tok_g[t0:t0 + n, None] == key_g[None, k0:k1]) & (key_c[None, k0:k1] <= tok_c[t0:t0 + n, None])
        adm[0:n, SEG[q]:SEG[q + 1]] = np.where(ok, 0, NEG)

    lg = [np.log(np.float32(g)).astype(np.float64) for g in GAMMA]
    ret = np.zeros((P, 4, 720), np.float32)
    kdec = np.zeros((P, 4, 3), np.float32)
    loc = np.concatenate([np.arange(NS_TOK), np.arange(TP)])
    glen = np.concatenate([np.full(NS_TOK, NS_TOK), np.full(TP, TP)])
    for h in range(4):
        o = 0
        for t, (a, b) in enumerate(TT):
            i0 = (0, 80, 208)[t]
            i = np.arange(i0, T)
            j = np.arange(a, b)
            d = i[None, :] - j[:, None]
            ok = (d >= 0) & (tok_g[i][None, :] == tok_g[j][:, None])
            ret[0:b - a, h, o:o + T - i0] = np.where(ok, np.exp(lg[h] * np.maximum(d, 0)), 0) / 16
            kdec[0:b - a, h, t] = np.exp(lg[h] * (glen[j] - 1 - loc[j])) / 16
            o += T - i0
    decq = np.zeros((P, 4, NS_TOK), np.float32)
    for h in range(4):
        decq[:, h] = np.exp(lg[h] * (np.arange(NS_TOK) + 1))[None, :]
    return tabs, cst, adm, ret, kdec.reshape(P, 12), decq


def kernel(**inputs):
    import concourse.bacc as _bacc
    from concourse.bass_utils import run_bass_kernel_spmd as _run
    np_ = np
    a = {k: np_.asarray(v) for k, v in inputs.items()}
    f4 = np_.float32
    tabs, cst, adm, ret, kdec, decq = constants()

    def cols(v):
        return v.reshape(-1, P).T

    def pair_rows(v):
        return np_.concatenate([v[:32], v[:32], v[32:], v[32:]])[:, None]

    tok = np_.concatenate([a["x_sample"][0], a["meta_tokens"], a["x_prompt"][0]], 0)
    x_in = tok.T.reshape(KT, P, T).transpose(1, 0, 2)

    w = a["ab_w_in"][0]
    qi0 = 1536
    heads = []
    for i in range(8):
        c0, c1 = qi0 + 128 * i, qi0 + 128 * i + 64
        heads += [w[:, c0:c0 + 32], w[:, c1:c1 + 32], w[:, c0 + 32:c0 + 64], w[:, c1 + 32:c1 + 64]]
    ki, kr = 2560, 3408
    abin = np_.concatenate([w[:, 0:1280]] + heads
                           + [w[:, ki:ki + 32], w[:, kr:kr + 32], w[:, ki + 32:ki + 64], w[:, kr + 32:kr + 64]]
                           + [w[:, 2624:2640], np_.zeros((D, 112), f4), w[:, 2640:3152], w[:, 3152:3408],
                              w[:, 1280:1536]], 1)
    uq = a["b_w_uq"][0].reshape(512, 8, 192)
    ropes = []
    for i in range(4):
        r0, r1 = uq[:, 2 * i, 128:], uq[:, 2 * i + 1, 128:]
        ropes += [r0[:, :32], r1[:, :32], r0[:, 32:], r1[:, 32:]]
    uqp = np_.concatenate([uq[:, :, :128].reshape(512, 1024)] + ropes, 1)
    ukv = a["b_w_ukv"][0].reshape(256, 8, 256)

    def units(m):
        k, n = m.shape
        return m.reshape(k // 256, 2, P, n // 512, 512).transpose(3, 0, 2, 1, 4).reshape(-1, P, UNIT)

    w = a["cd_w_in"][0]
    cd_w = np_.concatenate([w[:, 0:2048], w[:, 3072:4096], w[:, 2048:3072], w[:, 4096:]], 1)

    def mlp_units(i):
        up, down = a["mlp_w_up"][i], a["mlp_w_down"][i]
        return [x_ for f in range(4) for x_ in (units(up[:, D * f:D * f + D]), units(down[D * f:D * f + D]))]

    cd = units(cd_w)
    pieces = []
    for c in range(N_CDIN):
        if c in GATE_CHUNKS:
            b = 2 * GATE_CHUNKS.index(c)
            gate = [a[n][0][i] for n in ("c_gate_a_w", "c_gate_x_w") for i in (b, b + 1)]
            gate = np_.concatenate(gate + [np_.zeros((P, 512), f4)], 1)[None]
            pieces += [cd[CU * c:CU * c + GATE_AT], gate, cd[CU * c + GATE_AT:CU * c + CU]]
        else:
            pieces += [cd[CU * c:CU * c + CU]]
    wstream = np_.concatenate(
        [units(abin), units(uqp), units(np_.ascontiguousarray(ukv[:, :, :128]).reshape(256, 1024)),
         units(np_.ascontiguousarray(ukv[:, :, 128:]).reshape(256, 1024)), units(a["ab_w_out"][0])]
        + mlp_units(0) + pieces + [units(a["cd_w_out"][0])] + mlp_units(1), 0)

    norms = [a["norm_mix"][0], a["norm_mlp"][0], a["norm_mix"][1], a["norm_mlp"][1]]
    kkg = np_.ones((P, 1), f4)
    kkg[32:64, 0], kkg[96:128, 0] = a["b_kr_norm"][0][:32], a["b_kr_norm"][0][32:]
    mkr = np_.zeros((P, 1), f4)
    mkr[32:64] = mkr[96:128] = 1
    gains = np_.concatenate(
        [cols(n) for n in norms]
        + [a["a_q_norm"][0][:, None], a["a_k_norm"][0][:, None], kkg, pair_rows(a["b_qr_norm"][0]),
           a["b_qn_norm"][0][:, None], a["b_kn_norm"][0][:, None], cols(a["b_q_lat_norm"][0]),
           cols(a["b_kv_lat_norm"][0])]
        + [cols(a["c_conv_w"][0][j]) for j in range(4)]
        + [cols(a[n][0]) for n in ("c_conv_b", "c_gate_a_b", "c_gate_x_b", "c_lambda", "d_out_norm", "state_c_h")]
        + [np_.full((P, 1), EPS, f4), mkr, np_.where(mkr > 0, 0, 1).astype(f4), kdec, np_.zeros((P, 1), f4)], 1)
    past_k = a["cache_a_k"][0, 0].transpose(2, 1, 0)
    idx, rope = a["cache_a_kidx"][0, 0].T, a["cache_b_krope"][0, 0].T
    past_kk = np_.concatenate([idx[:32], rope[:32], idx[32:], rope[32:]], 0)
    past_v = a["cache_a_v"][0, 0].reshape(PAST, 256)
    past_lat = a["cache_b_latent"][0, 0].T.reshape(2, P, PAST).transpose(1, 0, 2)
    conv_in = a["state_c_conv"][0, 0].T.reshape(8, P, 3).transpose(1, 0, 2)
    s0_in = a["state_d_s"][0, 0].reshape(4, 2, P, 256).transpose(2, 1, 0, 3)

    ins = [("x_in", x_in), ("wstream", wstream), ("gains", gains), ("cst", cst), ("tabs", tabs), ("adm", adm),
           ("ret", ret), ("decq", decq), ("past_k", past_k), ("past_kk", past_kk), ("past_v", past_v),
           ("past_lat", past_lat), ("conv_in", conv_in), ("s0_in", s0_in)]
    outs = [("y", (P, KT, T)), ("k", (P, 2, T)), ("v", (P, 2, T)), ("kk", (P, T)), ("lat", (P, 2, T)),
            ("conv", (P, 8, 2, 3)), ("h", (P, 8, 2)), ("s", (P, 2, 4, 2, 256))]
    nc = _bacc.Bacc("TRN2", target_bir_lowering=False, num_devices=1)
    arrays, args = {}, []
    for name, v in ins:
        v = np_.ascontiguousarray(v)
        arrays[f"in_{name}"] = v
        args.append(nc.dram_tensor(f"in_{name}", v.shape, mybir.dt.from_np(v.dtype), kind="ExternalInput").ap())
    for name, shape in outs:
        args.append(nc.dram_tensor(f"out_{name}", shape, F32, kind="ExternalOutput").ap())
    build(nc, *args)
    r = _run(nc, [arrays], core_ids=[0])
    o = {name: np_.asarray(r.results[0][f"out_{name}"]) for name, _ in outs}

    def rows(v):
        return v.transpose(2, 1, 0).reshape(v.shape[2], -1)

    y, k, v, lat = rows(o["y"]), rows(o["k"]), rows(o["v"]), rows(o["lat"])
    kk = o["kk"].T
    kidx = np_.concatenate([kk[:, 0:32], kk[:, 64:96]], 1)
    krope = np_.concatenate([kk[:, 32:64], kk[:, 96:128]], 1)
    res = [y[NS_TOK + NMETA:][None], y[:NS_TOK][None]]
    for g, sl in ((1, slice(NS_TOK, T)), (0, slice(0, NS_TOK))):
        n = TP if g else NS_TOK
        res += [k[sl].reshape(1, 1, n, 2, P), v[sl].reshape(1, 1, n, 2, P), kidx[sl][None, None],
                lat[sl][None, None], krope[sl][None, None],
                o["conv"][:, :, g].transpose(2, 1, 0).reshape(1, 1, 3, 1024),
                o["h"][:, :, g].T.reshape(1, 1, 1024),
                o["s"][:, g].transpose(1, 2, 0, 3).reshape(1, 1, 4, 256, 256)]
    return tuple(np_.ascontiguousarray(z) for z in res)
```

```python
from contextlib import ExitStack

import numpy as np
import concourse.bass as bass
from concourse import mybir

F32 = mybir.dt.float32
F32R = mybir.dt.float32r
ACT = mybir.ActivationFunctionType
ALU = mybir.AluOpType

P = 128
D = 2048
KT = D // P
NS_TOK, NMETA, SEQ = 64, 16, 256
TP = NMETA + SEQ
T = NS_TOK + TP
PAST = 128
KEYS = PAST + T
CHUNK = 64
EPS = 1e-6

UNIT = 1024
CU = 8
NR = 4
U_ABIN, N_ABIN = 0, 7
U_UQ = U_ABIN + CU * N_ABIN
U_KN = U_UQ + 6
U_V = U_KN + 2
U_ABOUT = U_V + 2
U_MLP0 = U_ABOUT + 4 * CU
U_CDIN, N_CDIN = U_MLP0 + 32 * CU, 12
GATE_CHUNKS, GATE_AT = (2, 3, 4, 5), 6
U_CDOUT = U_CDIN + N_CDIN * CU + len(GATE_CHUNKS)
U_MLP1 = U_CDOUT + 4 * CU
N_UNITS = U_MLP1 + 32 * CU
G_ABIN = 0
G_ABOUT = G_ABIN + N_ABIN
G_MLP0 = G_ABOUT + 4
G_CDIN = G_MLP0 + 32
G_CDOUT = G_CDIN + N_CDIN
G_MLP1 = G_CDOUT + 4
G_END = G_MLP1 + 32

KA, KK, WI, QI, CKV, VA, CQ, QA = 0, 2, 3, 4, 12, 14, 16, 20
CX, CG, DK, DQ, DV, DG = 0, 8, 16, 24, 32, 40


def cd_chunk(c):
    return U_CDIN + CU * c + sum(g < c for g in GATE_CHUNKS), CU + (c in GATE_CHUNKS)


QT = [(0, 0, 208), (80, 128, 336), (208, 128, 464)]
SEG = [0, 208, 416, 752]
QN = [(0, 80), (80, 208), (208, 336)]
KTILE = [(0, 128), (128, 208), (208, 336), (336, 464)]
TT = [(0, 80), (80, 208), (208, 336)]
TOPK_S, TOPK_P = (PAST + NS_TOK) // 4, SEQ // 4
NEG, TAKEN = -1e30, -3e38

GAIN = {}
_n = 0
for _name, _w in (("norm", 64), ("aq", 1), ("ak", 1), ("kk", 1), ("qr", 1), ("qn", 1), ("kn", 1),
                  ("qlat", 4), ("kvlat", 2), ("conv_w", 32), ("conv_b", 8), ("ga_b", 8), ("gx_b", 8),
                  ("lam", 8), ("dn", 2), ("h0", 8), ("eps", 1), ("mkr", 1), ("mki", 1), ("kdec", 12),
                  ("sel128", 31), ("sel64", 31), ("selpair", 22)):
    GAIN[_name] = _n
    _n += _w
NGAIN = _n

GAMMA = [1.0 - 2.0 ** (-5.0 - h) for h in range(4)]


def at(i, per, c):
    if i is None:
        return c
    return i * per + c


class Chain:

    def __init__(self, eng, sem):
        self.eng, self.sem, self.n = eng, sem, 0

    def mark(self, ins):
        ins.then_inc(self.sem, 1)
        self.n += 1
        return self.n

    def need(self, n):
        self.eng.wait_ge(self.sem, n)

    def link(self, ins):
        self.need(self.mark(ins))


def build(nc, x_in, wstream, gains_in, cst_in, tabs_in, adm_in, ret_in, decq_in,
          past_k, past_kk, past_v, past_lat, conv_in, s0_in,
          y_out, k_out, v_out, kk_out, lat_out, conv_out, h_out, s_out):
    ctx = ExitStack()
    with ctx:
        def sem(name):
            return ctx.enter_context(nc.semaphore(name))

        base, end = 16512, 229344
        cur = [base]

        def keep(name, shape, dt=F32):
            t = nc.alloc_sbuf_tensor_at(name, shape, dt, offset=cur[0])
            cur[0] += int(np.prod(shape[1:])) * 4
            cur[0] = (cur[0] + 31) // 32 * 32
            return t

        def place(name, shape, offset, dt=F32):
            size = int(np.prod(shape[1:])) * 4
            assert offset % 32 == 0 and offset + size <= end, (name, offset, size, end)
            return nc.alloc_sbuf_tensor_at(name, shape, dt, offset=offset)

        TB = T * 4
        x = keep("x", [P, KT, T])
        stage = keep("stage", [P, NR, UNIT])
        w_hi = keep("w_hi", [P, NR, UNIT], F32R)
        w_lo = keep("w_lo", [P, NR, UNIT], F32R)
        cst = keep("cst", [P, 2, P])
        tab_at = cur[0]
        tab = keep("tab", [P, 4, T])
        rstd = keep("rstd", [P, T])
        gains = keep("gains", [P, NGAIN])
        wiT = keep("wiT", [P, 3, 16])
        m8 = keep("m8", [P, 3, 8])
        mx = keep("mx", [P, 3, 3])
        rsum = keep("rsum", [P, 3, 3])
        sp8 = keep("sp8", [P, 2, 8])
        spt = keep("spt", [P, 4, 8])
        hlast = keep("hlast", [P, 8, 2])
        clast = keep("clast", [P, 8, 2, 3])
        cstate = keep("cstate", [P, 8, 3])
        ident, ones = cst[:, 0, :], cst[:, 1, :]

        decq = place("decq", [P, 4, NS_TOK], tab_at + 2 * TB)
        A = cur[0]
        xh = place("xh", [P, KT, T], A, F32R)
        xl = place("xl", [P, KT, T], A + KT * TB, F32R)
        moh = place("moh", [P, KT, T], A, F32R)
        mol = place("mol", [P, KT, T], A + KT * TB, F32R)
        qlath = place("qlath", [P, 4, T], A, F32R)
        qlatl = place("qlatl", [P, 4, T], A + KT * TB, F32R)
        lath = place("lath", [P, 2, KEYS], A + 8 * TB, F32R)
        latl = place("latl", [P, 2, KEYS], A + 8 * TB + 2 * KEYS * 4, F32R)
        sdq = place("sdq", [P, T], A + 14 * TB)
        sqq = place("sqq", [P, 12, T], A + 20 * TB)
        rbq = place("rbq", [P, 4, T], A + 24 * TB)
        sdk = place("sdk", [P, KEYS], A + 28 * TB)
        B = A + 2 * KT * TB
        zt = place("zt", [P, 28, T], B)
        qb = place("qb", [P, 12, T], B)
        kn = place("kn", [P, 8, KEYS], B + 12 * TB)
        C = B + 28 * TB
        kpad = place("kpad", [P, 4, KEYS], C)
        C2 = C + 4 * KEYS * 4
        adm = place("adm", [P, SEG[3]], C2)
        C3 = C2 + SEG[3] * 4
        lat = place("lat", [P, 2, KEYS], C3)
        W = C3 + 2 * KEYS * 4
        sqk = place("sqk", [P, 2, 4, KEYS], W)
        acc = place("acc", [P, SEG[3]], W)
        rt = place("rt", [P, 2, SEG[3]], W + SEG[3] * 4)
        sq4 = place("sq4", [P, 4, T], W + SEG[3] * 4)
        rb4 = place("rb4", [P, 4, T], W + 3 * SEG[3] * 4)
        sqm = place("sqm", [P, 4, T], W + 3 * SEG[3] * 4)
        sdr = place("sdr", [P, T], W + 3 * SEG[3] * 4 + 4 * TB)
        pr = place("pr", [P, 3, SEG[3]], W)
        pta = place("pta", [P, 2, 4, P], W + 9 * 1024)
        ptb = place("ptb", [P, 2, 3, P], W + 9 * 1024 + 4096)
        V = W + 9 * 1024 + 4096 + 3072
        kA = place("kA", [P, 2, KEYS], V)
        kk = place("kk", [P, KEYS], V + 2 * KEYS * 4)
        vA = place("vA", [P, 4, 256], V + 3 * KEYS * 4)
        biasA = place("biasA", [P, SEG[3]], V + 3 * KEYS * 4 + 4096)
        sdm = place("sdm", [P, 2, T], V + 3 * KEYS * 4 + 4096 + SEG[3] * 4)
        vB = place("vB", [P, 4, 1024], V)
        pairrow = place("pairrow", [P, 4, P], V + 16384)
        hh = place("hh", [P, 16, T], B, F32R)
        hl = place("hl", [P, 16, T], B + 16 * TB, F32R)
        mt1 = place("mt1", [P, 4, T], B + 32 * TB)
        mt2 = place("mt2", [P, 4, T], B + 36 * TB)
        ssq = place("ssq", [P, 4, T], W)
        sst = place("sst", [P, 4, T], W + 4 * TB)
        z2 = place("z2", [P, 48, T], B)
        xs = place("xs", [P, KT, NS_TOK], B + DG * TB)
        t1 = place("t1", [P, 8, T], B + DG * TB)
        C1 = B + 48 * TB
        cxp = place("cxp", [P, 2, T + 6], C1)
        G1 = (C1 + 2 * (T + 6) * 4 + 31) // 32 * 32
        xc = place("xc", [P, 2, T], G1)
        xch = place("xch", [P, 2, T], G1 + 2 * TB, F32R)
        xcl = place("xcl", [P, 2, T], G1 + 4 * TB, F32R)
        rg = place("rg", [P, 2, T], G1 + 6 * TB)
        ig = place("ig", [P, 2, T], G1 + 8 * TB)
        av = place("av", [P, 2, T], G1 + 10 * TB)
        tv = place("tv", [P, 2, T], G1 + 12 * TB)
        rr = place("rr", [P, 4, 2, T], C1)
        sgd = place("sgd", [P, 8, T], A + 24 * TB)
        ktok = place("ktok", [P, 2, 3, 256], C1)
        vtok = place("vtok", [P, 2, 3, 256], C1 + 6144)
        pT = place("pT", [P, 2, 720], C1 + 12288)
        dmask = place("dmask", [P, 2, 720], C1 + 12288 + 5760)
        s0 = place("s0", [P, 2, 4, 256], B)
        so = place("so", [P, 4, 2, 256], B + 8192)
        qd = place("qd", [P, 2, 2, NS_TOK], B + 16384)
        osq = place("osq", [P, 2, T], B + 17408)
        osd = place("osd", [P, T], B + 17408 + 2 * TB)

        PS = ctx.enter_context(nc.psum_tensor("PS", [P, 8, 512], F32))

        def gcol(name, i=0, rows=slice(0, P)):
            c = GAIN[name] + i
            return gains[rows, c:c + 1]

        stage_full = [sem(f"stage_full{i}") for i in range(NR)]
        hi_ready = sem("hi_ready")
        lo_ready = sem("lo_ready")
        unit_done = sem("unit_done")
        evac = sem("evac")
        const_in = sem("const_in")
        x_in_s, gains_in_s = [sem(f"x_in_s{i}") for i in range(5)], sem("gains_in_s")
        x_moved, y_outs = sem("x_moved"), sem("y_outs")
        past_in = sem("past_in")
        pad_zero = sem("pad_zero")
        xh_ready, xl_ready = sem("xh_ready"), sem("xl_ready")
        ssq_ready, ssum_done, rms_ready = sem("ssq_ready"), sem("ssum_done"), sem("rms_ready")
        dchain, pchain = sem("dchain"), sem("pchain")
        hh_ready, hl_ready, hsq_done = sem("hh_ready"), sem("hl_ready"), sem("hsq_done")
        latsq, latms, latsd, lat_ready, lath_ready, latl_ready = (
            sem("latsq"), sem("latms"), sem("latsd"), sem("lat_ready"), sem("lath_ready"),
            sem("latl_ready"))
        va_psum, tok_copied = sem("va_psum"), sem("tok_copied")
        k_sq, k_ms, k_psum, k_sd, k_rinv, k_turned = (sem("k_sq"), sem("k_ms"), sem("k_psum"), sem("k_sd"),
                                                      sem("k_rinv"), sem("k_turned"))
        qi_turned = sem("qi_turned")
        qa_sq, qa_ms, qa_sd, qa_rinv, qa_bc, qa_turned = (
            sem("qa_sq"), sem("qa_ms"), sem("qa_sd"), sem("qa_rinv"), sem("qa_bc"), sem("qa_turned"))
        qb_sq, qb_ms, qb_sd, qb_rinv, qb_bc, qb_turned = (
            sem("qb_sq"), sem("qb_ms"), sem("qb_sd"), sem("qb_rinv"), sem("qb_bc"), sem("qb_turned"))
        kn_raw, kn_sq, kn_ms, kn_sd, kn_rinv, kn_bc, kn_turned = (
            sem("kn_raw"), sem("kn_sq"), sem("kn_ms"), sem("kn_sd"), sem("kn_rinv"), sem("kn_bc"), sem("kn_turned"))
        kpad_ready, pair_ready = sem("kpad_ready"), sem("pair_ready")
        idx_psum, relu_ready, idx_added, bias_ready = (sem("idx_psum"), sem("relu_ready"),
                                                       sem("idx_added"), sem("bias_ready"))
        qkv_evac = sem("qkv_evac")
        sc_psum, smax, p_ready, pn_ready = sem("sc_psum"), sem("smax"), sem("p_ready"), sem("pn_ready")
        pt_psum, pta_ready, ptb_ready = sem("pt_psum"), sem("pta_ready"), sem("ptb_ready")
        o_psum, moh_ready, mol_ready = sem("o_psum"), sem("moh_ready"), sem("mol_ready")
        out_s = sem("out_s")
        tab2_in, cx_in, cx_copied, conv_outs = sem("tab2_in"), sem("cx_in"), sem("cx_copied"), sem("conv_outs")
        clast_ready, exp_ready, tanh_ready, asq_ready, w_ready = (
            sem("clast_ready"), sem("exp_ready"), sem("tanh_ready"), sem("asq_ready"), sem("w_ready"))
        cx_zero = sem("cx_zero")
        xc_ready, xch_ready, xcl_ready = sem("xc_ready"), sem("xch_ready"), sem("xcl_ready")
        gate_ready = sem("gate_ready")
        sqrt_ready, igx_ready, scan_done = sem("sqrt_ready"), sem("igx_ready"), sem("scan_done")
        gelu_in, gelu_sig = sem("gelu_in"), sem("gelu_sig")
        silu_sig, silu_ready = sem("silu_sig"), sem("silu_ready")
        outc_ready, h_outs = sem("outc_ready"), sem("h_outs")
        sp_exp, sp_abs, sp_ready = sem("sp_exp"), sem("sp_abs"), sem("sp_ready")
        rope2_d, rope2_p = sem("rope2_d"), sem("rope2_p")
        s0_in_s = sem("s0_in_s")
        mask_in = [sem("mask_in0"), sem("mask_in1")]
        kv_psum, ktok_ready, ds_psum, pT_ready, qd_ready = (sem("kv_psum"), sem("ktok_ready"),
                                                            sem("ds_psum"), sem("pT_ready"), sem("qd_ready"))
        on_ready = sem("on_ready")
        do_psum, osq_ready, oms_psum, osd_ready, od_ready = (sem("do_psum"), sem("osq_ready"),
                                                             sem("oms_psum"), sem("osd_ready"), sem("od_ready"))
        st_psum, st_sample, st_prompt = sem("st_psum"), sem("st_sample"), sem("st_prompt")
        st_out = [sem("st_out0"), sem("st_out1")]
        doh_ready, dol_ready = sem("doh_ready"), sem("dol_ready")

        block = ctx.enter_context(nc.Block())
        zt4 = zt[:].rearrange("p (c m) t -> p c m t", m=4)
        cosb = tab[:, 0, :].unsqueeze(1).to_broadcast([P, 2, T])
        sinb = tab[:, 1, :].unsqueeze(1).to_broadcast([P, 2, T])

        def halves(k):
            t0 = (DK, DQ)[k // 2] + 4 * (k % 2)
            v = z2[:, t0:t0 + 4, :].rearrange("p (h e) t -> p h e t", e=2)
            return v[:, :, 0, :], v[:, :, 1, :]

        X_FINAL = [0, G_MLP0, G_CDIN, G_MLP1]
        NORM_G = [G_ABIN, G_MLP0, G_CDIN, G_MLP1]
        X_PIECES = [(0, 2), (2, 4), (4, 8), (8, 12), (12, 16)]
        ALL, LIVE = slice(0, T), slice(NMETA, T)
        COLS = [ALL, ALL, ALL, LIVE]
        MOVES = ((slice(0, NS_TOK), slice(NMETA, NMETA + NS_TOK)), (slice(NMETA + NS_TOK, T),) * 2)

        def SB(n):
            return 4 * (1 - NORM_G[n] % 2) + 3

        IDX_AT = [(3, 4), (3, 5), (3, 6)] + [(4, k) for k in range(1, 6)]

        @block.sync
        def _(sp):
            sp.dma_start(gains[:], gains_in).then_inc(gains_in_s, 16)
            for what in ("w0", "x0", "x1", "w1", "x2", "w2", "w3", "x3", "x4"):
                s = int(what[1])
                if what[0] == "w":
                    sp.dma_start(stage[:, s, :], wstream[s]).then_inc(stage_full[s], 16)
                else:
                    a, b = X_PIECES[s]
                    sp.dma_start(x[:, a:b], x_in[:, a:b]).then_inc(x_in_s[s], 16)
            sp.dma_start(cst[:], cst_in).then_inc(const_in, 16)
            sp.dma_start(tab[:], tabs_in[:, 0:4, :]).then_inc(const_in, 16)
            with sp.Fori(1, N_UNITS // NR) as i:
                for s in range(NR):
                    sp.wait_ge(lo_ready, i * NR + (s + 1 - NR))
                    sp.dma_start(stage[:, s, :], wstream[i * NR + s]).then_inc(stage_full[s], 16)
            for u in range(N_UNITS // NR * NR, N_UNITS):
                sp.wait_ge(lo_ready, u - NR + 1)
                sp.dma_start(stage[:, u % NR, :], wstream[u]).then_inc(stage_full[u % NR], 16)

        @block.scalar
        def _(act):
            def split(u, i=None, per=0):
                s = u % NR
                act.wait_ge(stage_full[s], at(i, 16 * per // NR, 16 * (u // NR + 1)))
                if u >= NR:
                    act.wait_ge(unit_done, at(i, per, u - NR + 1))
                act.activation(w_hi[:, s, :], stage[:, s, :], ACT.Copy).then_inc(hi_ready, 1)

            def step(u0, i=None, per=0, last=False, hook=None, each=None):
                for k in range(NR, CU + (0 if last else NR)):
                    split(u0 + k, i, per)
                    if hook and k == NR + 5:
                        hook()
                    if each:
                        each(k)

            def norm_tiles(n, t0, t1):
                cs = COLS[n]
                for t in range(t0, t1):
                    act.activation(xh[:, t, cs], x[:, t, cs], ACT.Copy,
                                   scale=gcol("norm", 16 * n + t)).then_inc(xh_ready, 1)

            def norm_ahead(n):
                def f(k):
                    if k == NR:
                        act.wait_ge(evac, X_FINAL[n] - 1)
                    if k < NR + 6:
                        norm_tiles(n, 2 * (k - NR), 2 * (k - NR) + 2)
                return f

            def norm_rest(n):
                act.wait_ge(evac, X_FINAL[n])
                norm_tiles(n, 12, KT)

            def rms(n):
                def f():
                    act.wait_ge(ssum_done, n + 1)
                    act.activation(rstd[:, COLS[n]], PS[:, SB(n), COLS[n]], ACT.Sqrt, scale=1.0 / D,
                                   bias=gcol("eps")).then_inc(rms_ready, 1)
                return f

            def attend(g0, h0, sb):
                pb, ob = 4 - sb, 6 - sb
                for s in range(8 + 3):
                    if s < 8:
                        g = g0 + s
                        act.wait_ge(smax, g + 1)
                        for q in range(3):
                            seg = pr[:, g % 3, SEG[q]:SEG[q + 1]]
                            e = act.activation(seg, seg, ACT.Exp, bias=mx[:, g % 3, q:q + 1],
                                               accum_out=rsum[:, g % 3, q:q + 1])
                        e.then_inc(p_ready, 1)
                    if 2 <= s < 10:
                        g = g0 + s - 2
                        act.wait_ge(pt_psum, g + 1)
                        if g >= 2:
                            act.wait_ge(o_psum, g - 1)
                        act.activation(pta[:, g % 2], PS[:, pb, :].rearrange("p (a b) -> p a b", a=4),
                                       ACT.Copy).then_inc(pta_ready, 1)
                    if s >= 3:
                        g = g0 + s - 3
                        act.wait_ge(o_psum, g + 1)
                        act.activation(moh[:, h0 + s - 3, :], PS[:, ob + g % 2, 0:T],
                                       ACT.Copy).then_inc(moh_ready, 1)

            def mlp(n, u_mlp, g_mlp, L, whole, ahead=None):
                cs = COLS[n]

                def body(f):
                    for c in range(4):
                        step(u_mlp + CU * c, f, 64, hook=rms(n) if whole and c == 0 else None)
                        g = 16 * L + c
                        act.wait_ge(evac, at(f, 8, g_mlp + c + 1))
                        if not (whole and c == 0 and L == 0):
                            act.wait_ge(hl_ready, at(f, 4, g))
                        act.activation(mt2[:, :, cs], mt1[:, :, cs], ACT.Square).then_inc(hsq_done, 1)
                        act.wait_ge(hsq_done, at(f, 4, g + 1))
                        act.activation(hh[:, 4 * c:4 * c + 4, cs], mt2[:, :, cs], ACT.Copy).then_inc(hh_ready, 1)
                    for c in range(4):
                        step(u_mlp + 32 + CU * c, f, 64, each=ahead if c == 3 else None)
                return body

            def mlp_last(u_mlp, g_mlp, L):
                f = 3
                cs = LIVE
                for c in range(4):
                    step(u_mlp + 64 * f + CU * c)
                    g = 16 * L + 4 * f + c
                    act.wait_ge(evac, g_mlp + 8 * f + c + 1)
                    act.wait_ge(hl_ready, g)
                    act.activation(mt2[:, :, cs], mt1[:, :, cs], ACT.Square).then_inc(hsq_done, 1)
                    act.wait_ge(hsq_done, g + 1)
                    act.activation(hh[:, 4 * c:4 * c + 4, cs], mt2[:, :, cs], ACT.Copy).then_inc(hh_ready, 1)
                for c in range(4):
                    step(u_mlp + 64 * f + 32 + CU * c, last=c == 3)
                    if c:
                        act.wait_ge(evac, G_END - 4 + c)
                        act.dma_start(y_out[:, 4 * c - 4:4 * c], x[:, 4 * c - 4:4 * c]).then_inc(y_outs, 16)

            act.wait_ge(gains_in_s, 16)
            lam = gains[:, GAIN["lam"]:GAIN["lam"] + 8]
            act.activation(spt[:, 0, :], lam, ACT.Abs).then_inc(sp_abs, 1)
            act.wait_ge(sp_abs, 1)
            act.activation(spt[:, 1, :], spt[:, 0, :], ACT.Exp, scale=-1.0).then_inc(sp_exp, 1)
            for u, i_ in ((0, (0, 1)), (1, (2,)), (2, ()), (3, (3, 4))):
                split(u)
                for i in i_:
                    act.wait_ge(x_in_s[i], 16)
                    norm_tiles(0, *X_PIECES[i])

            def ab_piece(g, j):
                if g == 0 and 5 <= j < 10:
                    dst, src = ((kk[:, 0:PAST], past_kk), (kA[:, :, 0:PAST], past_k), (lat[:, :, 0:PAST], past_lat),
                                (adm[:], adm_in), (vA[:, 0, :], past_v))[j - 5]
                    act.dma_start(dst, src).then_inc(past_in, 16)
                if g == 1:
                    if j == 4:
                        act.wait_ge(evac, 1)
                        act.activation(sq4[:, 0:3], zt[:, 0:3, :], ACT.Square).then_inc(k_sq, 1)
                    if j == 6:
                        act.wait_ge(k_ms, 1)
                        act.activation(sdr[0:8], PS[0:8, 0, 0:T], ACT.Sqrt, bias=gcol("eps", rows=slice(0, 8))
                                       ).then_inc(k_sd, 1)
                    if j == 9:
                        act.wait_ge(k_psum, 1)
                        act.activation(wiT[:].rearrange("p a b -> p (a b)"), PS[:, 0, 0:48],
                                       ACT.Copy).then_inc(tok_copied, 1)
                for n, (gc, k) in enumerate(IDX_AT):
                    if (g, j) == (gc, k + 4):
                        for h in (2 * n, 2 * n + 1):
                            act.wait_ge(idx_psum, h + 1)
                            if h >= 2:
                                act.wait_ge(idx_added, h - 1)
                            b = 4 * (1 - g % 2) + 2 * (h % 2)
                            act.activation(rt[:, h % 2, 0:416], PS[:, b, 0:416], ACT.Relu, scale=1.0 / 32)
                            act.activation(rt[:, h % 2, 416:752], PS[:, b + 1, 0:336], ACT.Relu,
                                           scale=1.0 / 32).then_inc(relu_ready, 1)
                if g == 4 and j == 9:
                    act.wait_ge(evac, 4)
                    act.wait_ge(qi_turned, 2)
                    act.activation(sqm[:, 0:2, :], zt[:, CKV:CKV + 2, :], ACT.Square).then_inc(latsq, 1)
                if g == 4 and j == 10:
                    act.wait_ge(latms, 1)
                    act.activation(sdm[:, 0, :], PS[:, 7, 0:T], ACT.Sqrt, scale=1.0 / 256,
                                   bias=gcol("eps")).then_inc(latsd, 1)
                    act.wait_ge(va_psum, 1)
                    act.activation(vA[:, 2:4, :], PS[:, 5, :].rearrange("p (a b) -> p a b", a=2), ACT.Copy)
                    act.activation(vA[0:80, 1, :], PS[0:80, 6, 0:256], ACT.Copy).then_inc(tok_copied, 1)
                if g == 5 and j == 4:
                    act.wait_ge(evac, 5)
                    act.activation(sqm[:], zt[:, CQ:CQ + 4, :], ACT.Square).then_inc(latsq, 1)
                if g == 5 and j == 7:
                    act.wait_ge(latms, 2)
                    act.activation(sdm[:, 1, :], PS[:, 0, 0:T], ACT.Sqrt, scale=1.0 / 512,
                                   bias=gcol("eps")).then_inc(latsd, 1)
                if (g, j) in ((6, 4), (7, 3)):
                    if g == 6:
                        act.wait_ge(idx_added, 16)
                    act.wait_ge(evac, g)
                    act.activation(sq4[:], zt4[:, g - 1], ACT.Square).then_inc(qa_sq, 1)
                if g == 6 and j == 5:
                    act.wait_ge(lat_ready, 2)
                    act.wait_ge(past_in, 80)
                    act.activation(qlath[:], zt[:, CQ:CQ + 4, :], ACT.Copy).then_inc(lath_ready, 1)
                if g == 6 and j == 11:
                    act.activation(lath[:], lat[:], ACT.Copy).then_inc(lath_ready, 1)
                if (g, j) in ((6, 6), (7, 5)):
                    act.wait_ge(qa_ms, g - 5)
                    act.activation(sdr[0:8], PS[0:8, 4 * (1 - g % 2), 0:T], ACT.Sqrt,
                                   bias=gcol("eps", rows=slice(0, 8))).then_inc(qa_sd, 1)

            for g in range(N_ABIN):
                for j in range(NR, CU + NR):
                    split(U_ABIN + CU * g + j)
                    if g == 0 and j == NR + 5:
                        rms(0)()
                    ab_piece(g, j)
            ab_piece(7, 3)
            for k in range(6):
                split(U_UQ + 4 + k)
                ab_piece(7, 4 + k)
                if k % 2:
                    c = k // 2
                    act.wait_ge(qkv_evac, c + 1)
                    act.activation(sqq[:, 4 * c:4 * c + 4], qb[:, 4 * c:4 * c + 4, :], ACT.Square).then_inc(qb_sq, 1)
            act.wait_ge(qb_ms, 1)
            act.activation(sdq[0:16], PS[0:16, 4, 0:T], ACT.Sqrt, bias=gcol("eps", rows=slice(0, 16))
                           ).then_inc(qb_sd, 1)
            attend(0, 0, 0)
            for c in range(2):
                act.wait_ge(unit_done, U_KN + c + 1)
                if c == 0:
                    act.wait_ge(out_s, 64)
                k4 = kn[:, 4 * c:4 * c + 4, :]
                act.activation(k4, PS[:, 0:4, 0:KEYS], ACT.Copy).then_inc(kn_raw, 1)
                act.wait_ge(kn_raw, c + 1)
                act.activation(sqk[:, c], k4, ACT.Square).then_inc(kn_sq, 1)
                split(U_KN + 4 + c)
            for c in range(2):
                act.wait_ge(unit_done, U_V + c + 1)
                dst = vB[:, :, 512 * c:512 * c + 512]
                act.activation(dst[0:80, 1, :], PS[0:80, 1, :], ACT.Copy)
                act.activation(dst[:, 0, :], PS[:, 0, :], ACT.Copy)
                act.activation(dst[:, 2:4, :], PS[:, 2:4, :], ACT.Copy).then_inc(qkv_evac, 1)
                split(U_V + 4 + c)
                if c == 0:
                    act.wait_ge(kn_ms, 1)
                    act.activation(sdk[0:8], PS[0:8, 4, 0:KEYS], ACT.Sqrt, bias=gcol("eps", rows=slice(0, 8))
                                   ).then_inc(kn_sd, 1)
            attend(8, 8, 4)
            for c in range(4):
                step(U_ABOUT + CU * c, each=norm_ahead(1) if c == 3 else None)
            norm_rest(1)
            mlp(1, U_MLP0, G_MLP0, 0, True)(0)
            with act.Fori(1, 3) as f:
                mlp(1, U_MLP0, G_MLP0, 0, False)(f)
            mlp(1, U_MLP0, G_MLP0, 0, False, norm_ahead(2))(3)

            norm_rest(2)

            def gate_piece(c, j):
                g = c - 2
                if 0 <= g < 4:
                    if j == 4:
                        act.wait_ge(evac, G_CDIN + 1 + g // 2)
                        if g == 0:
                            act.wait_ge(cx_zero, 1)
                            act.wait_ge(cx_in, 16)
                        else:
                            act.wait_ge(xc_ready, 4 * g)
                        src = z2[:, CX + 2 * g:CX + 2 * g + 2, :]
                        act.activation(cxp[:, :, 0:3], cstate[:, 2 * g:2 * g + 2, :], ACT.Copy)
                        act.activation(cxp[:, :, 3:3 + NS_TOK], src[:, :, 0:NS_TOK], ACT.Copy)
                        act.activation(cxp[:, :, 6 + NS_TOK:], src[:, :, NS_TOK:], ACT.Copy).then_inc(cx_copied, 1)
                    if j == 7:
                        act.wait_ge(xc_ready, 4 * g + 4)
                        act.activation(xch[:], xc[:], ACT.Copy).then_inc(xch_ready, 1)
                    if j == 10:
                        act.wait_ge(unit_done, cd_chunk(c)[0] + GATE_AT + 1)
                        if g:
                            act.wait_ge(w_ready, g)
                            act.wait_ge(scan_done, 4 * g)
                        for n in range(4):
                            dst, bias = (rg, "ga_b") if n < 2 else (ig, "gx_b")
                            act.activation(dst[:, n % 2, :], PS[:, 4 * (1 - (G_CDIN + c) % 2) + n, 0:T],
                                           ACT.Sigmoid, bias=gcol(bias, 2 * g + n % 2)).then_inc(gate_ready, 1)
                g = c - 3
                if 0 <= g < 4:
                    if j == 5:
                        act.wait_ge(gate_ready, 4 * g + 4)
                        act.wait_ge(sp_ready, 2)
                        for n in range(2):
                            act.activation(av[:, n, :], rg[:, n, :], ACT.Exp,
                                           scale=sp8[:, 1, 2 * g + n:2 * g + n + 1]).then_inc(exp_ready, 1)
                        for n in range(2):
                            act.activation(tv[:, n, :], rg[:, n, :], ACT.Tanh,
                                           scale=sp8[:, 0, 2 * g + n:2 * g + n + 1]).then_inc(tanh_ready, 1)
                    if j == 6:
                        act.wait_ge(exp_ready, 2 * g + 2)
                        act.wait_ge(tanh_ready, 2 * g + 2)
                        act.activation(rg[:], av[:], ACT.Square).then_inc(asq_ready, 1)
                    if j == 8:
                        act.wait_ge(w_ready, g + 1)
                        act.activation(tv[:], tv[:], ACT.Sqrt).then_inc(sqrt_ready, 1)
                if c == 6 and j == 10:
                    act.wait_ge(gelu_in, 1)
                    act.activation(t1[:, 0:4], t1[:, 0:4], ACT.Sigmoid, scale=2 * 0.7978845608028654)
                if c == 6 and j == 11:
                    act.activation(t1[:, 4:8], t1[:, 4:8], ACT.Sigmoid,
                                   scale=2 * 0.7978845608028654).then_inc(gelu_sig, 1)
                if c == 11 and j == 8:
                    act.wait_ge(outc_ready, 1)
                    for src, dst in MOVES:
                        e = act.activation(moh[:, 0:8, dst], z2[:, CG:CG + 8, src], ACT.Copy)
                    e.then_inc(doh_ready, 1)
                if c == 11 and j == 10:
                    act.wait_ge(rope2_d, 8)
                    act.wait_ge(rope2_p, 8)
                    tokens_first(0)

            def tokens_first(h):
                act.wait_ge(kv_psum, h + 1)
                if h >= 2:
                    act.wait_ge(st_psum, 2 * (h - 1))
                kd = [gains[r, GAIN["kdec"] + 3 * h + t:GAIN["kdec"] + 3 * h + t + 1]
                      for t, r in ((0, slice(0, 80)), (1, slice(0, P)), (2, slice(0, P)))]
                act.activation(ktok[0:80, h % 2, 0, :], PS[0:80, 6, 0:256], ACT.Copy, scale=kd[0])
                act.activation(ktok[:, h % 2, 1, :], PS[:, 7, 0:256], ACT.Copy, scale=kd[1])
                act.activation(ktok[:, h % 2, 2, :], PS[:, 7, 256:512], ACT.Copy, scale=kd[2])
                act.activation(vtok[0:80, h % 2, 0, :], PS[0:80, 6, 256:512], ACT.Copy)
                act.activation(vtok[:, h % 2, 1:3, :], PS[:, 5, :].rearrange("p (a b) -> p a b", a=2),
                               ACT.Copy).then_inc(ktok_ready, 1)

            for c in range(N_CDIN):
                u0, n = cd_chunk(c)
                for j in range(NR, n + NR):
                    split(u0 + j)
                    if c == 0 and j == NR + 5:
                        rms(2)()
                    gate_piece(c, j)
            act.wait_ge(evac, G_CDIN + 12)
            act.activation(sgd[:, 0:4], z2[:, DG:DG + 4, :], ACT.Sigmoid).then_inc(silu_sig, 1)
            for h in range(4):
                act.wait_ge(st_psum, 2 * h + 1)
                if h >= 2:
                    act.wait_ge(st_out[h % 2], 32)
                act.activation(so[:, 2 + h % 2], PS[:, 5, :].rearrange("p (a b) -> p a b", a=2),
                               ACT.Copy).then_inc(st_prompt, 1)
                act.wait_ge(do_psum, h + 1)
                act.activation(osq[:], PS[:, 1:3, 0:T], ACT.Square).then_inc(osq_ready, 1)
                if h < 3:
                    tokens_first(h + 1)
                act.wait_ge(oms_psum, h + 1)
                act.activation(osd[:], PS[:, 0, 0:T], ACT.Sqrt, scale=1.0 / 256,
                               bias=gcol("eps")).then_inc(osd_ready, 1)
                if h == 0:
                    act.activation(sgd[:, 4:8], z2[:, DG + 4:DG + 8, :], ACT.Sigmoid).then_inc(silu_sig, 1)
                act.wait_ge(od_ready, h + 1)
                for src, dst in MOVES:
                    e = act.activation(moh[:, 8 + 2 * h:10 + 2 * h, dst], z2[:, DG + 2 * h:DG + 2 * h + 2, src],
                                       ACT.Copy)
                e.then_inc(doh_ready, 1)
            for c in range(4):
                step(U_CDOUT + CU * c, each=norm_ahead(3) if c == 3 else None)
            norm_rest(3)
            mlp(3, U_MLP1, G_MLP1, 1, True)(0)
            with act.Fori(1, 3) as f:
                mlp(3, U_MLP1, G_MLP1, 1, False)(f)
            mlp_last(U_MLP1, G_MLP1, 1)
            act.wait_ge(evac, G_END)
            act.dma_start(y_out[:, 12:KT], x[:, 12:KT]).then_inc(y_outs, 16)
            act.wait_ge(y_outs, 64)

        @block.vector
        def _(dve):
            ch = Chain(dve, dchain)

            def split(u, i=None, per=0):
                s = u % NR
                dve.wait_ge(hi_ready, at(i, per, u + 1))
                dve.tensor_tensor(w_lo[:, s, :], stage[:, s, :], w_hi[:, s, :].bitcast(F32),
                                  ALU.subtract).then_inc(lo_ready, 1)

            def step(u0, take, i=None, per=0, last=False, each=None):
                for k in range(NR, CU + (0 if last else NR)):
                    if k == CU + NR - 1:
                        take()
                    split(u0 + k, i, per)
                    if each:
                        each(k)
                if last:
                    take()

            def norm_tiles(n, t0, t1):
                cs = COLS[n]
                for t in range(t0, t1):
                    dve.wait_ge(xh_ready, 16 * n + t + 1)
                    dve.scalar_tensor_tensor(xl[:, t, cs], x[:, t, cs], gcol("norm", 16 * n + t),
                                             xh[:, t, cs].bitcast(F32), ALU.mult,
                                             ALU.subtract).then_inc(xl_ready, 1)

            def norm_ahead(n):
                def f(k):
                    if k < NR + 6:
                        norm_tiles(n, 2 * (k - NR), 2 * (k - NR) + 2)
                return f

            def norm_rest(n):
                dve.wait_ge(evac, X_FINAL[n])
                norm_tiles(n, 12, KT)

            def rms(n):
                dve.wait_ge(rms_ready, n + 1)
                ch.link(dve.reciprocal(rstd[:, COLS[n]], rstd[:, COLS[n]]))

            rstd4 = rstd[:].unsqueeze(1).to_broadcast([P, 4, T])

            def banks(g, cs=ALL):
                b = 4 * (g % 2)
                return PS[:, b:b + 4, cs]

            def take_scaled(u0, g, dst, i=None, su=0, sg=0):
                dve.wait_ge(unit_done, at(i, su, u0 + CU))
                dve.tensor_tensor(dst, banks(g), rstd4, ALU.mult).then_inc(evac, 1)

            def take_added(u0, g, c, cs, i=None, su=0):
                dve.wait_ge(unit_done, at(i, su, u0 + CU))
                dst = x[:, 4 * c:4 * c + 4, cs]
                dve.tensor_tensor(dst, banks(g, cs), dst, ALU.add).then_inc(evac, 1)

            z24 = z2[:].rearrange("p (c m) t -> p c m t", m=4)

            def attend(g0, h0, bias, scale, sb):
                pb, ob = 4 - sb, 6 - sb
                for s in range(8 + 3):
                    if g0 == 0 and s == 10:
                        dve.wait_ge(qb_sd, 1)
                        dve.reciprocal(sdq[0:16], sdq[0:16]).then_inc(qb_rinv, 1)
                    if s < 8:
                        g = g0 + s
                        dve.wait_ge(sc_psum, g + 1)
                        if g >= 3:
                            dve.wait_ge(pt_psum, g - 2)
                        for q in range(3):
                            src = PS[:, sb + 2 * (g % 2) + q // 2, SEG[q] - 416 * (q // 2):SEG[q + 1] - 416 * (q // 2)]
                            e = dve.tensor_tensor_reduce(pr[:, g % 3, SEG[q]:SEG[q + 1]], src,
                                                         bias[:, SEG[q]:SEG[q + 1]], scale, TAKEN,
                                                         ALU.add, ALU.max, mx[:, g % 3, q:q + 1])
                        ch.link(e)
                        dve.tensor_scalar(mx[:, g % 3, :], mx[:, g % 3, :], -1.0, None,
                                          ALU.mult).then_inc(smax, 1)
                    if 1 <= s < 9:
                        g = g0 + s - 1
                        dve.wait_ge(p_ready, g + 1)
                        ch.link(dve.reciprocal(rsum[:, g % 3, :], rsum[:, g % 3, :]))
                        for q in range(3):
                            seg = pr[:, g % 3, SEG[q]:SEG[q + 1]]
                            e = dve.tensor_scalar(seg, seg, rsum[:, g % 3, q:q + 1], None, ALU.mult)
                        e.then_inc(pn_ready, 1)
                    if 2 <= s < 10:
                        g = g0 + s - 2
                        dve.wait_ge(pt_psum, g + 1)
                        if g >= 2:
                            dve.wait_ge(o_psum, g - 1)
                        dve.tensor_copy(ptb[0:80, g % 2], PS[0:80, pb + 1, 0:384].rearrange(
                            "p (a b) -> p a b", a=3)).then_inc(ptb_ready, 1)
                    if s >= 3:
                        g = g0 + s - 3
                        dve.wait_ge(moh_ready, g + 1)
                        dve.tensor_tensor(mol[:, h0 + s - 3, :], PS[:, ob + g % 2, 0:T],
                                          moh[:, h0 + s - 3, :].bitcast(F32),
                                          ALU.subtract).then_inc(mol_ready, 1)

            def take_up(u0, g, c, f, whole, L, cs):
                dve.wait_ge(unit_done, at(f, 64, u0 + CU))
                if not (whole and c == 0 and L == 0):
                    dve.wait_ge(hh_ready, at(f, 4, 16 * L + c))
                dve.scalar_tensor_tensor(mt1[:, :, cs], banks(g, cs), 0.0,
                                         rstd[:, cs].unsqueeze(1).to_broadcast([P, 4, cs.stop - cs.start]),
                                         ALU.max, ALU.mult).then_inc(evac, 1)

            def low_h(c, f, L, cs):
                dve.wait_ge(hh_ready, at(f, 4, 16 * L + c + 1))
                dve.tensor_tensor(hl[:, 4 * c:4 * c + 4, cs], mt2[:, :, cs], hh[:, 4 * c:4 * c + 4, cs].bitcast(F32),
                                  ALU.subtract).then_inc(hl_ready, 1)

            def mlp(n, u_mlp, g_mlp, L, whole, last=False, ahead=None):
                cs = COLS[n]

                def body(f):
                    for c in range(4):
                        def take():
                            if whole and c == 0:
                                rms(n)
                            take_up(u_mlp + CU * c, g_mlp + c, c, f, whole, L, cs)

                        step(u_mlp + CU * c, take, f, 64)
                        low_h(c, f, L, cs)
                    for c in range(4):
                        step(u_mlp + 32 + CU * c,
                             lambda: take_added(u_mlp + 32 + CU * c, g_mlp + c, c, cs, f, 64), f, 64,
                             last=last and c == 3, each=ahead if c == 3 else None)
                return body

            dve.wait_ge(gains_in_s, 16)
            for u, i_ in ((0, (0, 1)), (1, (2,)), (2, ()), (3, (3, 4))):
                split(u)
                for i in i_:
                    norm_tiles(0, *X_PIECES[i])
            u_, z_, z2_ = spt[:, 1, :], spt[:, 2, :], spt[:, 3, :]
            dve.wait_ge(sp_exp, 1)
            ch.link(dve.tensor_scalar(z_, u_, 2.0, None, ALU.add))
            ch.link(dve.reciprocal(z_, z_))
            ch.link(dve.tensor_tensor(z_, z_, u_, ALU.mult))
            ch.link(dve.tensor_tensor(z2_, z_, z_, ALU.mult))
            ch.link(dve.tensor_scalar(u_, z2_, 1.0 / 17, 1.0 / 15, ALU.mult, ALU.add))
            for k in (13, 11, 9, 7, 5, 3, 1):
                ch.link(dve.tensor_tensor(u_, u_, z2_, ALU.mult))
                ch.link(dve.tensor_scalar(u_, u_, 1.0 / k, None, ALU.add))
            ch.link(dve.tensor_tensor(u_, u_, z_, ALU.mult))
            lam = gains[:, GAIN["lam"]:GAIN["lam"] + 8]
            ch.link(dve.tensor_scalar(z_, lam, -1.0, 0.0, ALU.mult, ALU.max))
            ch.link(dve.scalar_tensor_tensor(u_, u_, 2.0, z_, ALU.mult, ALU.add))
            dve.tensor_scalar(sp8[:, 0, :], u_, 8.0, None, ALU.mult).then_inc(sp_ready, 1)
            dve.tensor_scalar(sp8[:, 1, :], u_, -8.0, None, ALU.mult).then_inc(sp_ready, 1)


            def tabb(k, n):
                return tab[:, k, :].unsqueeze(1).to_broadcast([P, n, T])

            def half_sines(out, q, k, side, gain=None):
                a, b = (slice(0, 64), slice(64, P)) if side == 0 else (slice(64, P), slice(0, 64))
                n = q.shape[1]
                tb = tab[a, k + 1, :].unsqueeze(1).to_broadcast([64, n, T])
                if gain is None:
                    return ch.mark(dve.tensor_tensor(out[b], q[a], tb, ALU.mult))
                return ch.mark(dve.scalar_tensor_tensor(out[b], q[a], gcol(gain, rows=a), tb, ALU.mult, ALU.mult))

            def ab_piece(g, j):
                side = PS[:, 4 * (1 - g % 2):4 * (1 - g % 2) + 4, 0:T]
                if g == 1:
                    kA_, kk_ = kA[:, :, PAST:], kk[:, PAST:]
                    if j == 4:
                        dve.wait_ge(evac, 1)
                        ka = zt[:, KA:KA + 2, :]
                        half_sines(rb4[:, 0:2], ka, 0, 0, "ak")
                        half_sines(rb4[:, 0:2], ka, 0, 1, "ak")
                        ch.mark(dve.scalar_tensor_tensor(kA_, ka, gcol("ak"), tabb(0, 2), ALU.mult, ALU.mult))
                    if j == 5:
                        k_ = zt[:, KK:KK + 1, :]
                        half_sines(rb4[:, 2:3], k_, 2, 0, "kk")
                        half_sines(rb4[:, 2:3], k_, 2, 1, "kk")
                        ch.link(dve.scalar_tensor_tensor(kk_, zt[:, KK, :], gcol("kk"), tab[:, 2, :], ALU.mult,
                                                         ALU.mult))
                        ch.mark(dve.tensor_tensor(kA_, kA_, rb4[:, 0:2], ALU.add))
                        ch.mark(dve.tensor_tensor(kk_, kk_, rb4[:, 2], ALU.add))
                    if j == 6:
                        dve.wait_ge(k_sd, 1)
                        dve.reciprocal(sdr[0:8], sdr[0:8]).then_inc(k_rinv, 1)
                    if j == 9:
                        dve.wait_ge(k_psum, 1)
                        ch.need(ch.n)
                        dve.tensor_tensor(kA_, kA_, PS[:, 1:3, 0:T], ALU.mult).then_inc(k_turned, 1)
                        ch.link(dve.tensor_scalar(sdm[:, 0, :], PS[:, 3, 0:T], gcol("mkr"), gcol("mki"),
                                                  ALU.mult, ALU.add))
                        dve.tensor_tensor(kk_, kk_, sdm[:, 0, :], ALU.mult).then_inc(k_turned, 1)
                if g in (2, 3):
                    q4 = zt4[:, g - 1]
                    if j == 4:
                        dve.wait_ge(evac, g)
                        half_sines(rb4, q4, 2, 0)
                    if j == 5:
                        half_sines(rb4, q4, 2, 1)
                    if j == 6:
                        ch.need(ch.n)
                        ch.mark(dve.tensor_tensor(q4, q4, tabb(2, 4), ALU.mult))
                    if j == 7:
                        ch.need(ch.n)
                        dve.tensor_tensor(q4, q4, rb4[:], ALU.add).then_inc(qi_turned, 1)
                for n, (gc, k) in enumerate(IDX_AT):
                    if (g, j) == (gc, k + 5):
                        if n == 0:
                            dve.wait_ge(tok_copied, 1)
                            dve.wait_ge(past_in, 80)
                        for h in (2 * n, 2 * n + 1):
                            dve.wait_ge(relu_ready, h + 1)
                            if h:
                                dve.wait_ge(idx_added, h)
                            for q in range(3):
                                sl = slice(SEG[q], SEG[q + 1])
                                e = dve.scalar_tensor_tensor(acc[:, sl], rt[:, h % 2, sl], wiT[:, q, h:h + 1],
                                                             (adm if h == 0 else acc)[:, sl], ALU.mult, ALU.add)
                            e.then_inc(idx_added, 1)
                if g == 4 and j == 11:
                    dve.wait_ge(latsd, 1)
                    ch.link(dve.reciprocal(sdm[:, 0, :], sdm[:, 0, :]))
                    dve.wait_ge(evac, 4)
                    for t in range(2):
                        e = dve.scalar_tensor_tensor(lat[:, t, PAST:], zt[:, CKV + t, :], gcol("kvlat", t),
                                                     sdm[:, 0, :], ALU.mult, ALU.mult)
                    e.then_inc(lat_ready, 1)
                if g == 5 and j == 9:
                    dve.wait_ge(latsd, 2)
                    ch.link(dve.reciprocal(sdm[:, 1, :], sdm[:, 1, :]))
                    dve.wait_ge(evac, 5)
                    for t in range(4):
                        e = dve.scalar_tensor_tensor(zt[:, CQ + t, :], zt[:, CQ + t, :], gcol("qlat", t),
                                                     sdm[:, 1, :], ALU.mult, ALU.mult)
                    e.then_inc(lat_ready, 1)
                if g == 5 and j >= 4:
                    r = j - 4
                    if r == 0:
                        dve.wait_ge(idx_added, 16)
                    rows = [q for q in range(3) if r < (TOPK_S if q == 0 else TOPK_P) // 8]
                    for q in rows:
                        e = dve.max(m8[:, q, :], acc[:, SEG[q]:SEG[q + 1]])
                    ch.link(e)
                    for q in rows:
                        sl = slice(SEG[q], SEG[q + 1])
                        e = dve.match_replace(acc[:, sl], m8[:, q, :], acc[:, sl], TAKEN)
                    ch.link(e)
                if g == 6 and j == 4:
                    ch.link(dve.tensor_scalar(biasA[:], acc[:], TAKEN / 2, NEG, ALU.is_gt, ALU.mult))
                    dve.tensor_tensor(biasA[:], biasA[:], adm[:], ALU.add).then_inc(bias_ready, 1)
                if g < 6:
                    return
                q4 = zt4[:, g - 1]
                if (g, j) in ((6, 4), (7, 3)):
                    dve.wait_ge(evac, g)
                    half_sines(rb4, q4, 0, 0, "aq")
                if (g, j) in ((6, 5), (7, 3)):
                    half_sines(rb4, q4, 0, 1, "aq")
                if (g, j) in ((6, 6), (7, 5)):
                    dve.wait_ge(qa_sd, g - 5)
                    dve.reciprocal(sdr[0:8], sdr[0:8]).then_inc(qa_rinv, 1)
                if (g, j) in ((6, 7), (7, 4)):
                    ch.need(ch.n)
                    ch.mark(dve.scalar_tensor_tensor(q4, q4, gcol("aq"), tabb(0, 4), ALU.mult, ALU.mult))
                if (g, j) in ((6, 8), (7, 6)):
                    ch.need(ch.n)
                    ch.mark(dve.tensor_tensor(q4, q4, rb4[:], ALU.add))
                if (g, j) in ((6, 9), (7, 7)):
                    dve.wait_ge(qa_bc, g - 5)
                    ch.need(ch.n)
                    dve.tensor_tensor(q4, q4, side, ALU.mult).then_inc(qa_turned, 1)
                if g == 6 and j == 10:
                    dve.wait_ge(lath_ready, 1)
                    dve.tensor_tensor(qlatl[:], zt[:, CQ:CQ + 4, :], qlath[:].bitcast(F32),
                                      ALU.subtract).then_inc(latl_ready, 1)

            for g in range(N_ABIN):
                def take():
                    if g == 0:
                        rms(0)
                    take_scaled(U_ABIN + CU * g, g, zt4[:, g])

                step(U_ABIN + CU * g, take, each=lambda j: ab_piece(g, j))
            ab_piece(7, 3)
            for k in range(6):
                if k % 2:
                    c = k // 2
                    dve.wait_ge(unit_done, U_UQ + 2 * c + 2)
                    dve.tensor_copy(qb[:, 4 * c:4 * c + 4, :], PS[:, 4:8, 0:T]).then_inc(qkv_evac, 1)
                split(U_UQ + 4 + k)
                ab_piece(7, 4 + k)
                if k == 3:
                    dve.wait_ge(lath_ready, 2)
                    dve.tensor_tensor(latl[:], lat[:], lath[:].bitcast(F32), ALU.subtract).then_inc(latl_ready, 1)
            dve.wait_ge(bias_ready, 1)
            attend(0, 0, biasA, 128 ** -0.5, 0)
            for c in range(3):
                dve.wait_ge(qb_bc, c + 1)
                q4 = qb[:, 4 * c:4 * c + 4, :]
                e = dve.scalar_tensor_tensor(q4, q4, gcol("qn" if c < 2 else "qr"), PS[:, 4:8, 0:T], ALU.mult,
                                             ALU.mult)
                e.then_inc(qb_turned, 1)
                if c < 2:
                    split(U_KN + 4 + c)
            split(U_KN + 6)
            dve.wait_ge(qb_turned, 3)
            half_sines(rbq, q4, 2, 0)
            half_sines(rbq, q4, 2, 1)
            dve.wait_ge(kn_sd, 1)
            dve.reciprocal(sdk[0:8], sdk[0:8]).then_inc(kn_rinv, 1)
            ch.need(ch.n)
            ch.mark(dve.tensor_tensor(q4, q4, tabb(2, 4), ALU.mult))
            ch.need(ch.n)
            dve.tensor_tensor(q4, q4, rbq[:], ALU.add).then_inc(qb_turned, 1)
            split(U_KN + 7)
            for c, t0, bank in ((0, 0, 4), (1, 4, 0)):
                dve.wait_ge(kn_bc, c + 1)
                k_ = kn[:, t0:t0 + 4, :]
                dve.scalar_tensor_tensor(k_, k_, gcol("kn"), PS[:, bank:bank + 4, 0:KEYS], ALU.mult,
                                         ALU.mult).then_inc(kn_turned, 1)
            attend(8, 8, adm, 192 ** -0.5, 4)
            for c in range(4):
                step(U_ABOUT + CU * c, lambda: take_added(U_ABOUT + CU * c, G_ABOUT + c, c, ALL),
                     each=norm_ahead(1) if c == 3 else None)
            norm_rest(1)
            mlp(1, U_MLP0, G_MLP0, 0, True)(0)
            with dve.Fori(1, 3) as f:
                mlp(1, U_MLP0, G_MLP0, 0, False)(f)
            mlp(1, U_MLP0, G_MLP0, 0, False, ahead=norm_ahead(2))(3)

            def state_queries(h):
                if h >= 2:
                    dve.wait_ge(do_psum, h - 1)
                q8 = z2[:, DQ + 2 * h:DQ + 2 * h + 2, 0:NS_TOK]
                dve.tensor_tensor(qd[:, h % 2], q8, decq[:, h, :].unsqueeze(1).to_broadcast([P, 2, NS_TOK]),
                                  ALU.mult).then_inc(qd_ready, 1)

            norm_rest(2)
            parts = ((0, NS_TOK, 0), (NS_TOK, T, 3))

            def gate_piece(c, j):
                g = c - 2
                if 0 <= g < 4:
                    if 5 <= j <= 6:
                        for k in (2 * j - 10, 2 * j - 9):
                            if k == 0:
                                dve.wait_ge(cx_copied, g + 1)
                                if g:
                                    dve.wait_ge(igx_ready, g)
                            else:
                                ch.need(ch.n)
                            for n in range(2):
                                for a, b, off in parts:
                                    dst, src = xc[:, n, a:b], cxp[:, n, a + off + k:b + off + k]
                                    w = gcol("conv_w", 8 * k + 2 * g + n)
                                    if k == 0:
                                        e = dve.tensor_scalar(dst, src, w, gcol("conv_b", 2 * g + n), ALU.mult,
                                                              ALU.add)
                                    else:
                                        e = dve.scalar_tensor_tensor(dst, src, w, dst, ALU.mult, ALU.add)
                                    if k == 3:
                                        e.then_inc(xc_ready, 1)
                                    else:
                                        ch.mark(e)
                    if j == 8:
                        dve.wait_ge(xch_ready, g + 1)
                        dve.tensor_tensor(xcl[:], xc[:], xch[:].bitcast(F32), ALU.subtract).then_inc(xcl_ready, 1)
                g = c - 3
                if 0 <= g < 4:
                    if j == 7:
                        dve.wait_ge(asq_ready, g + 1)
                        dve.scalar_tensor_tensor(tv[:], rg[:], 1.0, tv[:], ALU.add, ALU.mult).then_inc(w_ready, 1)
                    if j == 9:
                        dve.wait_ge(sqrt_ready, g + 1)
                        dve.wait_ge(igx_ready, g + 1)
                        dve.wait_ge(clast_ready, 1)
                        ch.link(dve.tensor_tensor(tv[:], tv[:], ig[:], ALU.mult))
                        for n in range(2):
                            for a, b, h0 in ((0, NS_TOK, gcol("h0", 2 * g + n)), (NS_TOK, T, 0.0)):
                                dve.tensor_tensor_scan(z2[:, CX + 2 * g + n, a:b], av[:, n, a:b], tv[:, n, a:b],
                                                       h0, ALU.mult, ALU.add).then_inc(scan_done, 1)
                if 7 <= c <= 10:
                    k = c - 7
                    x1, x2 = halves(k)
                    if j == 5:
                        if k == 0:
                            dve.wait_ge(scan_done, 16)
                            dve.wait_ge(tab2_in, 32)
                        dve.wait_ge(evac, G_CDIN + (6, 6, 8, 8)[k])
                        dve.tensor_tensor(rr[:, 0], x1, cosb, ALU.mult)
                    if j == 6:
                        dve.tensor_tensor(rr[:, 1], x2, sinb, ALU.mult).then_inc(rope2_d, 1)
                    if j == 9:
                        dve.wait_ge(rope2_d, 2 * k + 1)
                        dve.wait_ge(rope2_p, 2 * k + 1)
                        dve.tensor_tensor(x1, rr[:, 0], rr[:, 1], ALU.subtract).then_inc(rope2_d, 1)
                    if j == 10:
                        dve.wait_ge(rope2_d, 2 * k + 2)

            for c in range(N_CDIN):
                u0, n = cd_chunk(c)
                for j in range(NR, n + NR):
                    if j == n + NR - 1:
                        if c == 0:
                            rms(2)
                        if c == 10:
                            dve.wait_ge(outc_ready, 1)
                        dve.wait_ge(unit_done, u0 + n)
                        dve.tensor_tensor(z24[:, c], banks(G_CDIN + c), rstd4, ALU.mult).then_inc(evac, 1)
                    split(u0 + j)
                    gate_piece(c, j)
                    if c == 11 and j == 9:
                        dve.wait_ge(doh_ready, 1)
                        for src, dst in MOVES:
                            e = dve.tensor_tensor(mol[:, 0:8, dst], z2[:, CG:CG + 8, src],
                                                  moh[:, 0:8, dst].bitcast(F32), ALU.subtract)
                        e.then_inc(dol_ready, 1)
                    if c == 11 and j == 10:
                        dve.wait_ge(dol_ready, 1)
                        state_queries(0)
            def decayed_scores(h):
                dve.wait_ge(ds_psum, h + 1)
                dve.wait_ge(mask_in[h % 2], 16 * (h // 2 + 1))
                dve.tensor_tensor(pT[0:80, h % 2, 0:336], PS[0:80, 3, 0:336], dmask[0:80, h % 2, 0:336],
                                  ALU.mult)
                dve.tensor_tensor(pT[:, h % 2, 336:720], PS[:, 4, 0:384], dmask[:, h % 2, 336:720],
                                  ALU.mult).then_inc(pT_ready, 1)

            dve.wait_ge(s0_in_s, 16)
            decayed_scores(0)
            for h in range(4):
                dve.wait_ge(st_psum, 2 * h + 2)
                if h >= 2:
                    dve.wait_ge(st_out[h % 2], 32)
                dve.scalar_tensor_tensor(so[:, h % 2], s0[:, :, h, :], float(np.float32(GAMMA[h] ** NS_TOK)),
                                         PS[:, 0, :].rearrange("p (a b) -> p a b", a=2),
                                         ALU.mult, ALU.add).then_inc(st_sample, 1)
                if h < 3:
                    state_queries(h + 1)
                dve.wait_ge(osd_ready, h + 1)
                ch.link(dve.reciprocal(osd[:], osd[:]))
                if h < 3:
                    decayed_scores(h + 1)
                for e_ in range(2):
                    dve.scalar_tensor_tensor(osq[:, e_, :], PS[:, 1 + e_, 0:T], gcol("dn", e_), osd[:],
                                             ALU.mult, ALU.mult).then_inc(on_ready, 1)
                dve.wait_ge(on_ready, 2 * h + 2)
                dve.wait_ge(silu_ready, h // 2 + 1)
                dg = z2[:, DG + 2 * h:DG + 2 * h + 2, :]
                dve.tensor_tensor(dg, dg, osq[:], ALU.mult).then_inc(od_ready, 1)
                dve.wait_ge(doh_ready, h + 2)
                dve.wait_ge(od_ready, h + 1)
                for src, dst in MOVES:
                    e = dve.tensor_tensor(mol[:, 8 + 2 * h:10 + 2 * h, dst], dg[:, :, src],
                                          moh[:, 8 + 2 * h:10 + 2 * h, dst].bitcast(F32), ALU.subtract)
                e.then_inc(dol_ready, 1)
            dve.wait_ge(x_moved, 1)
            for c in range(4):
                step(U_CDOUT + CU * c, lambda: take_added(U_CDOUT + CU * c, G_CDOUT + c, c, LIVE),
                     each=norm_ahead(3) if c == 3 else None)
            norm_rest(3)
            mlp(3, U_MLP1, G_MLP1, 1, True)(0)
            with dve.Fori(1, 3) as f:
                mlp(3, U_MLP1, G_MLP1, 1, False)(f)
            mlp(3, U_MLP1, G_MLP1, 1, False, last=True)(3)

        @block.tensor
        def _(pe):
            def product(u, j, kt, rh, rl, first, last, bank0, m=4, cols=ALL):
                s = u % NR
                for o in range(m):
                    c = 512 * j + P * o
                    wh, wl = w_hi[:, s, c:c + P], w_lo[:, s, c:c + P]
                    out = PS[:, bank0 + o, cols]
                    pe.matmul(out, wh, rh, start=first, stop=False)
                    pe.matmul(out, wh, rl, start=False, stop=False)
                    mm = pe.matmul(out, wl, rh, start=False, stop=last)
                return mm

            def chunk(u0, g, xh, xl, i=None, su=0, sg=0, need=None, hook=None, cs=ALL, ks=range(CU)):
                if g >= 2 or i is not None:
                    pe.wait_ge(evac, at(i, sg, g - 1))
                for k in ks:
                    if need:
                        need(k)
                    pe.wait_ge(lo_ready, at(i, su, u0 + k + 1))
                    for j in range(2):
                        kt = 2 * k + j
                        mm = product(u0 + k, j, kt, xh[:, kt, cs], xl[:, kt, cs], kt == 0, kt == KT - 1,
                                     4 * (g % 2), cols=cs)
                    mm.then_inc(unit_done, 1)
                    if hook:
                        hook(k)

            def need_x(n):
                return lambda k: pe.wait_ge(xl_ready, 16 * n + 2 * k + 2)

            def sum_squares(n):
                def f(k=5):
                    if k != 5:
                        return
                    if n == 0:
                        pe.wait_ge(const_in, 32)
                    pe.wait_ge(ssq_ready, n + 1)
                    if n:
                        pe.wait_ge(evac, NORM_G[n])
                    pe.matmul(PS[:, SB(n), COLS[n]], ones, ssq[:, 0, COLS[n]], start=True,
                              stop=True).then_inc(ssum_done, 1)
                return f

            def attend(g0, scores, values, sb, tail):
                pb, ob = 4 - sb, 6 - sb
                for s in range(8 + 3):
                    if s < 8:
                        g = g0 + s
                        if s >= 2:
                            pe.wait_ge(smax, g - 1)
                        for q, (t0, k0, k1) in enumerate(QT):
                            o = SEG[q] - 416 * (q // 2)
                            mm = scores(s, PS[:, sb + 2 * (g % 2) + q // 2, o:o + k1 - k0], t0, k0, k1)
                        mm.then_inc(sc_psum, 1)
                    if 2 <= s < 10:
                        g = g0 + s - 2
                        pe.wait_ge(pn_ready, g + 1)
                        if g == 0:
                            pe.wait_ge(qb_sd, 1)
                        if g == 8:
                            pe.wait_ge(kn_turned, 2)
                        if s >= 3:
                            pe.wait_ge(pta_ready, g)
                            pe.wait_ge(ptb_ready, g)
                        for a, (q, k) in enumerate(((0, 0), (1, 2), (2, 2), (2, 3))):
                            o = SEG[q] + KTILE[k][0] - QT[q][1]
                            pe.transpose(PS[:, pb, P * a:P * a + P], pr[:, g % 3, o:o + P], ident)
                        for q in range(3):
                            o = SEG[q] + KTILE[1][0] - QT[q][1]
                            mm = pe.transpose(PS[0:80, pb + 1, P * q:P * q + P], pr[:, g % 3, o:o + 80], ident)
                        mm.then_inc(pt_psum, 1)
                    if s >= 3:
                        g = g0 + s - 3
                        h = s - 3
                        pe.wait_ge(pta_ready, g + 1)
                        pe.wait_ge(ptb_ready, g + 1)
                        if s >= 5:
                            pe.wait_ge(mol_ready, g - 1)
                        for q, (t0, t1_) in enumerate(QN):
                            out = PS[:, ob + g % 2, t0:t1_]
                            n = t1_ - t0
                            full = {0: [(0, 0)], 1: [(1, 2)], 2: [(2, 2), (3, 3)]}[q]
                            pe.matmul(out, values(h, 1)[0:80], ptb[0:80, g % 2, q, 0:n], start=True,
                                      stop=False)
                            for a, (slot, k) in enumerate(full):
                                mm = pe.matmul(out, values(h, k), pta[:, g % 2, slot, 0:n], start=False,
                                               stop=a == len(full) - 1)
                        mm.then_inc(o_psum, 1)
                    if s >= 8:
                        tail(s)

            def sel(kind, j, n=8):
                c = GAIN[kind] + 15 - j
                return gains[:, c:c + n]

            def spread(out, j, rows, n=8):
                return pe.matmul(out, ident[0:n, j:j + 1].to_broadcast([n, P]), rows, start=True, stop=True)

            def ab_side(g):
                def hook(k):
                    bank = 4 * (1 - g % 2)
                    if (g, k) == (1, 1):
                        pe.wait_ge(evac, 1)
                        pe.wait_ge(k_sq, 1)
                        for j, kind in enumerate(("sel128", "sel128", "sel64")):
                            mm = pe.matmul(PS[0:8, 0, 0:T], sel(kind, j), sq4[:, j, :], start=j == 0,
                                           stop=j == 2)
                        mm.then_inc(k_ms, 1)
                    if (g, k) == (1, 4):
                        pe.wait_ge(k_rinv, 1)
                        for j in range(3):
                            spread(PS[:, 1 + j, 0:T], j, sdr[0:8])
                        for q, (t0, _, _) in enumerate(QT):
                            mm = pe.transpose(PS[:, 0, 16 * q:16 * q + 16], zt[0:16, WI, t0:t0 + P],
                                              ident[0:16, 0:16])
                        mm.then_inc(k_psum, 1)
                    if (g, k) in IDX_AT:
                        n = IDX_AT.index((g, k))
                        if n == 0:
                            pe.wait_ge(qi_turned, 2)
                            pe.wait_ge(kpad_ready, 1)
                        if n == 3:
                            pe.wait_ge(evac, 4)
                        elif n:
                            pe.wait_ge(relu_ready, 2 * n)
                        for h in (2 * n, 2 * n + 1):
                            b = bank + 2 * (h % 2)
                            for q, (t0, k0, k1) in enumerate(QT):
                                o = SEG[q] - 416 * (q // 2)
                                mm = pe.matmul(PS[:, b + q // 2, o:o + k1 - k0], zt[:, QI + h // 2, t0:t0 + P],
                                               kpad[:, h % 2, k0:k1], start=True, stop=True)
                            mm.then_inc(idx_psum, 1)
                    if (g, k) == (4, 6):
                        pe.wait_ge(relu_ready, 16)
                        pe.wait_ge(latsq, 1)
                        for j in range(2):
                            mm = pe.matmul(PS[:, 7, 0:T], ones, sqm[:, j, :], start=j == 0, stop=j == 1)
                        mm.then_inc(latms, 1)
                        for c in range(2):
                            pe.transpose(PS[0:80, 6, P * c:P * c + P], zt[:, VA + c, 0:80], ident)
                            for t in range(2):
                                a, b = TT[1 + t]
                                mm = pe.transpose(PS[:, 5, 256 * t + P * c:256 * t + P * c + P],
                                                  zt[:, VA + c, a:b], ident)
                        mm.then_inc(va_psum, 1)
                    if (g, k) == (5, 2):
                        pe.wait_ge(evac, 5)
                        pe.wait_ge(latsq, 2)
                        for j in range(4):
                            mm = pe.matmul(PS[:, 0, 0:T], ones, sqm[:, j, :], start=j == 0, stop=j == 3)
                        mm.then_inc(latms, 1)
                    if (g, k) in ((6, 2), (7, 1)):
                        pe.wait_ge(evac, g)
                        pe.wait_ge(qa_sq, g - 5)
                        for j in range(4):
                            mm = pe.matmul(PS[0:8, bank, 0:T], sel("sel128", j), sq4[:, j, :], start=j == 0,
                                           stop=j == 3)
                        mm.then_inc(qa_ms, 1)
                    if (g, k) in ((6, 4), (7, 3)):
                        pe.wait_ge(qa_rinv, g - 5)
                        for j in range(4):
                            mm = spread(PS[:, bank + j, 0:T], j, sdr[0:8])
                        mm.then_inc(qa_bc, 1)
                return hook

            for g in range(N_ABIN):
                if g == 2:
                    pe.wait_ge(k_turned, 2)
                    pe.wait_ge(tok_copied, 1)
                if g == 4:
                    pe.wait_ge(relu_ready, 6)
                if g == 5:
                    pe.wait_ge(latsd, 1)
                    pe.wait_ge(tok_copied, 2)
                if g == 6:
                    pe.wait_ge(latsd, 2)
                if g == 0:
                    chunk(U_ABIN, 0, xh, xl, need=need_x(0), hook=sum_squares(0))
                    pe.wait_ge(rms_ready, 1)
                else:
                    chunk(U_ABIN + CU * g, g, xh, xl, hook=ab_side(g))
            pe.wait_ge(latl_ready, 1)
            pe.wait_ge(qa_turned, 1)
            for c in range(3):
                if c:
                    pe.wait_ge(qkv_evac, c)
                for k in range(2):
                    u = U_UQ + 2 * c + k
                    pe.wait_ge(lo_ready, u + 1)
                    for j in range(2):
                        kt = 2 * k + j
                        mm = product(u, j, kt, qlath[:, kt, :], qlatl[:, kt, :], kt == 0, kt == 3, 4)
                    mm.then_inc(unit_done, 1)
                    ab_side(7)(2 * c + k)
            pe.wait_ge(qkv_evac, 3)
            pe.wait_ge(qb_sq, 2)
            for j in range(8):
                pe.matmul(PS[0:16, 4, 0:T], sel("sel128", j, 16), sqq[:, j, :], start=j == 0, stop=False)
            pe.wait_ge(qb_sq, 3)
            for j in range(4):
                c = GAIN["selpair"] + 14 - (8 + 2 * j)
                mm = pe.matmul(PS[0:16, 4, 0:T], gains[:, c:c + 16], sqq[:, 8 + j, :], start=False, stop=j == 3)
            mm.then_inc(qb_ms, 1)
            pe.wait_ge(qa_turned, 2)

            def scores_a(h, out, t0, k0, k1):
                return pe.matmul(out, zt[:, QA + h, t0:t0 + P], kA[:, h // 4, k0:k1], start=True, stop=True)

            def keys_b(c):
                u = U_KN + c
                pe.wait_ge(lo_ready, u + 1)
                if c:
                    pe.wait_ge(kn_raw, c)
                else:
                    pe.wait_ge(latl_ready, 2)
                    pe.wait_ge(smax, 8)
                for j in range(2):
                    mm = product(u, j, j, lath[:, j, :], latl[:, j, :], j == 0, j == 1, 0, cols=slice(0, KEYS))
                mm.then_inc(unit_done, 1)

            attend(0, scores_a, lambda h, k: vA[:, k, P * (h // 4):P * (h // 4) + P], 0,
                   lambda s: keys_b(0) if s == 9 else None)
            def spread_qb(c):
                if c == 0:
                    pe.wait_ge(mol_ready, 8)
                    pe.wait_ge(qb_rinv, 1)
                    pe.wait_ge(pair_ready, 1)
                else:
                    pe.wait_ge(qb_turned, c)
                for j in range(4):
                    if c < 2:
                        mm = spread(PS[:, 4 + j, 0:T], 4 * c + j, sdq[0:16], 16)
                    else:
                        mm = pe.matmul(PS[:, 4 + j, 0:T], pairrow[0:16, j], sdq[0:16], start=True, stop=True)
                mm.then_inc(qb_bc, 1)

            def values_b(c):
                u = U_V + c
                s = u % NR
                pe.wait_ge(lo_ready, u + 1)
                for k, (a, b) in enumerate(KTILE):
                    out = PS[0:b - a, k, :]
                    for j in range(2):
                        wh, wl = w_hi[:, s, 512 * j:512 * j + 512], w_lo[:, s, 512 * j:512 * j + 512]
                        pe.matmul(out, lath[:, j, a:b], wh, start=j == 0, stop=False)
                        pe.matmul(out, latl[:, j, a:b], wh, start=False, stop=False)
                        mm = pe.matmul(out, lath[:, j, a:b], wl, start=False, stop=j == 1)
                mm.then_inc(unit_done, 1)

            spread_qb(0)
            keys_b(1)
            spread_qb(1)
            pe.wait_ge(kn_raw, 2)
            values_b(0)
            spread_qb(2)
            pe.wait_ge(kn_sq, 2)
            pe.wait_ge(qb_turned, 3)
            for j in range(8):
                mm = pe.matmul(PS[0:8, 4, 0:KEYS], sel("sel128", j), sqk[:, j // 4, j % 4, :], start=j == 0,
                               stop=j == 7)
            mm.then_inc(kn_ms, 1)
            pe.wait_ge(qkv_evac, 4)
            values_b(1)
            pe.wait_ge(kn_rinv, 1)
            for c in range(2):
                if c:
                    pe.wait_ge(qkv_evac, 5)
                for j in range(4):
                    mm = spread(PS[:, 4 * (1 - c) + j, 0:KEYS], 4 * c + j, sdk[0:8])
                mm.then_inc(kn_bc, 1)
            pe.wait_ge(qb_turned, 4)

            def need_heads(k):
                if k == 0:
                    pe.wait_ge(smax, 16)
                    pe.wait_ge(mol_ready, 8)
                if k >= 4:
                    pe.wait_ge(mol_ready, 2 * k + 2)

            def scores_b(h, out, t0, k0, k1):
                pe.wait_ge(kn_turned, 1 + h // 4)
                pe.matmul(out, qb[:, h, t0:t0 + P], kn[:, h, k0:k1], start=True, stop=False)
                return pe.matmul(out, qb[:, 8 + h // 2, t0:t0 + P], kpad[:, 2 + h % 2, k0:k1], start=False,
                                 stop=True)

            attend(8, scores_b, lambda h, k: vB[:, k, P * h:P * h + P], 4,
                   lambda s: chunk(U_ABOUT, G_ABOUT, moh, mol, ks=(s - 8,), need=need_heads))
            chunk(U_ABOUT, G_ABOUT, moh, mol, ks=range(3, CU), need=need_heads)
            for c in range(1, 4):
                chunk(U_ABOUT + CU * c, G_ABOUT + c, moh, mol)

            def mlp(n, u_mlp, g_mlp, L, whole):
                def body(f):
                    for c in range(4):
                        if whole and c == 1:
                            pe.wait_ge(rms_ready, n + 1)
                        chunk(u_mlp + CU * c, g_mlp + c, xh, xl, f, 64, 8,
                              need=need_x(n) if whole and c == 0 else None,
                              hook=sum_squares(n) if whole and c == 0 else None, cs=COLS[n])
                    for c in range(4):
                        chunk(u_mlp + 32 + CU * c, g_mlp + 4 + c, hh, hl, f, 64, 8, cs=COLS[n],
                              need=(lambda k: pe.wait_ge(hl_ready, at(f, 4, 16 * L + k // 2 + 1)))
                              if c == 0 else None)
                return body

            mlp(1, U_MLP0, G_MLP0, 0, True)(0)
            with pe.Fori(1, 4) as f:
                mlp(1, U_MLP0, G_MLP0, 0, False)(f)
            def tokens_first(h):
                if h:
                    pe.wait_ge(ktok_ready, h)
                for d in range(2):
                    k_, v_ = z2[:, DK + 2 * h + d], z2[:, DV + 2 * h + d]
                    pe.transpose(PS[0:80, 6, P * d:P * d + P], k_[:, 0:80], ident)
                    pe.transpose(PS[0:80, 6, 256 + P * d:256 + P * d + P], v_[:, 0:80], ident)
                    for k in range(2):
                        a, b = TT[1 + k]
                        o = 256 * k + P * d
                        pe.transpose(PS[:, 7, o:o + P], k_[:, a:b], ident)
                        mm = pe.transpose(PS[:, 5, o:o + P], v_[:, a:b], ident)
                mm.then_inc(kv_psum, 1)

            for c in range(N_CDIN):
                g = G_CDIN + c
                u0, nu = cd_chunk(c)
                pe.wait_ge(evac, g - 1)
                if c == 1:
                    pe.wait_ge(rms_ready, 3)
                if c - 1 in GATE_CHUNKS:
                    pe.wait_ge(gate_ready, 4 * (c - 2))
                for j in range(nu):
                    u = u0 + j
                    s = u % NR
                    if nu > CU and j == GATE_AT:
                        b = c - 2
                        pe.wait_ge(evac, g)
                        pe.wait_ge(xcl_ready, b + 1)
                        pe.wait_ge(lo_ready, u + 1)
                        for n in range(4):
                            wh, wl = w_hi[:, s, P * n:P * n + P], w_lo[:, s, P * n:P * n + P]
                            out = PS[:, 4 * (1 - g % 2) + n, 0:T]
                            pe.matmul(out, wh, xch[:, n % 2, :], start=True, stop=False)
                            pe.matmul(out, wh, xcl[:, n % 2, :], start=False, stop=False)
                            mm = pe.matmul(out, wl, xch[:, n % 2, :], start=False, stop=True)
                    else:
                        k = j - (nu > CU and j > GATE_AT)
                        if c == 0:
                            need_x(2)(k)
                        pe.wait_ge(lo_ready, u + 1)
                        for i in range(2):
                            kt = 2 * k + i
                            mm = product(u, i, kt, xh[:, kt, :], xl[:, kt, :], kt == 0, kt == KT - 1, 4 * (g % 2))
                    mm.then_inc(unit_done, 1)
                    if c == 0 and j == 5:
                        sum_squares(2)()
                    if c == 11 and j == 5:
                        pe.wait_ge(rope2_d, 8)
                        pe.wait_ge(rope2_p, 8)
                        tokens_first(0)
            def decayed_scores(h, parts=(1, 2, 0)):
                if h:
                    pe.wait_ge(pT_ready, h)
                for j in parts:
                    bank, o, i0 = ((3, 0, 0), (4, 0, 80), (4, 256, 208))[j]
                    a, b = TT[j]
                    for d in range(2):
                        mm = pe.matmul(PS[0:b - a, bank, o:o + T - i0], z2[:, DK + 2 * h + d, a:b],
                                       z2[:, DQ + 2 * h + d, i0:T], start=d == 0, stop=d == 1)
                if 0 in parts:
                    mm.then_inc(ds_psum, 1)

            def prompt_state(h):
                pe.wait_ge(ktok_ready, h + 1)
                for d in range(2):
                    out = PS[:, 5, 256 * d:256 * d + 256]
                    pe.matmul(out, ktok[64:80, h % 2, 0, P * d:P * d + P], vtok[64:80, h % 2, 0, :],
                              start=True, stop=False)
                    for k in (1, 2):
                        mm = pe.matmul(out, ktok[:, h % 2, k, P * d:P * d + P], vtok[:, h % 2, k, :],
                                       start=False, stop=k == 2)
                mm.then_inc(st_psum, 1)

            def sample_state(h):
                if h:
                    pe.wait_ge(osd_ready, h)
                for d in range(2):
                    mm = pe.matmul(PS[:, 0, 256 * d:256 * d + 256], ktok[0:64, h % 2, 0, P * d:P * d + P],
                                   vtok[0:64, h % 2, 0, :], start=True, stop=True)
                mm.then_inc(st_psum, 1)

            def retained(h):
                if h:
                    pe.wait_ge(on_ready, 2 * h)
                else:
                    pe.wait_ge(s0_in_s, 16)
                pe.wait_ge(qd_ready, h + 1)
                pe.wait_ge(pT_ready, h + 1)
                for e in range(2):
                    bank = 1 + e
                    c = P * e
                    pe.matmul(PS[:, bank, 0:T], vtok[0:80, h % 2, 0, c:c + P], pT[0:80, h % 2, 0:336],
                              start=True, stop=False)
                    pe.matmul(PS[:, bank, 80:T], vtok[:, h % 2, 1, c:c + P], pT[:, h % 2, 336:592],
                              start=False, stop=False)
                    pe.matmul(PS[:, bank, 208:T], vtok[:, h % 2, 2, c:c + P], pT[:, h % 2, 592:720],
                              start=False, stop=False)
                    for d in range(2):
                        mm = pe.matmul(PS[:, bank, 0:NS_TOK], s0[:, d, h, c:c + P], qd[:, h % 2, d, :],
                                       start=False, stop=d == 1)
                mm.then_inc(do_psum, 1)

            def output_squares(h):
                pe.wait_ge(osq_ready, h + 1)
                pe.wait_ge(st_sample, h + 1)
                for e in range(2):
                    mm = pe.matmul(PS[:, 0, 0:T], ones, osq[:, e, :], start=e == 0, stop=e == 1)
                mm.then_inc(oms_psum, 1)

            decayed_scores(0, (1, 2))
            prompt_state(0)
            pe.wait_ge(evac, G_CDIN + 12)
            decayed_scores(0, (0,))
            for h in range(4):
                if h:
                    prompt_state(h)
                sample_state(h)
                retained(h)
                if h < 3:
                    pe.wait_ge(st_prompt, h + 1)
                    tokens_first(h + 1)
                    output_squares(h)
                    decayed_scores(h + 1)
            pe.wait_ge(st_prompt, 4)
            chunk(U_CDOUT, G_CDOUT, moh, mol, need=lambda k: pe.wait_ge(dol_ready, max(1, k - 2)),
                  hook=lambda k: output_squares(3) if k == 0 else None, cs=LIVE)
            pe.wait_ge(od_ready, 4)
            pe.wait_ge(st_sample, 4)
            chunk(U_CDOUT + CU, G_CDOUT + 1, moh, mol, cs=LIVE)
            with pe.Fori(1, 2) as i:
                for c in range(2):
                    chunk(U_CDOUT + CU * c, G_CDOUT + c, moh, mol, i, 2 * CU, 2, cs=LIVE)
            mlp(3, U_MLP1, G_MLP1, 1, True)(0)
            with pe.Fori(1, 4) as f:
                mlp(3, U_MLP1, G_MLP1, 1, False)(f)

        @block.gpsimd
        def _(pool):
            ch = Chain(pool, pchain)

            def sum_squares(n):
                cs = COLS[n]
                for g in range(4):
                    if n == 0:
                        for i, (a, b) in enumerate(X_PIECES):
                            if 4 * g <= a < 4 * g + 4:
                                pool.wait_ge(x_in_s[i], 16)
                    else:
                        pool.wait_ge(evac, X_FINAL[n] - 3 + g)
                    xg = x[:, 4 * g:4 * g + 4, cs]
                    if g == 0:
                        ch.link(pool.tensor_tensor(ssq[:, :, cs], xg, xg, ALU.mult))
                    else:
                        ch.link(pool.tensor_tensor(sst[:, :, cs], xg, xg, ALU.mult))
                        e = pool.tensor_tensor(ssq[:, :, cs], ssq[:, :, cs], sst[:, :, cs], ALU.add)
                        if g < 3:
                            ch.link(e)
                ch.link(e)
                ch.link(pool.tensor_tensor(ssq[:, 0:2, cs], ssq[:, 0:2, cs], ssq[:, 2:4, cs], ALU.add))
                pool.tensor_tensor(ssq[:, 0, cs], ssq[:, 0, cs], ssq[:, 1, cs], ALU.add).then_inc(ssq_ready, 1)

            outs = [0]

            def send(dst, src):
                pool.dma_start(dst, src).then_inc(out_s, 16)
                outs[0] += 16

            pool.memset(kpad[:], 0.0).then_inc(pad_zero, 1)
            sum_squares(0)
            pool.wait_ge(const_in, 32)
            for j in range(4):
                pair = ident[0:16, 8 + 2 * j:10 + 2 * j].unsqueeze(1).unsqueeze(3).to_broadcast([16, 2, 2, 32])
                e = pool.tensor_copy(pairrow[0:16, j].rearrange("p (r e f) -> p r e f", r=2, e=2), pair)
            e.then_inc(pair_ready, 1)
            pool.wait_ge(k_turned, 2)
            pool.wait_ge(pad_zero, 1)
            pool.wait_ge(past_in, 80)
            for slot, (src, dst) in enumerate(((0, 0), (0, 32), (32, 0), (32, 32))):
                for half in (0, 64):
                    e = pool.tensor_copy(kpad[dst + half:dst + half + 32, slot, :],
                                         kk[src + half:src + half + 32, :])
            e.then_inc(kpad_ready, 1)
            send(k_out, kA[:, :, PAST:])
            send(kk_out, kk[:, PAST:])
            pool.wait_ge(evac, 4)
            send(v_out, zt[:, VA:VA + 2, :])
            pool.wait_ge(lat_ready, 1)
            send(lat_out, lat[:, :, PAST:])
            pool.wait_ge(mol_ready, 16)
            pool.wait_ge(out_s, outs[0])
            sum_squares(1)
            sum_squares(2)
            pool.wait_ge(mol_ready, 16)
            pool.dma_start(tab[:, 0:2, :], tabs_in[:, 4:6, :]).then_inc(tab2_in, 16)
            pool.dma_start(decq[:], decq_in).then_inc(tab2_in, 16)
            pool.dma_start(cstate[:], conv_in).then_inc(cx_in, 16)
            pool.wait_ge(ssum_done, 3)
            pool.wait_ge(xl_ready, 48)
            ch.link(pool.tensor_copy(xs[:], x[:, :, MOVES[0][0]]))
            pool.tensor_copy(x[:, :, MOVES[0][1]], xs[:]).then_inc(x_moved, 1)
            pool.wait_ge(x_moved, 1)
            pool.memset(cxp[:, :, 3 + NS_TOK:6 + NS_TOK], 0.0).then_inc(cx_zero, 1)
            pool.wait_ge(evac, G_CDIN + 2)
            for e, c in enumerate((NS_TOK, T)):
                pool.tensor_copy(clast[:, :, e, :], z2[:, CX:CX + 8, c - 3:c]).then_inc(clast_ready, 1)
            pool.wait_ge(clast_ready, 2)
            pool.dma_start(conv_out, clast[:]).then_inc(conv_outs, 16)
            cg = z2[:, CG:CG + 8, :]

            def gate_input(g):
                pool.wait_ge(gate_ready, 4 * g + 4)
                pool.tensor_tensor(ig[:], ig[:], xc[:], ALU.mult).then_inc(igx_ready, 1)

            gate_input(0)
            pool.wait_ge(evac, G_CDIN + 4)
            half = [slice(0, 4), slice(4, 8)]
            gate_input(1)
            for r in half:
                ch.link(pool.tensor_tensor(t1[:, r], cg[:, r], cg[:, r], ALU.mult))
            gate_input(2)
            for r in half:
                ch.link(pool.tensor_scalar(t1[:, r], t1[:, r], 0.044715, 1.0, ALU.mult, ALU.add))
            gate_input(3)
            for r in half:
                e = pool.tensor_tensor(t1[:, r], t1[:, r], cg[:, r], ALU.mult)
            e.then_inc(gelu_in, 1)
            pool.wait_ge(gelu_sig, 1)
            ch.link(pool.tensor_tensor(cg, cg, t1[:], ALU.mult))
            pool.wait_ge(scan_done, 16)
            for e, c in enumerate((NS_TOK - 1, T - 1)):
                ch.link(pool.tensor_copy(hlast[:, :, e], z2[:, CX:CX + 8, c]))
            pool.dma_start(h_out, hlast[:]).then_inc(h_outs, 16)
            pool.tensor_tensor(cg, cg, z2[:, CX:CX + 8, :], ALU.mult).then_inc(outc_ready, 1)
            pool.wait_ge(outc_ready, 1)
            pool.wait_ge(tab2_in, 32)
            for k in range(4):
                x1, x2 = halves(k)
                pool.wait_ge(evac, G_CDIN + (6, 6, 8, 8)[k])
                if k:
                    pool.wait_ge(rope2_p, 2 * k)
                pool.tensor_tensor(rr[:, 2], x1, sinb, ALU.mult)
                pool.tensor_tensor(rr[:, 3], x2, cosb, ALU.mult).then_inc(rope2_p, 1)
                pool.wait_ge(rope2_p, 2 * k + 1)
                pool.wait_ge(rope2_d, 2 * k + 1)
                pool.tensor_tensor(x2, rr[:, 2], rr[:, 3], ALU.add).then_inc(rope2_p, 1)
            pool.wait_ge(rope2_p, 8)
            pool.wait_ge(dol_ready, 1)
            pool.dma_start(s0[:], s0_in).then_inc(s0_in_s, 16)
            pool.wait_ge(rope2_d, 8)
            for h in range(2):
                pool.dma_start(dmask[:, h, :], ret_in[:, h, :]).then_inc(mask_in[h], 16)
            for r in range(2):
                pool.wait_ge(silu_sig, r + 1)
                dg = z2[:, DG + 4 * r:DG + 4 * r + 4, :]
                pool.tensor_tensor(dg, dg, sgd[:, 4 * r:4 * r + 4], ALU.mult).then_inc(silu_ready, 1)
            for h in range(1, 4):
                if h >= 2:
                    pool.wait_ge(pT_ready, h - 1)
                    pool.dma_start(dmask[:, h % 2, :], ret_in[:, h, :]).then_inc(mask_in[h % 2], 16)
                send_state(pool, h - 1, so, s_out, st_sample, st_prompt, st_out)
            send_state(pool, 3, so, s_out, st_sample, st_prompt, st_out)
            for h in range(2):
                pool.wait_ge(st_out[h], 64)
            sum_squares(3)
            pool.wait_ge(out_s, outs[0])
            pool.wait_ge(conv_outs, 16)
            pool.wait_ge(h_outs, 16)


def send_state(pool, h, so, s_out, st_sample, st_prompt, st_out):
    pool.wait_ge(st_sample, h + 1)
    pool.dma_start(s_out[:, 0, h], so[:, h % 2]).then_inc(st_out[h % 2], 16)
    pool.wait_ge(st_prompt, h + 1)
    pool.dma_start(s_out[:, 1, h], so[:, 2 + h % 2]).then_inc(st_out[h % 2], 16)


def constants():
    pos = np.concatenate([PAST + np.arange(NS_TOK), np.arange(TP)]).astype(np.float32)

    def angles(dim):
        inv = (np.float32(10000.0) ** (-np.arange(0, dim, 2, dtype=np.float32) / np.float32(dim))).astype(np.float32)
        return (inv[:, None] * pos[None, :]).astype(np.float32).astype(np.float64)

    tabs = np.zeros((P, 6, T), np.float32)
    a = np.tile(angles(128), (2, 1))
    tabs[:, 0], tabs[:, 1] = np.cos(a), np.sin(a)
    a = np.tile(angles(64), (4, 1))
    tabs[:, 2], tabs[:, 3] = np.cos(a), np.sin(a)
    for k in (1, 3):
        tabs[64:, k] *= -1
    a = angles(256)
    tabs[:, 4], tabs[:, 5] = np.cos(a), np.sin(a)

    cst = np.zeros((P, 2, P), np.float32)
    cst[:, 0] = np.eye(P)
    cst[:, 1] = 1

    tok_c = np.concatenate([(PAST + np.arange(NS_TOK)) // CHUNK, np.zeros(NMETA, int), 1 + np.arange(SEQ) // CHUNK])
    tok_g = np.arange(T) >= NS_TOK
    key_c = np.concatenate([np.arange(PAST) // CHUNK, tok_c])
    key_g = np.concatenate([np.zeros(PAST, bool), tok_g])
    adm = np.zeros((P, SEG[3]), np.float32)
    for q, (t0, k0, k1) in enumerate(QT):
        n = QN[q][1] - QN[q][0]
        ok = (tok_g[t0:t0 + n, None] == key_g[None, k0:k1]) & (key_c[None, k0:k1] <= tok_c[t0:t0 + n, None])
        adm[0:n, SEG[q]:SEG[q + 1]] = np.where(ok, 0, NEG)

    lg = [np.log(np.float32(g)).astype(np.float64) for g in GAMMA]
    ret = np.zeros((P, 4, 720), np.float32)
    kdec = np.zeros((P, 4, 3), np.float32)
    loc = np.concatenate([np.arange(NS_TOK), np.arange(TP)])
    glen = np.concatenate([np.full(NS_TOK, NS_TOK), np.full(TP, TP)])
    for h in range(4):
        o = 0
        for t, (a, b) in enumerate(TT):
            i0 = (0, 80, 208)[t]
            i = np.arange(i0, T)
            j = np.arange(a, b)
            d = i[None, :] - j[:, None]
            ok = (d >= 0) & (tok_g[i][None, :] == tok_g[j][:, None])
            ret[0:b - a, h, o:o + T - i0] = np.where(ok, np.exp(lg[h] * np.maximum(d, 0)), 0) / 16
            kdec[0:b - a, h, t] = np.exp(lg[h] * (glen[j] - 1 - loc[j])) / 16
            o += T - i0
    decq = np.zeros((P, 4, NS_TOK), np.float32)
    for h in range(4):
        decq[:, h] = np.exp(lg[h] * (np.arange(NS_TOK) + 1))[None, :]
    return tabs, cst, adm, ret, kdec.reshape(P, 12), decq


def kernel(**inputs):
    import concourse.bacc as _bacc
    from concourse.bass_utils import run_bass_kernel_spmd as _run
    np_ = np
    a = {k: np_.asarray(v) for k, v in inputs.items()}
    f4 = np_.float32
    tabs, cst, adm, ret, kdec, decq = constants()

    def cols(v):
        return v.reshape(-1, P).T

    def pair_rows(v):
        return np_.concatenate([v[:32], v[:32], v[32:], v[32:]])[:, None]

    tok = np_.concatenate([a["x_sample"][0], a["meta_tokens"], a["x_prompt"][0]], 0)
    x_in = tok.T.reshape(KT, P, T).transpose(1, 0, 2)

    w = a["ab_w_in"][0]
    qi0 = 1536
    heads = []
    for i in range(8):
        c0, c1 = qi0 + 128 * i, qi0 + 128 * i + 64
        heads += [w[:, c0:c0 + 32], w[:, c1:c1 + 32], w[:, c0 + 32:c0 + 64], w[:, c1 + 32:c1 + 64]]
    ki, kr = 2560, 3408
    abin = np_.concatenate([w[:, 1024:1280],
                            w[:, ki:ki + 32], w[:, kr:kr + 32], w[:, ki + 32:ki + 64], w[:, kr + 32:kr + 64],
                            w[:, 2624:2640], np_.zeros((D, 112), f4)] + heads
                           + [w[:, 3152:3408], w[:, 1280:1536], w[:, 2640:3152], w[:, 0:1024]], 1)
    uq = a["b_w_uq"][0].reshape(512, 8, 192)
    ropes = []
    for i in range(4):
        r0, r1 = uq[:, 2 * i, 128:], uq[:, 2 * i + 1, 128:]
        ropes += [r0[:, :32], r1[:, :32], r0[:, 32:], r1[:, 32:]]
    uqp = np_.concatenate([uq[:, :, :128].reshape(512, 1024)] + ropes, 1)
    ukv = a["b_w_ukv"][0].reshape(256, 8, 256)

    def units(m):
        k, n = m.shape
        return m.reshape(k // 256, 2, P, n // 512, 512).transpose(3, 0, 2, 1, 4).reshape(-1, P, UNIT)

    w = a["cd_w_in"][0]
    cd_w = np_.concatenate([w[:, 0:2048], w[:, 3072:4096], w[:, 2048:3072], w[:, 4096:]], 1)

    def mlp_units(i):
        up, down = a["mlp_w_up"][i], a["mlp_w_down"][i]
        return [x_ for f in range(4) for x_ in (units(up[:, D * f:D * f + D]), units(down[D * f:D * f + D]))]

    cd = units(cd_w)
    pieces = []
    for c in range(N_CDIN):
        if c in GATE_CHUNKS:
            b = 2 * GATE_CHUNKS.index(c)
            gate = [a[n][0][i] for n in ("c_gate_a_w", "c_gate_x_w") for i in (b, b + 1)]
            gate = np_.concatenate(gate + [np_.zeros((P, 512), f4)], 1)[None]
            pieces += [cd[CU * c:CU * c + GATE_AT], gate, cd[CU * c + GATE_AT:CU * c + CU]]
        else:
            pieces += [cd[CU * c:CU * c + CU]]
    wstream = np_.concatenate(
        [units(abin), units(uqp), units(np_.ascontiguousarray(ukv[:, :, :128]).reshape(256, 1024)),
         units(np_.ascontiguousarray(ukv[:, :, 128:]).reshape(256, 1024)), units(a["ab_w_out"][0])]
        + mlp_units(0) + pieces + [units(a["cd_w_out"][0])] + mlp_units(1), 0)

    norms = [a["norm_mix"][0], a["norm_mlp"][0], a["norm_mix"][1], a["norm_mlp"][1]]
    kkg = np_.ones((P, 1), f4)
    kkg[32:64, 0], kkg[96:128, 0] = a["b_kr_norm"][0][:32], a["b_kr_norm"][0][32:]
    mkr = np_.zeros((P, 1), f4)
    mkr[32:64] = mkr[96:128] = 1
    sel = np_.zeros((P, 2, 31), f4)
    sel[:, 0, 15] = 1 / 128
    sel[:, 1, 15] = mkr[:, 0] / 64
    selp = np_.zeros((P, 22), f4)
    selp[:, 14], selp[:, 15] = (1 - mkr[:, 0]) / 64, mkr[:, 0] / 64
    gains = np_.concatenate(
        [cols(n) for n in norms]
        + [a["a_q_norm"][0][:, None], a["a_k_norm"][0][:, None], kkg, pair_rows(a["b_qr_norm"][0]),
           a["b_qn_norm"][0][:, None], a["b_kn_norm"][0][:, None], cols(a["b_q_lat_norm"][0]),
           cols(a["b_kv_lat_norm"][0])]
        + [cols(a["c_conv_w"][0][j]) for j in range(4)]
        + [cols(a[n][0]) for n in ("c_conv_b", "c_gate_a_b", "c_gate_x_b", "c_lambda", "d_out_norm", "state_c_h")]
        + [np_.full((P, 1), EPS, f4), mkr, np_.where(mkr > 0, 0, 1).astype(f4), kdec, sel.reshape(P, 62), selp], 1)
    past_k = a["cache_a_k"][0, 0].transpose(2, 1, 0)
    idx, rope = a["cache_a_kidx"][0, 0].T, a["cache_b_krope"][0, 0].T
    past_kk = np_.concatenate([idx[:32], rope[:32], idx[32:], rope[32:]], 0)
    past_v = a["cache_a_v"][0, 0].reshape(PAST, 256)
    past_lat = a["cache_b_latent"][0, 0].T.reshape(2, P, PAST).transpose(1, 0, 2)
    conv_in = a["state_c_conv"][0, 0].T.reshape(8, P, 3).transpose(1, 0, 2)
    s0_in = a["state_d_s"][0, 0].reshape(4, 2, P, 256).transpose(2, 1, 0, 3)

    ins = [("x_in", x_in), ("wstream", wstream), ("gains", gains), ("cst", cst), ("tabs", tabs), ("adm", adm),
           ("ret", ret), ("decq", decq), ("past_k", past_k), ("past_kk", past_kk), ("past_v", past_v),
           ("past_lat", past_lat), ("conv_in", conv_in), ("s0_in", s0_in)]
    outs = [("y", (P, KT, T)), ("k", (P, 2, T)), ("v", (P, 2, T)), ("kk", (P, T)), ("lat", (P, 2, T)),
            ("conv", (P, 8, 2, 3)), ("h", (P, 8, 2)), ("s", (P, 2, 4, 2, 256))]
    nc = _bacc.Bacc("TRN2", target_bir_lowering=False, num_devices=1)
    arrays, args = {}, []
    for name, v in ins:
        v = np_.ascontiguousarray(v)
        arrays[f"in_{name}"] = v
        args.append(nc.dram_tensor(f"in_{name}", v.shape, mybir.dt.from_np(v.dtype), kind="ExternalInput").ap())
    for name, shape in outs:
        args.append(nc.dram_tensor(f"out_{name}", shape, F32, kind="ExternalOutput").ap())
    build(nc, *args)
    r = _run(nc, [arrays], core_ids=[0])
    o = {name: np_.asarray(r.results[0][f"out_{name}"]) for name, _ in outs}

    def rows(v):
        return v.transpose(2, 1, 0).reshape(v.shape[2], -1)

    y, k, v, lat = rows(o["y"]), rows(o["k"]), rows(o["v"]), rows(o["lat"])
    kk = o["kk"].T
    kidx = np_.concatenate([kk[:, 0:32], kk[:, 64:96]], 1)
    krope = np_.concatenate([kk[:, 32:64], kk[:, 96:128]], 1)
    res = [y[NS_TOK + NMETA:][None], y[NMETA:NMETA + NS_TOK][None]]
    for g, sl in ((1, slice(NS_TOK, T)), (0, slice(0, NS_TOK))):
        n = TP if g else NS_TOK
        res += [k[sl].reshape(1, 1, n, 2, P), v[sl].reshape(1, 1, n, 2, P), kidx[sl][None, None],
                lat[sl][None, None], krope[sl][None, None],
                o["conv"][:, :, g].transpose(2, 1, 0).reshape(1, 1, 3, 1024),
                o["h"][:, :, g].T.reshape(1, 1, 1024),
                o["s"][:, g].transpose(1, 2, 0, 3).reshape(1, 1, 4, 256, 256)]
    return tuple(np_.ascontiguousarray(z) for z in res)
```
